# Optimizing a Trainium2 kernel written in Bass

```python
import math
import jax, jax.numpy as jnp
from jax import lax
import numpy as np

D_MODEL = 1024
BATCH = 1
SEQ = 128
DEPTH = 2
DEC_BATCH = 1
DEC_SEQ = 128
PAST_LEN = 128

GRID_W = 64
HEAD_DIM = 64
ROPE_THETA = 10000.0
ROPE_FREQS = HEAD_DIM // 4
Q_BLOCK = 128
RMS_EPS = 1e-6
N_EVEN = (DEPTH + 1) // 2
N_ODD = DEPTH // 2
A_Q_HEADS = 8
A_KV_HEADS = 2
A_GROUP = A_Q_HEADS // A_KV_HEADS
B_HEADS = 4
B_V_DIM = 2 * HEAD_DIM
A_Q_W = A_Q_HEADS * HEAD_DIM
A_KV_W = A_KV_HEADS * HEAD_DIM
B_QK_W = B_HEADS * 2 * HEAD_DIM
B_V_W = B_HEADS * B_V_DIM
AB_IN = A_Q_W + 2 * A_KV_W + 2 * B_QK_W + B_V_W
AB_OUT = A_Q_W + B_V_W
AB_SPLITS = (A_Q_W, A_Q_W + A_KV_W, A_Q_W + 2 * A_KV_W, A_Q_W + 2 * A_KV_W + B_QK_W,
             A_Q_W + 2 * A_KV_W + 2 * B_QK_W)
C_HEADS = 16
C_WIDTH = C_HEADS * HEAD_DIM
NA_ROWS = 8
NA_COLS = 16
N_EXPERTS = 16
N_GROUPS = 4
EXPERTS_PER_GROUP = N_EXPERTS // N_GROUPS
TOP_K = 2
D_EXPERT = 1024

kernel_name = 'hybrid_diffusion_prefix_step'

F32 = jnp.float32

def _rmsnorm(x, g):
    xf = x.astype(F32)
    y = xf * lax.rsqrt(jnp.mean(xf * xf, axis=-1, keepdims=True) + RMS_EPS)
    return (y * g.astype(F32)).astype(x.dtype)

def _modulation(cond, w, b):
    m = jax.nn.silu(cond) @ w + b
    return tuple(t[:, None, :] for t in jnp.split(m, 6, axis=-1))

def _adaln(x, g, shift, scale):
    return _rmsnorm(x, g) * (1.0 + scale) + shift

def _axial_rope(x):
    seq = x.shape[1]
    pos = jnp.arange(seq, dtype=jnp.int32)
    rows = (pos // GRID_W).astype(F32)
    cols = (pos % GRID_W).astype(F32)
    inv = ROPE_THETA ** (-jnp.arange(ROPE_FREQS, dtype=F32) / ROPE_FREQS)

    def rot(xa, p):
        ang = p[:, None] * inv[None, :]
        ang = jnp.concatenate([ang, ang], axis=-1)[None, :, None, :]
        x1, x2 = jnp.split(xa.astype(F32), 2, axis=-1)
        return xa.astype(F32) * jnp.cos(ang) + jnp.concatenate([-x2, x1], axis=-1) * jnp.sin(ang)

    half = HEAD_DIM // 2
    out = jnp.concatenate([rot(x[..., :half], rows), rot(x[..., half:], cols)], axis=-1)
    return out.astype(x.dtype)

def _blocks(x):
    b, s = x.shape[:2]
    return jnp.moveaxis(x.reshape(b, s // Q_BLOCK, Q_BLOCK, *x.shape[2:]), 1, 0)

def _unblocks(y):
    nb, b, qb = y.shape[:3]
    return jnp.moveaxis(y, 0, 1).reshape(b, nb * qb, *y.shape[3:])

def _gqa_attend(q, k, v):
    scale = HEAD_DIM ** -0.5

    def one(qb):
        s = jnp.einsum('bqhgd,bkhd->bhgqk', qb, k).astype(F32) * scale
        p = jax.nn.softmax(s, axis=-1).astype(v.dtype)
        return jnp.einsum('bhgqk,bkhd->bqhgd', p, v)

    return _unblocks(lax.map(one, _blocks(q)))

def _diff_attend(q1, q2, k1, k2, v, lam):
    scale = HEAD_DIM ** -0.5

    def one(qs):
        qb1, qb2 = qs
        p1 = jax.nn.softmax(jnp.einsum('bqhd,bkhd->bhqk', qb1, k1).astype(F32) * scale, axis=-1)
        p2 = jax.nn.softmax(jnp.einsum('bqhd,bkhd->bhqk', qb2, k2).astype(F32) * scale, axis=-1)
        a = (p1 - lam * p2).astype(v.dtype)
        return jnp.einsum('bhqk,bkhe->bqhe', a, v)

    return _unblocks(lax.map(one, (_blocks(q1), _blocks(q2))))

def _diff_lambda(lq1, lk1, lq2, lk2, lam_init):
    return (jnp.exp(jnp.sum(lq1.astype(F32) * lk1.astype(F32)))
            - jnp.exp(jnp.sum(lq2.astype(F32) * lk2.astype(F32))) + lam_init)

def _ab_project(h, w_in, aqn, akn, bqn, bkn, rope):
    b, s, _ = h.shape
    aq, ak, av, bq, bk, bv = jnp.split(h @ w_in, list(AB_SPLITS), axis=-1)
    aq = _rmsnorm(aq.reshape(b, s, A_Q_HEADS, HEAD_DIM), aqn)
    ak = _rmsnorm(ak.reshape(b, s, A_KV_HEADS, HEAD_DIM), akn)
    av = av.reshape(b, s, A_KV_HEADS, HEAD_DIM)
    bq = _rmsnorm(bq.reshape(b, s, 2 * B_HEADS, HEAD_DIM), bqn)
    bk = _rmsnorm(bk.reshape(b, s, 2 * B_HEADS, HEAD_DIM), bkn)
    bv = bv.reshape(b, s, B_HEADS, B_V_DIM)
    if rope:
        aq, ak, bq, bk = _axial_rope(aq), _axial_rope(ak), _axial_rope(bq), _axial_rope(bk)
    bq = bq.reshape(b, s, B_HEADS, 2, HEAD_DIM)
    bk = bk.reshape(b, s, B_HEADS, 2, HEAD_DIM)
    return aq, ak, av, bq, bk, bv

def _ab_mix(aq, ak, av, bq, bk, bv, lam, lam_init, subln, w_out):
    b, s = aq.shape[:2]
    oa = _gqa_attend(aq.reshape(b, s, A_KV_HEADS, A_GROUP, HEAD_DIM), ak, av).reshape(b, s, A_Q_W)
    ob = _diff_attend(bq[..., 0, :], bq[..., 1, :], bk[..., 0, :], bk[..., 1, :], bv, lam)
    ob = (_rmsnorm(ob, subln) * (1.0 - lam_init)).reshape(b, s, B_V_W)
    return jnp.concatenate([oa, ob], axis=-1) @ w_out

def _c_project(h, w_in, qn, kn):
    b, s, _ = h.shape
    q, k, v = jnp.split(h @ w_in, 3, axis=-1)
    q = _rmsnorm(q.reshape(b, s, C_HEADS, HEAD_DIM), qn)
    k = _rmsnorm(k.reshape(b, s, C_HEADS, HEAD_DIM), kn)
    return q, k, v.reshape(b, s, C_HEADS, HEAD_DIM)

def _na_attend(q, k, v, ctx_k, ctx_v, rpb):
    b, seq, h, d = q.shape
    rows = seq // GRID_W
    kh = min(NA_ROWS, rows)
    t = ctx_k.shape[1]
    qg = q.reshape(b, rows, GRID_W, h, d)
    r = jnp.arange(rows)
    row_start = jnp.clip(r - kh // 2, 0, rows - kh)
    row_idx = row_start[:, None] + jnp.arange(kh)[None, :]
    kw = k.reshape(b, rows, GRID_W, h, d)[:, row_idx].reshape(b, rows, kh * GRID_W, h, d)
    vw = v.reshape(b, rows, GRID_W, h, d)[:, row_idx].reshape(b, rows, kh * GRID_W, h, d)
    cols = jnp.arange(GRID_W)
    col_start = jnp.clip(cols - NA_COLS // 2, 0, GRID_W - NA_COLS)
    col_in = (cols[None, :] >= col_start[:, None]) & (cols[None, :] < col_start[:, None] + NA_COLS)
    mask = jnp.broadcast_to(col_in[:, None, :], (GRID_W, kh, GRID_W)).reshape(GRID_W, kh * GRID_W)
    row_off = row_idx - r[:, None]
    col_off = jnp.clip(cols[None, :] - cols[:, None], -(NA_COLS - 1), NA_COLS - 1)
    bias = rpb[:, row_off[:, :, None, None] + (NA_ROWS - 1), col_off[None, None, :, :] + (NA_COLS - 1)]
    bias = bias.transpose(1, 0, 3, 2, 4).reshape(rows, h, GRID_W, kh * GRID_W).astype(F32)
    scale = HEAD_DIM ** -0.5
    s_lat = jnp.einsum('brqhd,brkhd->brhqk', qg, kw).astype(F32) * scale + bias[None]
    s_lat = jnp.where(mask, s_lat, -jnp.inf)
    s_ctx = jnp.einsum('brqhd,bkhd->brhqk', qg, ctx_k).astype(F32) * scale
    p = jax.nn.softmax(jnp.concatenate([s_ctx, s_lat], axis=-1), axis=-1).astype(v.dtype)
    o = (jnp.einsum('brhqk,bkhd->brqhd', p[..., :t], ctx_v)
         + jnp.einsum('brhqk,brkhd->brqhd', p[..., t:], vw))
    return o.reshape(b, seq, h * d)

def _moe(h, w_router, b_router, w_gate, w_up, w_down):
    b, s, d = h.shape
    n = h.reshape(b * s, d)
    scores = jax.nn.softmax(n.astype(F32) @ w_router.astype(F32), axis=-1)
    sel = scores + b_router.astype(F32)
    grp = lax.top_k(sel.reshape(-1, N_GROUPS, EXPERTS_PER_GROUP), TOP_K)[0].sum(-1)
    best = jnp.argmax(grp, axis=-1)
    in_group = (jnp.arange(N_EXPERTS) // EXPERTS_PER_GROUP)[None, :] == best[:, None]
    _, idx = lax.top_k(jnp.where(in_group, sel, -jnp.inf), TOP_K)
    w = jnp.take_along_axis(scores, idx, axis=-1)
    w = w / jnp.sum(w, axis=-1, keepdims=True)
    gates = jnp.sum(jax.nn.one_hot(idx, N_EXPERTS, dtype=F32) * w[..., None], axis=1)
    hid = jax.nn.silu(jnp.einsum('nd,edf->enf', n, w_gate)) * jnp.einsum('nd,edf->enf', n, w_up)
    hid = hid * gates.T[:, :, None].astype(hid.dtype)
    return jnp.einsum('enf,efd->nd', hid, w_down).reshape(b, s, d)

def setup_inputs(seed: int = 0) -> dict:
    key = jax.random.key(seed)
    ks = iter(jax.random.split(key, 40))

    def nrm(shape, scale=1.0):
        return jax.random.normal(next(ks), shape, jnp.float32) * scale

    def gain(shape):
        return 1.0 + nrm(shape, 0.02)

    D = D_MODEL
    return {
        'x_prompt': nrm((BATCH, SEQ, D)),
        'x_sample': nrm((DEC_BATCH, DEC_SEQ, D)),
        'cache_a_k': nrm((DEC_BATCH, N_EVEN, PAST_LEN, A_KV_HEADS, HEAD_DIM)),
        'cache_a_v': nrm((DEC_BATCH, N_EVEN, PAST_LEN, A_KV_HEADS, HEAD_DIM)),
        'cache_b_k': nrm((DEC_BATCH, N_EVEN, PAST_LEN, B_HEADS, 2, HEAD_DIM)),
        'cache_b_v': nrm((DEC_BATCH, N_EVEN, PAST_LEN, B_HEADS, B_V_DIM)),
        'cache_c_k': nrm((DEC_BATCH, N_ODD, PAST_LEN, C_HEADS, HEAD_DIM)),
        'cache_c_v': nrm((DEC_BATCH, N_ODD, PAST_LEN, C_HEADS, HEAD_DIM)),
        'c': nrm((DEC_BATCH, D)),
        'c_ctx': nrm((D,)),
        'w_mod': nrm((DEPTH, D, 6 * D), 0.5 * D ** -0.5),
        'b_mod': nrm((DEPTH, 6 * D), 0.02),
        'norm_mix': gain((DEPTH, D)),
        'norm_ffn': gain((DEPTH, D)),
        'w_in_ab': nrm((N_EVEN, D, AB_IN), D ** -0.5),
        'w_out_ab': nrm((N_EVEN, AB_OUT, D), AB_OUT ** -0.5),
        'a_q_norm': gain((N_EVEN, HEAD_DIM)),
        'a_k_norm': gain((N_EVEN, HEAD_DIM)),
        'b_q_norm': gain((N_EVEN, HEAD_DIM)),
        'b_k_norm': gain((N_EVEN, HEAD_DIM)),
        'lam_q1': nrm((N_EVEN, HEAD_DIM), 0.1),
        'lam_k1': nrm((N_EVEN, HEAD_DIM), 0.1),
        'lam_q2': nrm((N_EVEN, HEAD_DIM), 0.1),
        'lam_k2': nrm((N_EVEN, HEAD_DIM), 0.1),
        'b_subln': gain((N_EVEN, B_V_DIM)),
        'w_in_c': nrm((N_ODD, D, 3 * C_WIDTH), D ** -0.5),
        'w_out_c': nrm((N_ODD, C_WIDTH, D), C_WIDTH ** -0.5),
        'c_q_norm': gain((N_ODD, HEAD_DIM)),
        'c_k_norm': gain((N_ODD, HEAD_DIM)),
        'c_rpb': nrm((N_ODD, C_HEADS, 2 * NA_ROWS - 1, 2 * NA_COLS - 1), 0.1),
        'w_router': nrm((D, N_EXPERTS), D ** -0.5),
        'b_router': nrm((N_EXPERTS,), 0.01),
        'w_gate': nrm((DEPTH, N_EXPERTS, D, D_EXPERT), D ** -0.5),
        'w_up': nrm((DEPTH, N_EXPERTS, D, D_EXPERT), D ** -0.5),
        'w_down': nrm((DEPTH, N_EXPERTS, D_EXPERT, D), D_EXPERT ** -0.5),
    }

def reference(x_prompt, x_sample, cache_a_k, cache_a_v, cache_b_k, cache_b_v, cache_c_k, cache_c_v,
              c, c_ctx, w_mod, b_mod, norm_mix, norm_ffn, w_in_ab, w_out_ab, a_q_norm, a_k_norm,
              b_q_norm, b_k_norm, lam_q1, lam_k1, lam_q2, lam_k2, b_subln, w_in_c, w_out_c,
              c_q_norm, c_k_norm, c_rpb, w_router, b_router, w_gate, w_up, w_down):
    xp, xs = x_prompt, x_sample
    cond_ctx = c_ctx[None, :]
    new_a_k, new_a_v, new_b_k, new_b_v, new_c_k, new_c_v = [], [], [], [], [], []
    for l in range(DEPTH):
        sh_p, sc_p, g_p, shf_p, scf_p, gf_p = _modulation(cond_ctx, w_mod[l], b_mod[l])
        sh_s, sc_s, g_s, shf_s, scf_s, gf_s = _modulation(c, w_mod[l], b_mod[l])
        hp = _adaln(xp, norm_mix[l], sh_p, sc_p)
        hs = _adaln(xs, norm_mix[l], sh_s, sc_s)
        if l % 2 == 0:
            e = l // 2
            lam_init = 0.8 - 0.6 * math.exp(-0.3 * l)
            lam = _diff_lambda(lam_q1[e], lam_k1[e], lam_q2[e], lam_k2[e], lam_init)
            aq, ak, av, bq, bk, bv = _ab_project(hp, w_in_ab[e], a_q_norm[e], a_k_norm[e],
                                                 b_q_norm[e], b_k_norm[e], False)
            new_a_k.append(ak)
            new_a_v.append(av)
            new_b_k.append(bk)
            new_b_v.append(bv)
            op = _ab_mix(aq, ak, av, bq, bk, bv, lam, lam_init, b_subln[e], w_out_ab[e])
            aq, ak, av, bq, bk, bv = _ab_project(hs, w_in_ab[e], a_q_norm[e], a_k_norm[e],
                                                 b_q_norm[e], b_k_norm[e], True)
            os_ = _ab_mix(aq,
                          jnp.concatenate([cache_a_k[:, e], ak], axis=1),
                          jnp.concatenate([cache_a_v[:, e], av], axis=1),
                          bq,
                          jnp.concatenate([cache_b_k[:, e], bk], axis=1),
                          jnp.concatenate([cache_b_v[:, e], bv], axis=1),
                          lam, lam_init, b_subln[e], w_out_ab[e])
        else:
            o = l // 2
            q, k, v = _c_project(hp, w_in_c[o], c_q_norm[o], c_k_norm[o])
            new_c_k.append(k)
            new_c_v.append(v)
            op = _gqa_attend(q[:, :, :, None, :], k, v).reshape(xp.shape[0], xp.shape[1], C_WIDTH) @ w_out_c[o]
            q, k, v = _c_project(hs, w_in_c[o], c_q_norm[o], c_k_norm[o])
            os_ = _na_attend(q, k, v, cache_c_k[:, o], cache_c_v[:, o], c_rpb[o]) @ w_out_c[o]
        xp = xp + g_p * op
        xs = xs + g_s * os_
        xp = xp + gf_p * _moe(_adaln(xp, norm_ffn[l], shf_p, scf_p), w_router, b_router,
                              w_gate[l], w_up[l], w_down[l])
        xs = xs + gf_s * _moe(_adaln(xs, norm_ffn[l], shf_s, scf_s), w_router, b_router,
                              w_gate[l], w_up[l], w_down[l])
    return (xp, xs,
            jnp.stack(new_a_k, axis=1), jnp.stack(new_a_v, axis=1),
            jnp.stack(new_b_k, axis=1), jnp.stack(new_b_v, axis=1),
            jnp.stack(new_c_k, axis=1), jnp.stack(new_c_v, axis=1))


_drawn_inputs = setup_inputs


def setup_inputs(seed=0):
    import zlib

    import numpy as np

    out = dict(_drawn_inputs(seed))
    spreads = {}
    factors = {'cache_a_k': 4.526,
     'norm_mix': 2.965,
     'a_q_norm': 8.0,
     'a_k_norm': 2.844,
     'b_q_norm': 3.96,
     'b_k_norm': 2.806,
     'lam_q2': 3.914,
     'lam_k2': 64.0,
     'b_subln': 8.0,
     'c_q_norm': 8.0,
     'c_k_norm': 2.692,
     'c_rpb': 4.538,
     'cache_b_k': 8.0,
     'cache_b_v': 8.0,
     'cache_c_v': 3.705,
     'lam_q1': 8.0,
     'lam_k1': 5.547}
    for name, (base, spread) in spreads.items():
        noise = np.random.default_rng([zlib.crc32(name.encode()), seed]).standard_normal(out[name].shape)
        drawn = base * np.exp(spread * noise) if base else spread * noise
        out[name] = __import__('jax').numpy.asarray(drawn.astype(out[name].dtype))
    for name, factor in factors.items():
        out[name] = (out[name] * factor).astype(out[name].dtype)
    return out
```

```python
import numpy as np
import concourse.bass as bass
from concourse import mybir
from contextlib import ExitStack

F32 = mybir.dt.float32
I32 = mybir.dt.int32
ALU = mybir.AluOpType
ACT = mybir.ActivationFunctionType
AX = mybir.AxisListType

D = 1024
P = 128
DC = D // P
TT = 2
LAYERS = 2
HD = 64
GRID_W = 64
EPS = 1e-6
SCALE = HD ** -0.5
A_Q, A_KV, B_QK, B_V = 512, 128, 512, 512
AB_IN = A_Q + 2 * A_KV + 2 * B_QK + B_V
C_W = 1024
NE, NG, EG = 16, 4, 4
NA_COLS = 16
LAM_INIT = 0.2
MASKED = -1.0e30

UC = 512
SLOTS = 6
CAP = 64
ROUNDS_MAX = TT * P // CAP
PAIRS = NE // 2
MOE_UNITS = 12

CONST = {}
_at = 0
for _name, _n in (("ident", P), ("upper", P), ("ones", P), ("iota", CAP), ("sel2", 32), ("selg", 8), ("rev", P), ("mhalf", HD),
                  ("mask8", P), ("neg", P), ("low4", 16), ("cos", HD), ("ssin", HD), ("thr", ROUNDS_MAX - 1)):
    CONST[_name] = (_at, _n)
    _at += _n
NCONST = _at


def constants():
    c = np.zeros((P, NCONST), np.float32)

    def block(name):
        at, n = CONST[name]
        return c[:, at:at + n]

    row, lane = np.arange(P)[:, None], np.arange(P)[None, :]
    block("ident")[:] = row == lane
    block("upper")[:] = row < lane
    block("ones")[:] = 1.0
    block("iota")[:] = np.arange(CAP)[None, :]
    for t in range(TT):
        block("sel2")[:, t] = (np.arange(P) % 32) == t
        for k in range(4):
            block("selg")[:, 2 * k + t] = (np.arange(P) == 32 * k + t) | (np.arange(P) == 32 * k + 2)
    block("mhalf")[:] = -0.5
    block("rev")[:] = row == lane - lane % GRID_W + GRID_W - 1 - lane % GRID_W
    col = np.arange(P) % GRID_W
    first = np.clip(col - NA_COLS // 2, 0, GRID_W - NA_COLS)
    inside = (col[None, :] >= first[:, None]) & (col[None, :] < first[:, None] + NA_COLS)
    block("mask8")[:] = inside / SCALE
    block("neg")[:] = np.where(inside, 0.0, MASKED)
    block("low4")[:] = (np.arange(4)[None, :] < np.arange(4)[:, None]).reshape(1, 16)
    freq = 10000.0 ** (-np.arange(16, dtype=np.float32) / np.float32(16))
    for half, pos in enumerate((np.arange(P) // GRID_W, np.arange(P) % GRID_W)):
        angle = pos.astype(np.float32)[:, None] * freq.astype(np.float32)[None, :]
        for part, sign in ((0, -1.0), (1, 1.0)):
            at = half * 32 + part * 16
            block("cos")[:, at:at + 16] = np.cos(angle)
            block("ssin")[:, at:at + 16] = sign * np.sin(angle)
    block("thr")[:] = CAP * np.arange(1, ROUNDS_MAX)[None, :]
    return c


NORMED = {0: [(0, 8, 0), (512, 2, 1), (768, 8, 2), (1280, 8, 3)], 1: [(0, 16, 4), (1024, 16, 5)]}
SPANS = {0: [(0, 640), (768, 1792)], 1: [(0, 2048)]}
ROPED = [(0, 10), (768, 16)]
QKV_COLS = {0: AB_IN, 1: 3 * C_W}
Q_CHUNKS = {0: [0, 768], 1: [0, 512]}
O_COLS = {0: [0, 768], 1: [0, 512]}
K_JOBS = {(0, 0): 2, (0, 1): 3, (1, 0): 2, (1, 1): 4}
BATCHES = 4


def dense_units(layer):
    if layer == 0:
        return ([("mod", 0, u) for u in range(12)] + [("in", 0, u) for u in range(5)]
                + [("mod", 1, u) for u in range(12)] + [("out", 0, u) for u in range(2)])
    return [("in", 1, u) for u in range(6)] + [("out", 1, u) for u in range(2)]


def psum_jobs():
    jobs = [(("vecT",), "dve"), (("bT",), "dve")]

    def mod(l, u):
        jobs.append((("mod", l, u), "act"))
        jobs.append(((("modG" if u // 2 in (2, 5) else "modT"), l, u), "dve"))

    def norm(l, kind):
        for t in range(TT):
            jobs.append((("hT", l, kind, t, 0), "act"))
            jobs.append((("hT", l, kind, t, 1), "dve"))

    for u in range(12):
        mod(0, u)
    for l in range(LAYERS):
        norm(l, 0)
        for u in range(-(-QKV_COLS[l] // UC)):
            jobs.append((("qkv", l, u, 0), "act"))
            jobs.append((("qkv", l, u, 1), "dve"))
        if l == 0:
            for u in range(12):
                mod(1, u)
        else:
            for i in range(4):
                jobs.append((("rev", i), "dve"))
        for t in range(TT):
            for i in range(2 + K_JOBS[l, t]):
                jobs.append((("T", l, t, i), "act"))

            def scores(b):
                for e in range(2):
                    jobs.append((("S", l, t, b, e), "dve" if (l, t) == (1, 1) else "act"))

            scores(0)
            scores(1)
            for b in range(BATCHES):
                for kc in range(pt_jobs(l, t, b)):
                    jobs.append((("PT", l, t, b, kc), "act"))
                jobs.append((("O", l, t, b), "dve"))
                if b + 2 < BATCHES:
                    scores(b + 2)
        for t in range(TT):
            for h in range(2):
                jobs.append((("oT", l, t, h), "act"))
        for u in range(2):
            for t in range(TT):
                jobs.append((("gb", l, 0, u, t), "act"))
                jobs.append((("wo", l, u, t), "dve"))
        norm(l, 1)
        for t in range(TT):
            for h in range(2):
                jobs.append((("hk", l, t, h), "act"))
        jobs.append((("rt", l), "dve"))
        jobs.append((("pos", l), "dve"))
        jobs.append(None)
        for u in range(2):
            for t in range(TT):
                jobs.append((("gb", l, 1, u, t), "act"))
    return jobs


def pt_jobs(l, t, b):
    return 2 if t == 1 and (l == 1 or b < 2) else 1


def build(nc, a):
    ctx = ExitStack()
    with ctx:
        def sb(name, shape, dt=F32):
            return ctx.enter_context(nc.sbuf_tensor(name, shape, dt))

        def sem(name):
            return ctx.enter_context(nc.semaphore(name))

        ring = [sb(f"ring{i}", [P, DC, UC]) for i in range(SLOTS)]
        x = sb("x", [P, TT, D])
        hT = sb("hT", [P, DC, TT * P])
        work = sb("work", [P, 15360])
        const = sb("const", [P, NCONST])
        gates = sb("gates", [P, D])
        gbuf = sb("gbuf", [P, 2, UC])
        tmp = sb("tmp", [P, 2, UC])
        m4 = sb("m4", [P, 2, UC])
        vecs = sb("vecs", [48, P])
        bvec = sb("bvec", [96, P])
        vT = sb("vT", [P, 48])
        bT = sb("bT", [P, 96])
        sig = sb("sig", [P, 16])
        cond = sb("cond", [P, DC, 32])
        modc = sb("modc", [P, LAYERS, 4, TT, DC])
        gain = sb("gain", [P, 6, HD])
        subg = sb("subg", [P, P])
        lamv = sb("lamv", [P, 4, HD])
        lamw = sb("lamw", [P, 2, HD])
        lam = sb("lam", [P, 4])
        wr = sb("wr", [P, DC, NE])
        br = sb("br", [P, NE])
        ss = sb("ss", [P, 4])
        hss = sb("hss", [P, 64])
        nm = sb("nm", [P, 2, 4])
        rs = sb("rs", [P, 2, 4])
        rinv = sb("rinv", [P, 2, 4])
        lg = sb("lg", [P, TT, NE])
        sco = sb("sco", [P, TT, NE])
        sel = sb("sel", [P, TT, NE])
        cmp = sb("cmp", [P, 128])
        cmq = sb("cmq", [P, 128])
        top = sb("top", [P, TT, NE])
        gsum = sb("gsum", [P, TT * NG])
        chosen = sb("chosen", [P, TT, NE])
        gate = sb("gate", [P, TT, NE])
        st2 = sb("st2", [P, 4])
        cnt = sb("cnt", [P, 4])
        cnt8 = sb("cnt8", [P, TT * NG])
        rounds = sb("rounds", [P, 1], I32)
        slot_of = sb("slot_of", [P, TT, NE])
        SLOT_COLS = ROUNDS_MAX * NE + 2
        slot_t = sb("slot_t", [P, TT, SLOT_COLS])
        gate_t = sb("gate_t", [P, TT, SLOT_COLS])

        bank = [ctx.enter_context(nc.psum_tensor(f"bank{i}", [P, 512], F32)) for i in range(8)]

        def K(name):
            at, n = CONST[name]
            return const[:, at:at + n]

        qkv = [work[:, 3072 * t:3072 * (t + 1)] for t in range(TT)]
        cache = work[:, 6144:8192]
        QT = work[:, 8192:9216].rearrange("p (c q) -> p c q", c=8)
        KT = work[:, 9216:11264].rearrange("p (c k) -> p c k", c=8)
        oT = work[:, 9216:11264].rearrange("p (c q) -> p c q", c=8)
        PR = work[:, 11264:13312].rearrange("p (b h k) -> p b h k", b=2, h=4)
        PTs = work[:, 13312:15360].rearrange("p (b h q) -> p b h q", b=2, h=8)
        xn = work[:, 11264:13312].rearrange("p (t d) -> p t d", t=2)
        scratch = [work[:, 11264:13312], work[:, 13312:15360]]
        bias = hT[:, :, :].rearrange("p c n -> p (c n)").rearrange("p (h k) -> p h k", h=16)
        sc = work[:, 1024:3072].rearrange("p (b h k) -> p b h k", b=2, h=4)
        y = work[:, 0:2048].rearrange("p (t d) -> p t d", t=2)
        htok = work[:, 2048:4096].rearrange("p (t d) -> p t d", t=2)
        hgT = work[:, 4096:5120].rearrange("p (c s) -> p c s", c=8)
        yd = work[:, 5120:6144]
        sg = work[:, 8192:9216]
        hid = work[:, 9216:10240]
        hidT = work[:, 10240:11264].rearrange("p (c s) -> p c s", c=8)
        pick = work[:, 13312:13568].rearrange("p (t s) -> p t s", t=2)
        gpick = work[:, 13568:13824].rearrange("p (t s) -> p t s", t=2)
        GT = work[:, 13824:14080].rearrange("p (t q) -> p t q", t=2)

        filled = sem("bank_filled")
        emptied = {"act": sem("bank_emptied_act"), "dve": sem("bank_emptied_dve")}
        dense_ld = [sem(f"dense_loaded{i}") for i in range(SLOTS)]
        moe_used = [sem(f"moe_used{l}") for l in range(LAYERS)]
        moe_ld = [[sem(f"moe_loaded{l}_{i}") for i in range(SLOTS)] for l in range(LAYERS)]
        ld_const, ld_vec, ld_x, ld_gb, ld_small, ld_router = (
            sem(n) for n in ("ld_const", "ld_vec", "ld_x", "ld_gate_bias", "ld_small", "ld_router"))
        ld_cache = [sem(f"ld_cache{l}") for l in range(LAYERS)]
        ld_bias = sem("ld_bias")
        turns = sem("turns")
        out_kv = [sem(f"out_kv{l}") for l in range(LAYERS)]
        out_y = sem("out_y")
        cleared = sem("cleared")
        sig_ready, cond_ready, lam_dot, lam_exp, lam_ready = (
            sem(n) for n in ("sig_ready", "cond_ready", "lam_dot", "lam_exp", "lam_ready"))
        mod_ready = sem("mod_ready")
        power_asked, power_taken = sem("power_asked"), sem("power_taken")
        ssq_ready, xn_ready, x_ready = sem("ssq_ready"), sem("xn_ready"), sem("x_ready")
        squares, normed = sem("squares"), sem("qk_normed")
        max_ready, exps_ready, mixed, o_ready = (
            sem(n) for n in ("max_ready", "exps_ready", "probs_mixed", "o_ready"))
        ex_ready, mask_ready, rounds_ready = (sem(n) for n in ("router_exp", "mask_ready", "rounds_ready"))
        dve_step = sem("dve_step")
        M = [{n: sem(f"{n}{l}") for n in (
            "y_zeroed", "picked", "gathered", "hg_ready", "sig_done", "hid_done", "scattered", "y_added",
            "gt_done", "gt_ready", "ht_done", "ht_ready", "yd0_ready", "yd1_ready", "loop_step")} for l in range(LAYERS)]

        powers = {}
        for l in range(LAYERS):
            n = sum(hi - lo for lo, hi in SPANS[l]) // HD
            powers["norm", l, 0] = ss[:, 0:2]
            powers["qk", l, 0], powers["qk", l, 1] = hss[:, 0:n], hss[:, 32:32 + n]
            if l == 0:
                powers["sub", 0, 0], powers["sub", 0, 1] = hss[:, 0:4], hss[:, 0:4]
            powers["norm", l, 1] = ss[:, 0:2]

        jobs = [j for j in psum_jobs() if j]
        number = {name: k for k, (name, _) in enumerate(jobs)}
        engine_of = dict(jobs)
        done_at, seen = {}, {"act": 0, "dve": 0}
        for name, eng in jobs:
            seen[eng] += 1
            done_at[name] = seen[eng]
        after_loop, k = set(), 0
        for j in psum_jobs():
            if j is None:
                after_loop.update(range(k, k + 8))
            else:
                k += 1
        units = dense_units(0) + dense_units(1)
        N0 = len(dense_units(0))
        unit_no = {u: i for i, u in enumerate(units)}
        MOE_AT = [N0 % SLOTS, len(units) % SLOTS]

        def fill(name):
            return number[name] + 1

        def read_at(g):
            kind, l, u = units[g]
            return fill({"mod": ("mod", l, u), "in": ("qkv", l, u, 1), "out": ("wo", l, u, 1)}[kind])

        def emptied_by(name):
            return emptied[engine_of[name]], done_at[name]

        def exps_done(l, t, b):
            return (exps_ready, b + 1) if (l, t) == (1, 1) else emptied_by(("S", l, t, b, 1))

        def bank_of(name):
            return bank[number[name] % 8]

        w_in = [a["w_in_ab"][0], a["w_in_c"][0]]
        w_out = [a["w_out_ab"][0], a["w_out_c"][0]]

        def unit_cols(u):
            kind, l, i = u
            return min(UC, QKV_COLS[l] - i * UC) if kind == "in" else UC

        def unit_src(u):
            kind, l, i = u
            w = {"mod": a["w_mod"][l], "in": w_in[l], "out": w_out[l]}[kind]
            return w[:, i * UC:i * UC + unit_cols(u)].rearrange("(c p) n -> p c n", p=P)

        block = ctx.enter_context(nc.Block())

        @block.sync
        def _(sp):
            def dense(layer, rounds_of_0=None):
                for i, u in enumerate(dense_units(layer)):
                    g = N0 * layer + i
                    if layer == 1 and i < SLOTS:
                        sp.wait_ge(moe_used[0], rounds_of_0 * (PAIRS * MOE_UNITS) + (i + 1))
                    elif g >= SLOTS:
                        sp.wait_ge(filled, read_at(g - SLOTS))
                    sp.dma_start(ring[g % SLOTS][:, :, 0:unit_cols(u)], unit_src(u)).then_inc(dense_ld[g % SLOTS], 16)

            def experts(l):
                def load(k, at, wait):
                    w, half = [(a["w_gate"], 0), (a["w_up"], 0), (a["w_gate"], 1), (a["w_up"], 1),
                               (a["w_down"], 0), (a["w_down"], 1)][k // 2]
                    flat = w[l].rearrange("e k n -> (e k n)")[bass.ds(at, D * D)]
                    src = flat.rearrange("(c p n) -> p c n", p=P, n=D)[:, :, half * UC:(half + 1) * UC]
                    slot = (MOE_AT[l] + k) % SLOTS
                    if wait is not None:
                        sp.wait_ge(moe_used[l], wait)
                        sp.sem_inc(turns, 1)
                    sp.dma_start(ring[slot][:, :, :], src).then_inc(moe_ld[l][slot], 16)

                def units_of(n, i, which):
                    at = [sp.snap(i * (2 * D * D) + e * D * D) for e in range(2)]
                    for k in which:
                        load(k, at[k % 2], n * MOE_UNITS + (k + 1))

                first, later = range(SLOTS), range(SLOTS, MOE_UNITS)

                for k in range(SLOTS):
                    sp.wait_ge(filled, read_at((N0 if l == 0 else len(units)) - SLOTS + k))
                    load(k, (k % 2) * D * D, None)
                sp.wait_ge(rounds_ready, l + 1)
                r_end = sp.value_load(rounds[0:1, 0:1], min_val=1, max_val=ROUNDS_MAX)
                with sp.Fori(0, r_end) as r:
                    with sp.Fori(0, PAIRS - 1) as i:
                        units_of(r * PAIRS + i, i, later)
                        units_of(r * PAIRS + i + 1, i + 1, first)
                    units_of(r * PAIRS + (PAIRS - 1), PAIRS - 1, later)
                    with sp.If(r + 1 < r_end):
                        units_of((r + 1) * PAIRS, 0, first)
                    sp.nop()
                return r_end

            dense(0)
            r0 = experts(0)
            dense(1, r0)
            experts(1)

        @block.gpsimd
        def _(pool):
            pool.dma_start(const[:, :], a["tables"]).then_inc(ld_const, 16)
            for row, src in ((0, a["c_ctx"]), (8, a["c"]), (16, a["norm_mix"]), (32, a["norm_ffn"])):
                n = 16 if row >= 16 else 8
                flat = src if len(src.shape) == 1 else src.rearrange("a b -> (a b)")
                pool.dma_start(vecs[row:row + n, :], flat.rearrange("(r p) -> r p", p=P)).then_inc(ld_vec, 16)
            pool.dma_start(bvec[:, :], a["b_mod"].rearrange("l (r p) -> (l r) p", p=P)).then_inc(ld_vec, 16)
            pool.memset(cond[:, :, :], 0.0).then_inc(cleared, 1)
            pool.memset(gates[:, :], 0.0).then_inc(cleared, 1)
            pool.dma_start(x[:, 0, :], a["x_prompt"][0]).then_inc(ld_x, 16)
            pool.dma_start(x[:, 1, :], a["x_sample"][0]).then_inc(ld_x, 16)
            pool.wait_ge(cleared, 2)
            for l in range(LAYERS):
                for kind in range(2):
                    k = 2 * l + kind
                    at = (2 + 3 * kind) * D
                    pool.dma_start(gates[32 * k + 2:32 * k + 3, :], a["b_mod"][l:l + 1, at:at + D]).then_inc(ld_gb, 16)
            for i, name in enumerate(("a_q_norm", "a_k_norm", "b_q_norm", "b_k_norm", "c_q_norm", "c_k_norm")):
                pool.dma_start(gain[:, i, :], a[name][0].partition_broadcast(P)).then_inc(ld_small, 16)
            pool.dma_start(subg[:, :], a["b_subln"][0].partition_broadcast(P)).then_inc(ld_small, 16)
            for i, name in enumerate(("lam_q1", "lam_k1", "lam_q2", "lam_k2")):
                pool.dma_start(lamv[:, i, :], a[name][0].partition_broadcast(P)).then_inc(ld_small, 16)
            at = 0
            for name in ("cache_a_k", "cache_a_v", "cache_b_k", "cache_b_v"):
                src = a[name][0, 0]
                src = src.rearrange("k h s d -> k (h s d)") if len(src.shape) == 4 else src.rearrange("k h d -> k (h d)")
                pool.dma_start(cache[:, at:at + src.shape[1]], src).then_inc(ld_cache[0], 16)
                at += src.shape[1]
            pool.dma_start(wr[:, :, :], a["w_router"].rearrange("(c p) e -> p c e", p=P)).then_inc(ld_router, 16)
            pool.dma_start(br[:, :], a["b_router"].partition_broadcast(P)).then_inc(ld_router, 16)

            def power(*which):
                v = powers[which]
                pool.wait_ge(power_asked, list(powers).index(which) + 1)
                pool.tensor_tensor(v, v, K("mhalf")[:, 0:v.shape[1]], ALU.pow).then_inc(power_taken, 1)

            pool.wait_ge(ld_const, 16)
            for l in range(LAYERS):
                power("norm", l, 0)
                last = -(-QKV_COLS[l] // UC) - 1
                if l == 1:
                    pool.wait_ge(filled, fill(("qkv", 1, last, 1)))
                    rpb = a["c_rpb"]
                    for r in range(2):
                        for r2 in range(2):
                            src = bass.AP(rpb.tensor, rpb.offset + (r2 - r + 7) * 31 + 15 - 63, [[1, 64], [15 * 31, 16], [1, 64]])
                            pool.dma_start(bias[64 * r:64 * r + 64, :, 64 * r2:64 * r2 + 64], src).then_inc(ld_bias, 16)
                power("qk", l, 0)
                power("qk", l, 1)
                pool.wait_ge(normed, 2 * l + 1)
                pool.wait_ge(*emptied_by(("qkv", l, last, 0)))
                if l == 0:
                    outs = [("new_a_k", 512, 128), ("new_a_v", 640, 128), ("new_b_k", 1280, 512), ("new_b_v", 1792, 512)]
                else:
                    outs = [("new_c_k", 1024, 1024), ("new_c_v", 2048, 1024)]
                for name, at, n in outs:
                    pool.dma_start(a[name], qkv[0][:, at:at + n]).then_inc(out_kv[l], 16)
                if l == 0:
                    power("sub", 0, 0)
                    power("sub", 0, 1)
                    pool.wait_ge(filled, fill(("O", 0, 1, BATCHES - 1)))
                    pool.dma_start(cache[:, 0:1024], a["cache_c_k"][0, 0].rearrange("k h d -> k (h d)")).then_inc(ld_cache[1], 16)
                    pool.dma_start(cache[:, 1024:2048], a["cache_c_v"][0, 0].rearrange("k h d -> k (h d)")).then_inc(ld_cache[1], 16)
                power("norm", l, 1)
            pool.wait_ge(x_ready, 4 * 4)
            pool.dma_start(a["y_prompt"], x[:, 0, :]).then_inc(out_y, 16)
            pool.dma_start(a["y_sample"], x[:, 1, :]).then_inc(out_y, 16)
            pool.wait_ge(out_kv[0], 64)
            pool.wait_ge(out_kv[1], 32)
            pool.wait_ge(out_y, 32)

        @block.tensor
        def _(pe):
            def bank_free(name):
                k = number[name]
                if k >= 8 and k not in after_loop:
                    pe.wait_ge(*emptied_by(jobs[k - 8][0]))
                return bank_of(name)

            def arrived(u):
                g = unit_no[u]
                pe.wait_ge(dense_ld[g % SLOTS], 16 * len([h for h in range(g + 1) if h % SLOTS == g % SLOTS]))
                return ring[g % SLOTS]

            def transposes(name, parts):
                b = bank_free(name)
                for i, src in enumerate(parts):
                    ins = pe.transpose(b[:, i * P:(i + 1) * P], src, K("ident"))
                ins.then_inc(filled, 1)

            def mod(l, u):
                w = arrived(("mod", l, u))
                b = bank_free(("mod", l, u))
                for c in range(DC):
                    j = 32 * (c % 4)
                    ins = pe.matmul(b[j:j + 32, :], cond[:, c, :], w[:, c, :], start=c < 4, stop=c >= 4,
                                    tile_position=(0, j))
                ins.then_inc(filled, 1)
                v = u // 2
                name = ("modG" if v in (2, 5) else "modT", l, u)
                b = bank_free(name)
                pe.wait_ge(*emptied_by(("mod", l, u)))
                if v in (2, 5):
                    k = 2 * l + v // 5
                    ins = pe.matmul(b[32 * k:32 * k + 32, :], K("sel2"), m4[:, u % 2, :], start=True, stop=True,
                                    tile_position=(0, 32 * k))
                else:
                    for c in range(4):
                        ins = pe.matmul(b[:, 2 * c:2 * c + 2], m4[:, u % 2, c * P:(c + 1) * P], K("sel2")[:, 0:2],
                                        start=True, stop=True)
                ins.then_inc(filled, 1)

            def norm(l, kind):
                for t in range(TT):
                    pe.wait_ge(xn_ready, 4 * l + 2 * kind + t + 1)
                    for h in range(2):
                        transposes(("hT", l, kind, t, h), [xn[:, t, (4 * h + i) * P:(4 * h + i + 1) * P] for i in range(4)])

            def projection(l):
                for t in range(TT):
                    for h in range(2):
                        pe.wait_ge(*emptied_by(("hT", l, 0, t, h)))
                for u in range(-(-QKV_COLS[l] // UC)):
                    w = arrived(("in", l, u))
                    n = unit_cols(("in", l, u))
                    for t in range(TT):
                        b = bank_free(("qkv", l, u, t))
                        for c in range(DC):
                            ins = pe.matmul(b[:, 0:n], hT[:, c, t * P:(t + 1) * P], w[:, c, 0:n], start=c == 0, stop=c == DC - 1)
                        ins.then_inc(filled, 1)

            def attention(l, t):
                pe.wait_ge(normed, 2 * l + t + 1)
                pe.wait_ge(*emptied_by(("qkv", l, -(-QKV_COLS[l] // UC) - 1, t)))
                if t == 1:
                    pe.wait_ge(ld_cache[l], 16 * (4 if l == 0 else 2))
                X = qkv[t]
                chunk = lambda base, at: base[:, at:at + P]
                parts = [[chunk(X, at + i * P) for i in range(4)] for at in Q_CHUNKS[l]]
                if l == 0:
                    parts += [([chunk(cache, 0)] if t else []) + [chunk(X, 512)], [chunk(X, 1280 + i * P) for i in range(4)]]
                    if t:
                        parts += [[chunk(cache, 256 + i * P) for i in range(4)]]
                else:
                    parts += [[chunk(X, 1024 + (4 * h + i) * P) for i in range(4)] for h in range(2)]
                    if t:
                        parts += [[chunk(cache, (4 * h + i) * P) for i in range(4)] for h in range(2)]
                for i, p in enumerate(parts):
                    transposes(("T", l, t, i), p)
                for i in range(len(parts)):
                    pe.wait_ge(*emptied_by(("T", l, t, i)))
                nk = P * (1 + t)

                def scores(b):
                    banks = [bank_free(("S", l, t, b, e)) for e in range(2)]
                    for i in range(2):
                        for e in range(2):
                            h = 4 * b + 2 * i + e
                            kc = h // 2 if l == 1 else (h // 4 if h < 8 else 2 + (h - 8) // 2)
                            rows = slice(64 * e, 64 * e + 64)
                            ins = pe.matmul(banks[e][:, i * nk:(i + 1) * nk], QT[rows, h // 2, :], KT[rows, kc, 0:nk],
                                            start=True, stop=True, tile_position=(64 * e, 0))
                            if i == 1:
                                ins.then_inc(filled, 1)

                def values(b):
                    diff = l == 0 and b >= 2
                    pe.wait_ge(*((mixed, 2 * t + b - 1) if diff else exps_done(l, t, b)))
                    heads = range(2) if diff else range(4)
                    pr, pt = PR[:, b % 2], PTs[:, b % 2]
                    chunks = [(kc, h) for kc in range(1 + t) for h in heads]
                    n_jobs = pt_jobs(l, t, b)
                    per = len(chunks) // n_jobs
                    for k in range(n_jobs):
                        transposes(("PT", l, t, b, k), [pr[:, h, kc * P:(kc + 1) * P] for kc, h in chunks[k * per:(k + 1) * per]])
                    ob = bank_free(("O", l, t, b))
                    for k in range(n_jobs):
                        pe.wait_ge(*emptied_by(("PT", l, t, b, k)))
                    width = 2 * HD if diff else HD
                    for h in heads:
                        head = 4 * b + 2 * (h % 2) + h // 2
                        own, kept = {(0, False): (640 + HD * b, 128 + HD * b),
                                     (0, True): (1792 + P * (2 * (b - 2) + h), 768 + P * (2 * (b - 2) + h)),
                                     (1, False): (2 * C_W + HD * head, C_W + HD * head)}[l, diff]
                        for kc in range(1 + t):
                            v = cache[:, kept:kept + width] if kc < t else X[:, own:own + width]
                            ins = pe.matmul(ob[:, h * width:(h + 1) * width], pt[:, kc * len(heads) + h, :], v,
                                            start=kc == 0, stop=kc == t)
                    ins.then_inc(filled, 1)

                scores(0)
                scores(1)
                for b in range(BATCHES):
                    values(b)
                    if b + 2 < BATCHES:
                        scores(b + 2)

            def gate_rows(l, kind, u, t):
                name = ("gb", l, kind, u, t)
                b = bank_free(name)
                k = 2 * l + kind
                pe.matmul(b[:, :], K("selg")[:, 2 * k + t:2 * k + t + 1].to_broadcast([P, P]),
                          gates[:, u * UC:(u + 1) * UC], start=True, stop=True).then_inc(filled, 1)

            def out_projection(l):
                for t in range(TT):
                    pe.wait_ge(*((o_ready, t + 1) if l == 0 else emptied_by(("O", 1, t, BATCHES - 1))))
                    for h in range(2):
                        at = O_COLS[l][h]
                        transposes(("oT", l, t, h), [qkv[t][:, at + i * P:at + (i + 1) * P] for i in range(4)])
                for t in range(TT):
                    for h in range(2):
                        pe.wait_ge(*emptied_by(("oT", l, t, h)))
                for u in range(2):
                    w = arrived(("out", l, u))
                    for t in range(TT):
                        gate_rows(l, 0, u, t)
                        b = bank_free(("wo", l, u, t))
                        for c in range(DC):
                            ins = pe.matmul(b[:, :], oT[:, c, t * P:(t + 1) * P], w[:, c, :], start=c == 0, stop=c == DC - 1)
                        ins.then_inc(filled, 1)

            def router(l):
                for t in range(TT):
                    for h in range(2):
                        pe.wait_ge(*emptied_by(("hT", l, 1, t, h)))
                for t in range(TT):
                    for h in range(2):
                        transposes(("hk", l, t, h), [hT[:, 4 * h + i, t * P:(t + 1) * P] for i in range(4)])
                pe.wait_ge(ld_router, 32)
                b = bank_free(("rt", l))
                for t in range(TT):
                    for c in range(DC):
                        ins = pe.matmul(b[:, t * NE:(t + 1) * NE], hT[:, c, t * P:(t + 1) * P], wr[:, c, :], start=c == 0, stop=c == DC - 1)
                ins.then_inc(filled, 1)
                pe.wait_ge(mask_ready, l + 1)
                b = bank_free(("pos", l))
                pe.matmul(b[:, 0:16], K("upper"), chosen[:, 0, :], start=True, stop=True)
                pe.matmul(b[:, 16:32], K("upper"), chosen[:, 1, :], start=True, stop=False)
                pe.matmul(b[:, 16:32], K("ones"), chosen[:, 0, :], start=False, stop=True)
                pe.matmul(b[:, 32:48], K("ones"), chosen[:, 0, :], start=True, stop=False)
                pe.matmul(b[:, 32:48], K("ones"), chosen[:, 1, :], start=False, stop=True).then_inc(filled, 1)

            def experts(l):
                m = M[l]

                def gather(n):
                    pe.wait_ge(m["picked"], n + 1)
                    for h in range(2):
                        for c in range(4):
                            for t in range(TT):
                                at = (4 * h + c) * P
                                ins = pe.matmul(bank[h][:, c * P:(c + 1) * P], htok[:, t, at:at + P], pick[:, t, :],
                                                start=t == 0, stop=t == 1)
                        ins.then_inc(m["gathered"], 1)

                def scatter(n):
                    pe.wait_ge(m["yd0_ready"], n + 1)
                    pe.wait_ge(m["yd1_ready"], n + 1)
                    for t in range(TT):
                        for h in range(2):
                            pe.matmul(bank[4 + 2 * t + h][:, :], GT[:, t, :], yd[:, h * UC:(h + 1) * UC],
                                      start=True, stop=True).then_inc(m["scattered"], 1)

                def product(n, k, b, lhs):
                    slots = [(MOE_AT[l] + k + e) % SLOTS for e in range(2)]
                    for e in range(2):
                        pe.wait_ge(moe_ld[l][slots[e]], 32 * n + 16 * (1 + k // SLOTS))
                    for c in range(DC):
                        for e in range(2):
                            ins = pe.matmul(bank[b][64 * e:64 * e + 64, :], lhs[:, c, 64 * e:64 * e + 64], ring[slots[e]][:, c, :],
                                            start=c == 0, stop=c == DC - 1, tile_position=(0, 64 * e))
                            if c == DC - 1:
                                ins.then_inc(moe_used[l], 1)

                last = number[("pos", l)]
                for k in range(last - 7, last + 1):
                    pe.wait_ge(*emptied_by(jobs[k][0]))
                pe.wait_ge(rounds_ready, l + 1)
                r_end = pe.value_load(rounds[0:1, 0:1], min_val=1, max_val=ROUNDS_MAX)
                pe.wait_ge(m["y_zeroed"], 1)
                for t in range(TT):
                    for h in range(2):
                        pe.wait_ge(*emptied_by(("hk", l, t, h)))
                pe.sem_inc(moe_used[l], SLOTS)
                gather(0)
                with pe.Fori(0, r_end * PAIRS) as n:
                    pe.wait_ge(m["hg_ready"], 2 * n + 2)
                    product(n, 0, 0, hgT)
                    product(n, 2, 1, hgT)
                    scatter(n)
                    for t in range(TT):
                        ins = pe.transpose(bank[3][:, t * P:(t + 1) * P], gpick[:, t, :], K("ident"))
                    ins.then_inc(m["gt_done"], 1)
                    product(n, 4, 2, hgT)
                    pe.wait_ge(m["gt_ready"], n + 1)
                    product(n, 6, 3, hgT)
                    pe.wait_ge(m["hid_done"], 2 * n + 1)
                    pe.wait_ge(m["y_added"], 4 * n + 4)
                    for c in range(4):
                        ins = pe.transpose(bank[4][:, c * P:(c + 1) * P], hid[:, c * P:(c + 1) * P], K("ident"))
                    ins.then_inc(m["ht_done"], 1)
                    gather(n + 1)
                    pe.wait_ge(m["hid_done"], 2 * n + 2)
                    for c in range(4):
                        ins = pe.transpose(bank[5][:, c * P:(c + 1) * P], hid[:, (4 + c) * P:(5 + c) * P], K("ident"))
                    ins.then_inc(m["ht_done"], 1)
                    pe.wait_ge(m["ht_ready"], 2 * n + 2)
                    product(n, 8, 6, hidT)
                    product(n, 10, 7, hidT)
                scatter(r_end * PAIRS)
                pe.wait_ge(m["y_added"], r_end * (4 * PAIRS) + 4)
                pe.wait_ge(m["hg_ready"], r_end * (2 * PAIRS) + 2)
                for u in range(2):
                    for t in range(TT):
                        gate_rows(l, 1, u, t)

            pe.wait_ge(ld_const, 16)
            pe.wait_ge(ld_vec, 80)
            pe.transpose(bank_free(("vecT",))[:, 0:48], vecs[:, :], K("ident")[0:48, 0:48]).then_inc(filled, 1)
            pe.transpose(bank_free(("bT",))[:, 0:96], bvec[:, :], K("ident")[0:96, 0:96]).then_inc(filled, 1)
            pe.wait_ge(cond_ready, 1)
            for u in range(12):
                mod(0, u)
            for l in range(LAYERS):
                norm(l, 0)
                projection(l)
                if l == 0:
                    for u in range(12):
                        mod(1, u)
                    pe.wait_ge(ld_gb, 64)
                else:
                    pe.wait_ge(ld_bias, 64)
                    for i in range(4):
                        pe.matmul(bank_free(("rev", i))[:, :], K("rev"), bias[:, 4 * i:4 * i + 4, :], start=True, stop=True).then_inc(filled, 1)
                for t in range(TT):
                    attention(l, t)
                out_projection(l)
                norm(l, 1)
                router(l)
                experts(l)

        @block.scalar
        def _(act):
            def mod(l, u):
                act.wait_ge(filled, fill(("mod", l, u)))
                if 12 * l + u >= 2:
                    pl, pu = divmod(12 * l + u - 2, 12)
                    act.wait_ge(filled, fill(("modG" if pu // 2 in (2, 5) else "modT", pl, pu)))
                act.activation(m4[:, u % 2, :], bank_of(("mod", l, u))[:, :], ACT.Copy).then_inc(emptied["act"], 1)

            def norm(l, kind):
                act.wait_ge(*((ld_x, 32) if (l, kind) == (0, 0) else (x_ready, 4 * (2 * l + kind))))
                for t in range(TT):
                    act.activation(xn[:, t, :], x[:, t, :], ACT.Square, accum_out=ss[:, t:t + 1]).then_inc(ssq_ready, 1)
                act.wait_ge(mod_ready, 4 * l + 2 * kind + 2)
                for t in range(TT):
                    name = ("hT", l, kind, t, 0)
                    act.wait_ge(filled, fill(name))
                    for c in range(4):
                        ins = act.activation(hT[:, c, t * P:(t + 1) * P], bank_of(name)[:, c * P:(c + 1) * P], ACT.Identity,
                                             bias=modc[:, l, 2 * kind, t, c:c + 1], scale=modc[:, l, 2 * kind + 1, t, c:c + 1])
                    ins.then_inc(emptied["act"], 1)

            def projection(l):
                last = -(-QKV_COLS[l] // UC) - 1
                for u in range(last + 1):
                    name, n = ("qkv", l, u, 0), unit_cols(("in", l, u))
                    act.wait_ge(filled, fill(name))
                    act.activation(qkv[0][:, u * UC:u * UC + n], bank_of(name)[:, 0:n], ACT.Copy).then_inc(emptied["act"], 1)
                for t in range(TT):
                    act.wait_ge(*emptied_by(("qkv", l, last, t)))
                    for lo, hi in SPANS[l]:
                        ins = act.activation(scratch[t][:, lo:hi], qkv[t][:, lo:hi], ACT.Square)
                    ins.then_inc(squares, 1)

            def transposed(l, t):
                own = P * t
                for i in range(2 + K_JOBS[l, t]):
                    name = ("T", l, t, i)
                    act.wait_ge(filled, fill(name))
                    src = bank_of(name)[:, :].rearrange("p (c q) -> p c q", c=4)
                    if i < 2:
                        dst = QT[:, 4 * i:4 * i + 4, :]
                    elif l == 1:
                        at = 0 if i >= 4 else own
                        dst = KT[:, 4 * (i % 2):4 * (i % 2) + 4, at:at + P]
                    elif i == 2:
                        for kv in range(2):
                            for half in range(2):
                                ins = act.activation(KT[64 * half:64 * half + 64, kv, 0:own + P],
                                                     bank_of(name)[64 * kv:64 * kv + 64, 0:own + P], ACT.Copy)
                        ins.then_inc(emptied["act"], 1)
                        continue
                    else:
                        at = 0 if i == 4 else own
                        dst = KT[:, 2:6, at:at + P]
                    act.activation(dst, src, ACT.Copy).then_inc(emptied["act"], 1)

            def exps(l, t, b):
                nk = P * (1 + t)
                banked = (l, t) != (1, 1)
                act.wait_ge(max_ready, (l * TT + t) * BATCHES + b + 1)
                if b >= 2:
                    act.wait_ge(filled, fill(("PT", l, t, b - 2, pt_jobs(l, t, b - 2) - 1)))
                for e in range(2):
                    for i in range(2):
                        j = 2 * e + i
                        src = bank_of(("S", l, t, b, e))[:, i * nk:(i + 1) * nk] if banked else sc[:, b % 2, j, :]
                        ins = act.activation(PR[:, b % 2, j, 0:nk], src, ACT.Exp, bias=nm[:, b % 2, j:j + 1],
                                             scale=SCALE, accum_out=rs[:, b % 2, j:j + 1])
                    if banked:
                        ins.then_inc(emptied["act"], 1)
                if not banked:
                    ins.then_inc(exps_ready, 1)

            def probs_transposed(l, t, b):
                heads = 2 if l == 0 and b >= 2 else 4
                per = heads * (1 + t) // pt_jobs(l, t, b)
                for k in range(pt_jobs(l, t, b)):
                    name = ("PT", l, t, b, k)
                    act.wait_ge(filled, fill(name))
                    act.activation(PTs[:, b % 2, k * per:(k + 1) * per, :],
                                   bank_of(name)[:, 0:per * P].rearrange("p (c q) -> p c q", c=per),
                                   ACT.Copy).then_inc(emptied["act"], 1)

            def spread_gate(l, kind, u, t):
                name, k = ("gb", l, kind, u, t), 4 * (2 * l + kind) + 2 * u + t
                act.wait_ge(filled, fill(name))
                if k >= 2:
                    act.wait_ge(x_ready, k - 1)
                act.activation(gbuf[:, k % 2, :], bank_of(name)[:, :], ACT.Copy).then_inc(emptied["act"], 1)

            def experts(l):
                m = M[l]
                act.wait_ge(rounds_ready, l + 1)
                r_end = act.value_load(rounds[0:1, 0:1], min_val=1, max_val=ROUNDS_MAX)
                act.activation(yd[:, UC:2 * UC], const[:, 0:UC], ACT.Copy, scale=0.0).then_inc(m["yd1_ready"], 1)

                def gathered(n):
                    for h in range(2):
                        act.wait_ge(m["gathered"], 2 * n + h + 1)
                        act.activation(hgT[:, 4 * h:4 * h + 4, :], bank[h][:, :].rearrange("p (c s) -> p c s", c=4),
                                       ACT.Copy).then_inc(m["hg_ready"], 1)

                def hidden_transposed(n, h):
                    act.wait_ge(m["ht_done"], 2 * n + h + 1)
                    act.activation(hidT[:, 4 * h:4 * h + 4, :], bank[4 + h][:, :].rearrange("p (c s) -> p c s", c=4),
                                   ACT.Copy).then_inc(m["ht_ready"], 1)

                def sigmoid(n, h):
                    act.wait_ge(moe_used[l], n * MOE_UNITS + (SLOTS + 4 * h + 2))
                    act.activation(sg[:, h * UC:(h + 1) * UC], bank[2 * h][:, :], ACT.Sigmoid).then_inc(m["sig_done"], 1)

                gathered(0)
                with act.Fori(0, r_end * PAIRS) as n:
                    sigmoid(n, 0)
                    act.wait_ge(m["gt_done"], n + 1)
                    act.activation(GT[:, :, :], bank[3][:, 0:2 * P].rearrange("p (t q) -> p t q", t=2),
                                   ACT.Copy).then_inc(m["gt_ready"], 1)
                    sigmoid(n, 1)
                    hidden_transposed(n, 0)
                    gathered(n + 1)
                    hidden_transposed(n, 1)
                    act.wait_ge(moe_used[l], n * MOE_UNITS + (SLOTS + 12))
                    act.activation(yd[:, UC:2 * UC], bank[7][:, :], ACT.Copy).then_inc(m["yd1_ready"], 1)

            act.wait_ge(*emptied_by(("vecT",)))
            act.activation(sig[:, :], vT[:, 0:16], ACT.Sigmoid).then_inc(sig_ready, 1)
            for u in range(12):
                mod(0, u)
            for l in range(LAYERS):
                norm(l, 0)
                projection(l)
                if l == 0:
                    for u in range(12):
                        mod(1, u)
                    act.wait_ge(lam_dot, 1)
                    act.activation(lam[:, 2:4], lam[:, 0:2], ACT.Exp).then_inc(lam_exp, 1)
                for t in range(TT):
                    transposed(l, t)
                    exps(l, t, 0)
                    exps(l, t, 1)
                    for b in range(BATCHES):
                        probs_transposed(l, t, b)
                        if b + 2 < BATCHES:
                            exps(l, t, b + 2)
                for t in range(TT):
                    for h in range(2):
                        name = ("oT", l, t, h)
                        act.wait_ge(filled, fill(name))
                        act.activation(oT[:, 4 * h:4 * h + 4, t * P:(t + 1) * P],
                                       bank_of(name)[:, :].rearrange("p (c q) -> p c q", c=4), ACT.Copy).then_inc(emptied["act"], 1)
                for u in range(2):
                    for t in range(TT):
                        spread_gate(l, 0, u, t)
                norm(l, 1)
                act.wait_ge(out_kv[l], 64 if l == 0 else 32)
                for t in range(TT):
                    for h in range(2):
                        name = ("hk", l, t, h)
                        act.wait_ge(filled, fill(name))
                        act.activation(htok[:, t, h * UC:(h + 1) * UC], bank_of(name)[:, :], ACT.Copy).then_inc(emptied["act"], 1)
                act.wait_ge(*emptied_by(("rt", l)))
                act.activation(sco[:, :, :], lg[:, :, :], ACT.Exp).then_inc(ex_ready, 1)
                experts(l)
                for u in range(2):
                    for t in range(TT):
                        spread_gate(l, 1, u, t)

        @block.vector
        def _(dve):
            steps = [0]

            def then(ins):
                steps[0] += 1
                ins.then_inc(dve_step, 1)
                dve.wait_ge(dve_step, steps[0])

            def rms_inverse(which, n):
                v = powers[which]
                dve.tensor_scalar(v, v, 1.0 / n, EPS, ALU.mult, ALU.add).then_inc(power_asked, 1)
                dve.wait_ge(power_taken, list(powers).index(which) + 1)

            def mod(l, u):
                v = u // 2
                if v in (2, 5):
                    name, k = ("modG", l, u), 2 * l + v // 5
                    dve.wait_ge(filled, fill(name))
                    at = (u % 2) * UC
                    dve.tensor_copy(gates[32 * k:32 * k + 2, at:at + UC], bank_of(name)[32 * k:32 * k + 2, :]).then_inc(emptied["dve"], 1)
                    return
                name, v4, c0 = ("modT", l, u), v - v // 3, 4 * (u % 2)
                dve.wait_ge(filled, fill(name))
                dst = modc[:, l, v4, :, c0:c0 + 4]
                bias_cols = bT[:, 48 * l + 8 * v + c0:48 * l + 8 * v + c0 + 4]
                dve.tensor_tensor(dst, bank_of(name)[:, 0:8].rearrange("p (c t) -> p t c", t=2),
                                  bias_cols.unsqueeze(1).to_broadcast([P, TT, 4]), ALU.add).then_inc(emptied["dve"], 1)
                if v4 % 2:
                    g0 = 16 + 16 * (v4 // 2) + 8 * l + c0
                    dve.wait_ge(*emptied_by(name))
                    dve.scalar_tensor_tensor(out=dst, in0=dst, scalar=1.0, in1=vT[:, g0:g0 + 4].unsqueeze(1).to_broadcast([P, TT, 4]),
                                             op0=ALU.add, op1=ALU.mult).then_inc(mod_ready, 1)

            def norm(l, kind):
                dve.wait_ge(ssq_ready, 2 * (2 * l + kind) + 2)
                rms_inverse(("norm", l, kind), D)
                for t in range(TT):
                    dve.tensor_scalar(xn[:, t, :], x[:, t, :], ss[:, t:t + 1], None, ALU.mult).then_inc(xn_ready, 1)
                dve.wait_ge(mod_ready, 4 * l + 2 * kind + 2)
                for t in range(TT):
                    name = ("hT", l, kind, t, 1)
                    dve.wait_ge(filled, fill(name))
                    for c in range(4):
                        ins = dve.tensor_scalar(hT[:, 4 + c, t * P:(t + 1) * P], bank_of(name)[:, c * P:(c + 1) * P],
                                                modc[:, l, 2 * kind + 1, t, 4 + c:5 + c], modc[:, l, 2 * kind, t, 4 + c:5 + c],
                                                ALU.mult, ALU.add)
                    ins.then_inc(emptied["dve"], 1)

            def projection(l):
                for u in range(-(-QKV_COLS[l] // UC)):
                    name, n = ("qkv", l, u, 1), unit_cols(("in", l, u))
                    dve.wait_ge(filled, fill(name))
                    dve.tensor_copy(qkv[1][:, u * UC:u * UC + n], bank_of(name)[:, 0:n]).then_inc(emptied["dve"], 1)

            def heads_of(t, lo, n):
                return qkv[t][:, lo:lo + n * HD].rearrange("p (h d) -> p h d", d=HD)

            def qk_norm(l, t):
                dve.wait_ge(squares, 2 * l + t + 1)
                at, parts = 32 * t, []
                for lo, hi in SPANS[l]:
                    n = (hi - lo) // HD
                    parts.append((lo, n, at))
                    ins = dve.tensor_reduce(hss[:, at:at + n], scratch[t][:, lo:hi].rearrange("p (h d) -> p h d", d=HD), AX.X, ALU.add)
                    at += n
                then(ins)
                rms_inverse(("qk", l, t), HD)
                for lo, n, c in parts:
                    v = heads_of(t, lo, n)
                    ins = dve.tensor_tensor(v, v, hss[:, c:c + n].unsqueeze(2).to_broadcast([P, n, HD]), ALU.mult)
                then(ins)
                for lo, n, g in NORMED[l]:
                    v = heads_of(t, lo, n)
                    ins = dve.tensor_tensor(v, v, gain[:, g, :].unsqueeze(1).to_broadcast([P, n, HD]), ALU.mult)
                if (l, t) != (0, 1):
                    ins.then_inc(normed, 1)
                    return
                then(ins)
                cos, ssin = K("cos"), K("ssin").rearrange("p (a b f) -> p a b f", a=2, b=2)
                for lo, n in ROPED:
                    v = qkv[t][:, lo:lo + n * HD].rearrange("p (h a b f) -> p h a b f", a=2, b=2, f=16)
                    w = scratch[t][:, lo:lo + n * HD].rearrange("p (h a b f) -> p h a b f", a=2, b=2, f=16)
                    for part in range(2):
                        ins = dve.tensor_tensor(w[:, :, :, part, :], v[:, :, :, 1 - part, :],
                                                ssin[:, :, part, :].unsqueeze(1).to_broadcast([P, n, 2, 16]), ALU.mult)
                then(ins)
                for lo, n in ROPED:
                    v = heads_of(t, lo, n)
                    ins = dve.tensor_tensor(v, v, cos.unsqueeze(1).to_broadcast([P, n, HD]), ALU.mult)
                then(ins)
                for lo, n in ROPED:
                    ins = dve.tensor_tensor(qkv[t][:, lo:lo + n * HD], qkv[t][:, lo:lo + n * HD], scratch[t][:, lo:lo + n * HD], ALU.add)
                ins.then_inc(normed, 1)

            def maxima(l, t, b):
                nk = P * (1 + t)
                if b >= 2:
                    dve.wait_ge(*exps_done(l, t, b - 2))
                for e in range(2):
                    name = ("S", l, t, b, e)
                    dve.wait_ge(filled, fill(name))
                    s = bank_of(name)[:, 0:2 * nk].rearrange("p (h k) -> p h k", h=2)
                    if (l, t) == (1, 1):
                        dve.tensor_copy(sc[:, b % 2, 2 * e:2 * e + 2, 0:P], s[:, :, 0:P])
                        dve.tensor_tensor(sc[:, b % 2, 2 * e:2 * e + 2, P:2 * P], s[:, :, P:2 * P],
                                          bias[:, 4 * b + e:4 * b + e + 3:2, :], ALU.add).then_inc(emptied["dve"], 1)
                        dve.wait_ge(*emptied_by(name))
                        s = sc[:, b % 2, 2 * e:2 * e + 2, :]
                    ins = dve.tensor_reduce(nm[:, b % 2, 2 * e:2 * e + 2], s, AX.X, ALU.max, negate=True)
                then(ins)
                dve.tensor_scalar(nm[:, b % 2, :], nm[:, b % 2, :], SCALE, None, ALU.mult).then_inc(max_ready, 1)

            def shares(l, t, b):
                nk = P * (1 + t)
                dve.wait_ge(*exps_done(l, t, b))
                then(dve.reciprocal(rinv[:, b % 2, :], rs[:, b % 2, :]))
                if l == 0 and b >= 2:
                    then(dve.tensor_scalar(rinv[:, b % 2, 2:4], rinv[:, b % 2, 2:4], lam[:, 0:1], None, ALU.mult))
                    for i in range(2):
                        ins = dve.tensor_scalar(PR[:, b % 2, 2 + i, 0:nk], PR[:, b % 2, 2 + i, 0:nk], rinv[:, b % 2, 2 + i:3 + i], None, ALU.mult)
                    then(ins)
                    for i in range(2):
                        ins = dve.scalar_tensor_tensor(out=PR[:, b % 2, i, 0:nk], in0=PR[:, b % 2, i, 0:nk], scalar=rinv[:, b % 2, i:i + 1],
                                                       in1=PR[:, b % 2, 2 + i, 0:nk], op0=ALU.mult, op1=ALU.add)
                    ins.then_inc(mixed, 1)

            def outputs(l, t, b):
                name = ("O", l, t, b)
                dve.wait_ge(filled, fill(name))
                if l == 0 and b >= 2:
                    at = 768 + 256 * (b - 2)
                    dve.tensor_copy(qkv[t][:, at:at + 256], bank_of(name)[:, 0:256]).then_inc(emptied["dve"], 1)
                    return
                dst = qkv[t][:, 256 * b:256 * b + 256].rearrange("p (i e d) -> p e i d", i=2, e=2)
                src = bank_of(name)[:, 0:256].rearrange("p (e i d) -> p e i d", e=2, i=2)
                share = rinv[:, b % 2, :].rearrange("p (e i) -> p e i", e=2).unsqueeze(3).to_broadcast([P, 2, 2, HD])
                dve.tensor_tensor(dst, src, share, ALU.mult).then_inc(emptied["dve"], 1)

            def sub_norm(t):
                v = qkv[t][:, 768:1280].rearrange("p (h d) -> p h d", h=4)
                w = tmp[:, t, :].rearrange("p (h d) -> p h d", h=4)
                dve.wait_ge(*emptied_by(("O", 0, t, BATCHES - 1)))
                then(dve.tensor_tensor(w, v, v, ALU.mult))
                then(dve.tensor_reduce(hss[:, 0:4], w, AX.X, ALU.add))
                rms_inverse(("sub", 0, t), 2 * HD)
                then(dve.tensor_tensor(v, v, hss[:, 0:4].unsqueeze(2).to_broadcast([P, 4, 2 * HD]), ALU.mult))
                dve.tensor_tensor(v, v, subg[:, :].unsqueeze(1).to_broadcast([P, 4, 2 * HD]), ALU.mult).then_inc(o_ready, 1)

            def add_gated(l, kind):
                for u in range(2):
                    for t in range(TT):
                        k = 2 * u + t
                        dve.wait_ge(*emptied_by(("gb", l, kind, u, t)))
                        cols = slice(u * UC, (u + 1) * UC)
                        if kind == 0:
                            name = ("wo", l, u, t)
                            dve.wait_ge(filled, fill(name))
                            dve.tensor_tensor(tmp[:, k % 2, :], bank_of(name)[:, :], gbuf[:, k % 2, :], ALU.mult).then_inc(emptied["dve"], 1)
                            dve.wait_ge(*emptied_by(name))
                        else:
                            then(dve.tensor_tensor(tmp[:, k % 2, :], y[:, t, cols], gbuf[:, k % 2, :], ALU.mult))
                        dve.tensor_tensor(x[:, t, cols], x[:, t, cols], tmp[:, k % 2, :], ALU.add).then_inc(x_ready, 1)

            def beaten(out, values, groups, width):
                v = values.rearrange("p (g i) -> p g i", i=width)
                mine = v.unsqueeze(3).to_broadcast([P, groups, width, width])
                others = v.unsqueeze(2).to_broadcast([P, groups, width, width])
                n = groups * width * width
                more = cmp[:, 0:n].rearrange("p (g i j) -> p g i j", i=width, j=width)
                same = cmq[:, 0:n].rearrange("p (g i j) -> p g i j", i=width, j=width)
                dve.tensor_tensor(more, others, mine, ALU.is_gt)
                then(dve.tensor_tensor(same, others, mine, ALU.is_equal))
                low = K("low4").rearrange("p (i j) -> p i j", i=4).unsqueeze(1).to_broadcast([P, groups, width, width])
                then(dve.tensor_tensor(same, same, low, ALU.mult))
                then(dve.tensor_tensor(more, more, same, ALU.add))
                then(dve.tensor_reduce(out.rearrange("p (g i) -> p g i", i=width), more, AX.X, ALU.add))

            def router(l):
                flat = lambda v: v[:, :, :].rearrange("p t e -> p (t e)")
                per_token = lambda v: v.unsqueeze(2).to_broadcast([P, TT, NE])
                dve.wait_ge(filled, fill(("rt", l)))
                logits = bank_of(("rt", l))[:, 0:TT * NE].rearrange("p (t e) -> p t e", t=TT)
                then(dve.tensor_reduce(st2[:, 0:2], logits, AX.X, ALU.max))
                dve.tensor_tensor(lg[:, :, :], logits, per_token(st2[:, 0:2]), ALU.subtract).then_inc(emptied["dve"], 1)
                dve.wait_ge(*emptied_by(("rt", l)))
                dve.wait_ge(ex_ready, l + 1)
                then(dve.tensor_reduce(st2[:, 2:4], sco[:, :, :], AX.X, ALU.add))
                then(dve.reciprocal(st2[:, 2:4], st2[:, 2:4]))
                then(dve.tensor_tensor(sco[:, :, :], sco[:, :, :], per_token(st2[:, 2:4]), ALU.mult))
                then(dve.tensor_tensor(sel[:, :, :], sco[:, :, :], br[:, :].unsqueeze(1).to_broadcast([P, TT, NE]), ALU.add))
                beaten(flat(top), flat(sel), TT * NG, EG)
                then(dve.tensor_scalar(flat(top), flat(top), float(EG - 2), None, ALU.is_lt))
                then(dve.tensor_tensor(flat(chosen), flat(sel), flat(top), ALU.mult))
                then(dve.tensor_reduce(gsum[:, :], flat(chosen).rearrange("p (g i) -> p g i", i=EG), AX.X, ALU.add))
                beaten(cnt8[:, :], gsum[:, :], TT, NG)
                then(dve.tensor_scalar(cnt8[:, :], cnt8[:, :], 0.0, None, ALU.is_equal))
                dve.tensor_tensor(flat(chosen).rearrange("p (g i) -> p g i", i=EG), flat(top).rearrange("p (g i) -> p g i", i=EG),
                                  cnt8[:, :].unsqueeze(2).to_broadcast([P, TT * NG, EG]), ALU.mult).then_inc(mask_ready, 1)
                dve.wait_ge(mask_ready, l + 1)
                then(dve.tensor_tensor(gate[:, :, :], sco[:, :, :], chosen[:, :, :], ALU.mult))
                then(dve.tensor_reduce(st2[:, 0:2], gate[:, :, :], AX.X, ALU.add))
                then(dve.reciprocal(st2[:, 0:2], st2[:, 0:2]))
                then(dve.tensor_tensor(gate[:, :, :], gate[:, :, :], per_token(st2[:, 0:2]), ALU.mult))
                name = ("pos", l)
                dve.wait_ge(filled, fill(name))
                b = bank_of(name)
                then(dve.tensor_reduce(cnt[:, 0:1], b[:, 32:48], AX.X, ALU.max))
                dve.scalar_tensor_tensor(out=slot_of[:, :, :], in0=b[:, 0:32].rearrange("p (t e) -> p t e", t=TT), scalar=1.0,
                                         in1=chosen[:, :, :], op0=ALU.add, op1=ALU.mult).then_inc(emptied["dve"], 1)
                dve.wait_ge(*emptied_by(name))
                dve.memset(slot_t[:, :, ROUNDS_MAX * NE:], -1.0)
                dve.memset(gate_t[:, :, ROUNDS_MAX * NE:], 0.0)
                for r in range(ROUNDS_MAX):
                    dve.tensor_scalar(slot_t[:, :, r * NE:(r + 1) * NE], slot_of[:, :, :], -1.0 - CAP * r, None, ALU.add)
                    ins = dve.tensor_copy(gate_t[:, :, r * NE:(r + 1) * NE], gate[:, :, :])
                then(ins)
                then(dve.tensor_scalar(cmp[:, 0:ROUNDS_MAX - 1], K("thr"), cnt[:, 0:1], None, ALU.is_lt))
                then(dve.tensor_reduce(cnt[:, 1:2], cmp[:, 0:ROUNDS_MAX - 1], AX.X, ALU.add))
                dve.tensor_scalar(rounds[:, :], cnt[:, 1:2], 1.0, None, ALU.add).then_inc(rounds_ready, 1)
                dve.wait_ge(rounds_ready, l + 1)

            def experts(l):
                m = M[l]
                dve.wait_ge(out_kv[l], 64 if l == 0 else 32)
                dve.memset(work[:, 0:2048], 0.0)
                dve.memset(GT[:, :, :], 0.0).then_inc(m["y_zeroed"], 1)
                dve.memset(yd[:, 0:UC], 0.0).then_inc(m["yd0_ready"], 1)
                r_end = dve.value_load(rounds[0:1, 0:1], min_val=1, max_val=ROUNDS_MAX)

                def one_hots(n):
                    for t in range(TT):
                        for e in range(2):
                            col = bass.ds(2 * n + e, 1)
                            dve.tensor_scalar(pick[:, t, CAP * e:CAP * e + CAP], K("iota"), slot_t[:, t, col], None, ALU.is_equal)
                            ins = dve.tensor_scalar(gpick[:, t, CAP * e:CAP * e + CAP], K("iota"), slot_t[:, t, col], gate_t[:, t, col],
                                                    ALU.is_equal, ALU.mult)
                    ins.then_inc(m["picked"], 1)

                def hidden(n, h):
                    dve.wait_ge(m["sig_done"], 2 * n + h + 1)
                    half = slice(h * UC, (h + 1) * UC)
                    dve.tensor_tensor(hid[:, half], sg[:, half], bank[2 * h][:, :], ALU.mult).then_inc(m["loop_step"], 1)
                    dve.wait_ge(m["loop_step"], 2 * n + h + 1)
                    dve.wait_ge(moe_used[l], n * MOE_UNITS + (SLOTS + 4 * h + 4))
                    dve.tensor_tensor(hid[:, half], hid[:, half], bank[2 * h + 1][:, :], ALU.mult).then_inc(m["hid_done"], 1)

                def add_scattered(n):
                    for t in range(TT):
                        for h in range(2):
                            dve.wait_ge(m["scattered"], 4 * n + (2 * t + h + 1))
                            cols = slice(h * UC, (h + 1) * UC)
                            dve.tensor_tensor(y[:, t, cols], y[:, t, cols], bank[4 + 2 * t + h][:, :], ALU.add).then_inc(m["y_added"], 1)

                one_hots(0)
                with dve.Fori(0, r_end * PAIRS) as n:
                    hidden(n, 0)
                    add_scattered(n)
                    dve.wait_ge(m["gt_done"], n + 1)
                    one_hots(n + 1)
                    hidden(n, 1)
                    dve.wait_ge(moe_used[l], n * MOE_UNITS + (SLOTS + 10))
                    dve.tensor_copy(yd[:, 0:UC], bank[6][:, :]).then_inc(m["yd0_ready"], 1)
                add_scattered(r_end * PAIRS)

            for name, dst in ((("vecT",), vT), (("bT",), bT)):
                dve.wait_ge(filled, fill(name))
                dve.tensor_copy(dst[:, :], bank_of(name)[:, 0:dst.shape[1]]).then_inc(emptied["dve"], 1)
            dve.wait_ge(sig_ready, 1)
            dve.wait_ge(cleared, 2)
            dve.tensor_tensor(cond[:, :, 0:2].rearrange("p c t -> p t c"), vT[:, 0:16].rearrange("p (t c) -> p t c", t=2),
                              sig[:, :].rearrange("p (t c) -> p t c", t=2), ALU.mult).then_inc(cond_ready, 1)
            for u in range(12):
                mod(0, u)
            for l in range(LAYERS):
                norm(l, 0)
                projection(l)
                if l == 0:
                    dve.wait_ge(ld_small, 16 * 11)
                    then(dve.tensor_tensor(lamw[:, :, :], lamv[:, 0:4:2, :], lamv[:, 1:4:2, :], ALU.mult))
                    dve.tensor_reduce(lam[:, 0:2], lamw[:, :, :], AX.X, ALU.add).then_inc(lam_dot, 1)
                    then(dve.tensor_scalar(subg[:, :], subg[:, :], 1.0 - LAM_INIT, None, ALU.mult))
                for t in range(TT):
                    qk_norm(l, t)
                if l == 0:
                    for u in range(12):
                        mod(1, u)
                    dve.wait_ge(lam_exp, 1)
                    then(dve.tensor_tensor(lam[:, 0:1], lam[:, 3:4], lam[:, 2:3], ALU.subtract))
                    then(dve.tensor_scalar(lam[:, 0:1], lam[:, 0:1], -LAM_INIT, None, ALU.add))
                else:
                    for i in range(4):
                        name, part = ("rev", i), bias[:, 4 * i:4 * i + 4, :]
                        over_heads = lambda v: v.unsqueeze(1).to_broadcast([P, 4, P])
                        dve.wait_ge(filled, fill(name))
                        dve.tensor_tensor(part, bank_of(name)[:, :].rearrange("p (h k) -> p h k", h=4), over_heads(K("mask8")),
                                          ALU.mult).then_inc(emptied["dve"], 1)
                        dve.wait_ge(*emptied_by(name))
                        then(dve.tensor_tensor(part, part, over_heads(K("neg")), ALU.add))
                    dve.wait_ge(out_kv[1], 32)
                for t in range(TT):
                    maxima(l, t, 0)
                    maxima(l, t, 1)
                    for b in range(BATCHES):
                        shares(l, t, b)
                        outputs(l, t, b)
                        if b + 2 < BATCHES:
                            maxima(l, t, b + 2)
                    if l == 0:
                        sub_norm(t)
                add_gated(l, 0)
                norm(l, 1)
                router(l)
                experts(l)
                add_gated(l, 1)


_INS = ["x_prompt", "x_sample", "cache_a_k", "cache_a_v", "cache_b_k", "cache_b_v", "cache_c_k", "cache_c_v",
        "c", "c_ctx", "w_mod", "b_mod", "norm_mix", "norm_ffn", "w_in_ab", "w_out_ab", "a_q_norm", "a_k_norm",
        "b_q_norm", "b_k_norm", "lam_q1", "lam_k1", "lam_q2", "lam_k2", "b_subln", "w_in_c", "w_out_c",
        "c_q_norm", "c_k_norm", "c_rpb", "w_router", "b_router", "w_gate", "w_up", "w_down"]
_OUTS = [("y_prompt", (1, 128, 1024)), ("y_sample", (1, 128, 1024)),
         ("new_a_k", (1, 1, 128, 2, 64)), ("new_a_v", (1, 1, 128, 2, 64)),
         ("new_b_k", (1, 1, 128, 4, 2, 64)), ("new_b_v", (1, 1, 128, 4, 128)),
         ("new_c_k", (1, 1, 128, 16, 64)), ("new_c_v", (1, 1, 128, 16, 64))]


def kernel(**inputs):
    import concourse.bacc as bacc
    from concourse.bass_utils import run_bass_kernel_spmd

    nc = bacc.Bacc("TRN2", target_bir_lowering=False, num_devices=1)
    arrays, aps = {}, {}
    for name in _INS:
        arr = np.ascontiguousarray(inputs[name])
        arrays["in_" + name] = arr
        aps[name] = nc.dram_tensor("in_" + name, arr.shape, mybir.dt.from_np(arr.dtype), kind="ExternalInput").ap()
    arrays["in_tables"] = constants()
    aps["tables"] = nc.dram_tensor("in_tables", (P, NCONST), F32, kind="ExternalInput").ap()
    for name, shape in _OUTS:
        flat = nc.dram_tensor("out_" + name, (P, int(np.prod(shape)) // P), F32, kind="ExternalOutput").ap()
        aps[name] = flat
    build(nc, aps)
    r = run_bass_kernel_spmd(nc, [arrays], core_ids=[0])
    return tuple(r.results[0]["out_" + name].reshape(shape) for name, shape in _OUTS)
```

```python
import numpy as np
import concourse.bass as bass
from concourse import mybir
from contextlib import ExitStack

F32 = mybir.dt.float32
I32 = mybir.dt.int32
ALU = mybir.AluOpType
ACT = mybir.ActivationFunctionType
AX = mybir.AxisListType

D = 1024
P = 128
DC = D // P
TT = 2
LAYERS = 2
HD = 64
GRID_W = 64
EPS = 1e-6
SCALE = HD ** -0.5
A_Q, A_KV, B_QK, B_V = 512, 128, 512, 512
AB_IN = A_Q + 2 * A_KV + 2 * B_QK + B_V
C_W = 1024
NE, NG, EG = 16, 4, 4
NA_COLS = 16
LAM_INIT = 0.2
MASKED = -1.0e30

UC = 512
SLOTS = 6
CAP = 64
ROUNDS_MAX = TT * P // CAP
PAIRS = NE // 2
MOE_UNITS = 12

CONST = {}
_at = 0
for _name, _n in (("ident", P), ("upper", P), ("ones", P), ("iota", CAP), ("sel2", 32), ("selg", 8), ("rev", P), ("mhalf", HD),
                  ("mask8", P), ("neg", P), ("low4", 16), ("cos", HD), ("ssin", HD), ("thr", ROUNDS_MAX - 1)):
    CONST[_name] = (_at, _n)
    _at += _n
NCONST = _at


def constants():
    c = np.zeros((P, NCONST), np.float32)

    def block(name):
        at, n = CONST[name]
        return c[:, at:at + n]

    row, lane = np.arange(P)[:, None], np.arange(P)[None, :]
    block("ident")[:] = row == lane
    block("upper")[:] = row < lane
    block("ones")[:] = 1.0
    block("iota")[:] = np.arange(CAP)[None, :]
    for t in range(TT):
        block("sel2")[:, t] = (np.arange(P) % 32) == t
        for k in range(4):
            block("selg")[:, 2 * k + t] = (np.arange(P) == 32 * k + t) | (np.arange(P) == 32 * k + 2)
    block("mhalf")[:] = -0.5
    block("rev")[:] = row == lane - lane % GRID_W + GRID_W - 1 - lane % GRID_W
    col = np.arange(P) % GRID_W
    first = np.clip(col - NA_COLS // 2, 0, GRID_W - NA_COLS)
    inside = (col[None, :] >= first[:, None]) & (col[None, :] < first[:, None] + NA_COLS)
    block("mask8")[:] = inside / SCALE
    block("neg")[:] = np.where(inside, 0.0, MASKED)
    block("low4")[:] = (np.arange(4)[None, :] < np.arange(4)[:, None]).reshape(1, 16)
    freq = 10000.0 ** (-np.arange(16, dtype=np.float32) / np.float32(16))
    for half, pos in enumerate((np.arange(P) // GRID_W, np.arange(P) % GRID_W)):
        angle = pos.astype(np.float32)[:, None] * freq.astype(np.float32)[None, :]
        for part, sign in ((0, -1.0), (1, 1.0)):
            at = half * 32 + part * 16
            block("cos")[:, at:at + 16] = np.cos(angle)
            block("ssin")[:, at:at + 16] = sign * np.sin(angle)
    block("thr")[:] = CAP * np.arange(1, ROUNDS_MAX)[None, :]
    return c


NORMED = {0: [(0, 8, 0), (512, 2, 1), (768, 8, 2), (1280, 8, 3)], 1: [(0, 16, 4), (1024, 16, 5)]}
SPANS = {0: [(0, 640), (768, 1792)], 1: [(0, 2048)]}
ROPED = [(0, 10), (768, 16)]
QKV_COLS = {0: AB_IN, 1: 3 * C_W}
Q_CHUNKS = {0: [0, 768], 1: [0, 512]}
O_COLS = {0: [0, 768], 1: [0, 512]}
K_JOBS = {(0, 0): 2, (0, 1): 3, (1, 0): 2, (1, 1): 4}
BATCHES = 4


def fill_in(l, t, point):
    if l == 0:
        late = [(0, u) for u in range(4, 12)] + [(1, u) for u in range(12)]
        k = 2 * (5 * t + point)
        names = []
        for j in (k, k + 1):
            names.append(("mod",) + late[j])
            if j:
                names.append(mod_sum(*late[j - 1]))
        if (t, point) == (1, 4):
            names.append(mod_sum(*late[-1]))
            names += [("gb", 0, 0, u, tt) for tt in range(TT) for u in range(2)]
        return names
    return {(0, 0): [("qkv", 1, 4, 1)], (0, 1): [("qkv", 1, 5, 1)],
            (0, 2): [("gb", 1, 0, u, tt) for tt in range(TT) for u in range(2)], (0, 3): [("rev", i) for i in range(4)],
            (1, 0): [("wo", 1, 0, 0)], (1, 1): [("wo", 1, 1, 0)]}.get((t, point), [])


def mod_sum(l, u):
    return ("modG" if u // 2 in (2, 5) else "modT", l, u)


def dense_units(layer):
    if layer == 0:
        late = [n for t in range(TT) for point in range(5) for n in fill_in(0, t, point) if n[0] == "mod"]
        return ([("mod", 0, u) for u in range(4)] + [("in", 0, u) for u in range(5)] + late
                + [("out", 0, u) for u in range(2)])
    return [("in", 1, u) for u in range(6)] + [("out", 1, u) for u in range(2)]


EMPTIED_BY = {"vecT": "dve", "bT": "dve", "mod": "act", "modG": "dve", "modT": "dve", "T": "act", "PT": "act",
              "O": "dve", "oT": "act", "gb": "act", "wo": "dve", "hk": "act", "rt": "dve", "pos": "dve", "rev": "dve"}


def psum_jobs():
    names = [("vecT",), ("bT",)]
    for u in range(4):
        names += [("mod", 0, u), mod_sum(0, u)]
    for l in range(LAYERS):
        names += [("hT", l, 0, t, h) for t in range(TT) for h in range(2)]
        for u in range(-(-QKV_COLS[l] // UC)):
            names += [("qkv", l, u, t) for t in range(TT) if ("qkv", l, u, t) not in fill_in(l, 0, 0) + fill_in(l, 0, 1)]
        for t in range(TT):
            names += [("T", l, t, i) for i in range(2 + K_JOBS[l, t])]
            names += [("S", l, t, b, e) for b in range(2) for e in range(2)]
            names += fill_in(l, t, 0)
            for b in range(BATCHES):
                names += [("PT", l, t, b, k) for k in range(pt_jobs(l, t, b))] + [("O", l, t, b)]
                if b + 2 < BATCHES:
                    names += [("S", l, t, b + 2, e) for e in range(2)]
                names += fill_in(l, t, b + 1)
            if l == 0:
                names += [("oT", 0, t)]
        names += [("wo", l, u, t) for t in range(TT) for u in range(2) if (l, t) != (1, 0)]
        names += [("hT", l, 1, t, h) for t in range(TT) for h in range(2)]
        names += [("rt", l)] + [("hk", l, t, h) for t in range(TT) for h in range(2)]
        names += [("gb", l, 1, u, t) for t in range(TT) for u in range(2)] + [("pos", l), None]

    def engine(name):
        kind = name[0]
        if kind == "hT":
            return ("act", "dve")[name[4]]
        if kind == "qkv":
            return ("act", "dve")[name[3]]
        if kind == "S":
            return "dve" if name[1:3] == (1, 1) else "act"
        return EMPTIED_BY[kind]

    return [name and (name, engine(name)) for name in names]


def pt_jobs(l, t, b):
    return 2 if t == 1 and (l == 1 or b < 2) else 1


def build(nc, a):
    ctx = ExitStack()
    with ctx:
        def sb(name, shape, dt=F32):
            return ctx.enter_context(nc.sbuf_tensor(name, shape, dt))

        def sem(name):
            return ctx.enter_context(nc.semaphore(name))

        ring = [sb(f"ring{i}", [P, DC, UC]) for i in range(SLOTS)]
        x = sb("x", [P, TT, D])
        hT = sb("hT", [P, DC, TT * P])
        work = sb("work", [P, 15360])
        const = sb("const", [P, NCONST])
        gates = sb("gates", [P, D])
        gbuf = sb("gbuf", [P, 4, UC])
        tmp = sb("tmp", [P, 2, UC])
        m4 = sb("m4", [P, 2, UC])
        vecs = sb("vecs", [48, P])
        bvec = sb("bvec", [96, P])
        vT = sb("vT", [P, 48])
        bT = sb("bT", [P, 96])
        sig = sb("sig", [P, 16])
        cond = sb("cond", [P, DC, 32])
        modc = sb("modc", [P, LAYERS, 4, TT, DC])
        gain = sb("gain", [P, 6, HD])
        subg = sb("subg", [P, P])
        lamv = sb("lamv", [P, 4, HD])
        lamw = sb("lamw", [P, 2, HD])
        lam = sb("lam", [P, 4])
        wr = sb("wr", [P, DC, NE])
        br = sb("br", [P, NE])
        ss = sb("ss", [P, 4])
        hss = sb("hss", [P, 64])
        nm = sb("nm", [P, 2, 4])
        rs = sb("rs", [P, 2, 4])
        rinv = sb("rinv", [P, 2, 4])
        lg = sb("lg", [P, TT, NE])
        sco = sb("sco", [P, TT, NE])
        sel = sb("sel", [P, TT, NE])
        cmp = sb("cmp", [P, 128])
        cmq = sb("cmq", [P, 128])
        top = sb("top", [P, TT, NE])
        gsum = sb("gsum", [P, TT * NG])
        chosen = sb("chosen", [P, TT, NE])
        gate = sb("gate", [P, TT, NE])
        st2 = sb("st2", [P, 4])
        cnt = sb("cnt", [P, 4])
        cnt8 = sb("cnt8", [P, TT * NG])
        rounds = sb("rounds", [P, 1], I32)
        slot_of = sb("slot_of", [P, TT, NE])
        SLOT_COLS = ROUNDS_MAX * NE + 2
        slot_t = sb("slot_t", [P, TT, SLOT_COLS])
        gate_t = sb("gate_t", [P, TT, SLOT_COLS])

        bank = [ctx.enter_context(nc.psum_tensor(f"bank{i}", [P, 512], F32)) for i in range(8)]

        def K(name):
            at, n = CONST[name]
            return const[:, at:at + n]

        qkv = [work[:, 3072 * t:3072 * (t + 1)] for t in range(TT)]
        cache = work[:, 6144:8192]
        QT = work[:, 8192:9216].rearrange("p (c q) -> p c q", c=8)
        KT = work[:, 9216:11264].rearrange("p (c k) -> p c k", c=8)
        PR = work[:, 11264:13312].rearrange("p (b h k) -> p b h k", b=2, h=4)
        PTs = work[:, 13312:15360].rearrange("p (b h q) -> p b h q", b=2, h=8)
        xn = work[:, 11264:13312].rearrange("p (t d) -> p t d", t=2)
        scratch = [work[:, 11264:13312], work[:, 13312:15360]]
        bias = hT[:, :, :].rearrange("p c n -> p (c n)").rearrange("p (h k) -> p h k", h=16)
        sc = work[:, 1024:3072].rearrange("p (b h k) -> p b h k", b=2, h=4)
        def oT(l, t, c, n=1):
            at = 3072 * t + P * c + (2304 - 4 * P if l == 0 and c >= 4 else 0)
            return work[:, at:at + n * P]

        y = work[:, 0:2048].rearrange("p (t d) -> p t d", t=2)
        htok = work[:, 2048:4096].rearrange("p (t d) -> p t d", t=2)
        hgT = work[:, 4096:5120].rearrange("p (c s) -> p c s", c=8)
        yd = work[:, 5120:6144]
        sg = work[:, 8192:9216]
        hid = work[:, 9216:10240]
        hidT = work[:, 10240:11264].rearrange("p (c s) -> p c s", c=8)
        pick = work[:, 13312:13568].rearrange("p (t s) -> p t s", t=2)
        gpick = work[:, 13568:13824].rearrange("p (t s) -> p t s", t=2)
        GT = work[:, 13824:14080].rearrange("p (t q) -> p t q", t=2)

        filled = sem("bank_filled")
        emptied = {"act": sem("bank_emptied_act"), "dve": sem("bank_emptied_dve")}
        dense_ld = [sem(f"dense_loaded{i}") for i in range(SLOTS)]
        moe_used = [sem(f"moe_used{l}") for l in range(LAYERS)]
        moe_ld = [[sem(f"moe_loaded{l}_{i}") for i in range(SLOTS)] for l in range(LAYERS)]
        ld_const, ld_vec, ld_x, ld_gb, ld_small, ld_router = (
            sem(n) for n in ("ld_const", "ld_vec", "ld_x", "ld_gate_bias", "ld_small", "ld_router"))
        ld_cache = [sem(f"ld_cache{l}") for l in range(LAYERS)]
        ld_bias = sem("ld_bias")
        turns = sem("turns")
        out_kv = [sem(f"out_kv{l}") for l in range(LAYERS)]
        out_y = sem("out_y")
        cleared = sem("cleared")
        sig_ready, cond_ready, lam_dot, lam_exp, lam_ready = (
            sem(n) for n in ("sig_ready", "cond_ready", "lam_dot", "lam_exp", "lam_ready"))
        mod_ready = sem("mod_ready")
        power_asked, power_taken = sem("power_asked"), sem("power_taken")
        ssq_ready, xn_ready, x_ready = sem("ssq_ready"), sem("xn_ready"), sem("x_ready")
        squares, normed = sem("squares"), sem("qk_normed")
        max_ready, exps_ready, shared, o_ready = (
            sem(n) for n in ("max_ready", "exps_ready", "probs_shared", "o_ready"))
        ex_ready, mask_ready, rounds_ready = (sem(n) for n in ("router_exp", "mask_ready", "rounds_ready"))
        dve_step = sem("dve_step")
        M = [{n: sem(f"{n}{l}") for n in (
            "y_zeroed", "picked", "gathered", "hg_ready", "sig_done", "hid_done", "scattered", "y_added",
            "gt_done", "gt_ready", "ht_done", "ht_ready", "yd0_ready", "yd1_ready", "loop_step")} for l in range(LAYERS)]

        powers = {}
        for l in range(LAYERS):
            n = sum(hi - lo for lo, hi in SPANS[l]) // HD
            powers["norm", l, 0, 0], powers["norm", l, 0, 1] = ss[:, 0:1], ss[:, 1:2]
            powers["qk", l, 0], powers["qk", l, 1] = hss[:, 0:n], hss[:, 32:32 + n]
            if l == 0:
                powers["sub", 0, 0], powers["sub", 0, 1] = hss[:, 0:4], hss[:, 0:4]
            powers["norm", l, 1, 0], powers["norm", l, 1, 1] = ss[:, 0:1], ss[:, 1:2]

        jobs = [j for j in psum_jobs() if j]
        number = {name: k for k, (name, _) in enumerate(jobs)}
        engine_of = dict(jobs)
        done_at, seen = {}, {"act": 0, "dve": 0}
        for name, eng in jobs:
            seen[eng] += 1
            done_at[name] = seen[eng]
        after_loop, k = set(), 0
        for j in psum_jobs():
            if j is None:
                after_loop.update(range(k, k + 8))
            else:
                k += 1
        units = dense_units(0) + dense_units(1)
        N0 = len(dense_units(0))
        unit_no = {u: i for i, u in enumerate(units)}
        MOE_AT = [N0 % SLOTS, len(units) % SLOTS]

        def fill(name):
            return number[name] + 1

        def read_at(g):
            kind, l, u = units[g]
            return fill({"mod": ("mod", l, u), "in": ("qkv", l, u, 1), "out": ("wo", l, u, 1)}[kind])

        def emptied_by(name):
            return emptied[engine_of[name]], done_at[name]

        def exps_done(l, t, b):
            return (exps_ready, b + 1) if (l, t) == (1, 1) else emptied_by(("S", l, t, b, 1))

        def bank_of(name):
            return bank[number[name] % 8]

        w_in = [a["w_in_ab"][0], a["w_in_c"][0]]
        w_out = [a["w_out_ab"][0], a["w_out_c"][0]]

        def unit_cols(u):
            kind, l, i = u
            return min(UC, QKV_COLS[l] - i * UC) if kind == "in" else UC

        def unit_src(u):
            kind, l, i = u
            w = {"mod": a["w_mod"][l], "in": w_in[l], "out": w_out[l]}[kind]
            return w[:, i * UC:i * UC + unit_cols(u)].rearrange("(c p) n -> p c n", p=P)

        block = ctx.enter_context(nc.Block())

        @block.sync
        def _(sp):
            def dense(layer, rounds_of_0=None):
                for i, u in enumerate(dense_units(layer)):
                    g = N0 * layer + i
                    if layer == 1 and i < SLOTS:
                        sp.wait_ge(moe_used[0], rounds_of_0 * (PAIRS * MOE_UNITS) + (i + 1))
                    elif g >= SLOTS:
                        sp.wait_ge(filled, read_at(g - SLOTS))
                    sp.dma_start(ring[g % SLOTS][:, :, 0:unit_cols(u)], unit_src(u)).then_inc(dense_ld[g % SLOTS], 16)

            def experts(l):
                def load(k, at, wait):
                    w, half = [(a["w_gate"], 0), (a["w_up"], 0), (a["w_gate"], 1), (a["w_up"], 1),
                               (a["w_down"], 0), (a["w_down"], 1)][k // 2]
                    flat = w[l].rearrange("e k n -> (e k n)")[bass.ds(at, D * D)]
                    src = flat.rearrange("(c p n) -> p c n", p=P, n=D)[:, :, half * UC:(half + 1) * UC]
                    slot = (MOE_AT[l] + k) % SLOTS
                    if wait is not None:
                        sp.wait_ge(moe_used[l], wait)
                        sp.sem_inc(turns, 1)
                    sp.dma_start(ring[slot][:, :, :], src).then_inc(moe_ld[l][slot], 16)

                def units_of(n, i, which):
                    at = [sp.snap(i * (2 * D * D) + e * D * D) for e in range(2)]
                    for k in which:
                        load(k, at[k % 2], n * MOE_UNITS + (k + 1))

                first, later = range(SLOTS), range(SLOTS, MOE_UNITS)

                for k in range(SLOTS):
                    sp.wait_ge(filled, read_at((N0 if l == 0 else len(units)) - SLOTS + k))
                    load(k, (k % 2) * D * D, None)
                sp.wait_ge(rounds_ready, l + 1)
                r_end = sp.value_load(rounds[0:1, 0:1], min_val=1, max_val=ROUNDS_MAX)
                with sp.Fori(0, r_end) as r:
                    with sp.Fori(0, PAIRS - 1) as i:
                        units_of(r * PAIRS + i, i, later)
                        units_of(r * PAIRS + i + 1, i + 1, first)
                    units_of(r * PAIRS + (PAIRS - 1), PAIRS - 1, later)
                    with sp.If(r + 1 < r_end):
                        units_of((r + 1) * PAIRS, 0, first)
                    sp.nop()
                return r_end

            sp.dma_start(const[:, :], a["tables"]).then_inc(ld_const, 16)
            for row, src in ((0, a["c_ctx"]), (8, a["c"]), (16, a["norm_mix"]), (32, a["norm_ffn"])):
                n = 16 if row >= 16 else 8
                flat = src if len(src.shape) == 1 else src.rearrange("a b -> (a b)")
                sp.dma_start(vecs[row:row + n, :], flat.rearrange("(r p) -> r p", p=P)).then_inc(ld_vec, 16)
            sp.dma_start(bvec[:, :], a["b_mod"].rearrange("l (r p) -> (l r) p", p=P)).then_inc(ld_vec, 16)
            for t, name in enumerate(("x_prompt", "x_sample")):
                sp.dma_start(x[:, t, :], a[name][0]).then_inc(ld_x, 16)
            dense(0)
            r0 = experts(0)
            dense(1, r0)
            experts(1)

        @block.gpsimd
        def _(pool):
            pool.memset(cond[:, :, :], 0.0).then_inc(cleared, 1)
            pool.memset(gates[:, :], 0.0).then_inc(cleared, 1)
            pool.wait_ge(cleared, 2)
            for l in range(LAYERS):
                for kind in range(2):
                    k = 2 * l + kind
                    at = (2 + 3 * kind) * D
                    pool.dma_start(gates[32 * k + 2:32 * k + 3, :], a["b_mod"][l:l + 1, at:at + D]).then_inc(ld_gb, 16)
            for i, name in enumerate(("a_q_norm", "a_k_norm", "b_q_norm", "b_k_norm", "c_q_norm", "c_k_norm")):
                pool.dma_start(gain[:, i, :], a[name][0].partition_broadcast(P)).then_inc(ld_small, 16)
            pool.dma_start(subg[:, :], a["b_subln"][0].partition_broadcast(P)).then_inc(ld_small, 16)
            for i, name in enumerate(("lam_q1", "lam_k1", "lam_q2", "lam_k2")):
                pool.dma_start(lamv[:, i, :], a[name][0].partition_broadcast(P)).then_inc(ld_small, 16)
            at = 0
            for name in ("cache_a_k", "cache_a_v", "cache_b_k", "cache_b_v"):
                src = a[name][0, 0]
                src = src.rearrange("k h s d -> k (h s d)") if len(src.shape) == 4 else src.rearrange("k h d -> k (h d)")
                pool.dma_start(cache[:, at:at + src.shape[1]], src).then_inc(ld_cache[0], 16)
                at += src.shape[1]
            pool.dma_start(wr[:, :, :], a["w_router"].rearrange("(c p) e -> p c e", p=P)).then_inc(ld_router, 16)
            pool.dma_start(br[:, :], a["b_router"].partition_broadcast(P)).then_inc(ld_router, 16)

            def power(*which):
                v = powers[which]
                pool.wait_ge(power_asked, list(powers).index(which) + 1)
                pool.tensor_tensor(v, v, K("mhalf")[:, 0:v.shape[1]], ALU.pow).then_inc(power_taken, 1)

            pool.wait_ge(ld_const, 16)
            for l in range(LAYERS):
                power("norm", l, 0, 0)
                power("norm", l, 0, 1)
                last = -(-QKV_COLS[l] // UC) - 1
                power("qk", l, 0)
                power("qk", l, 1)
                pool.wait_ge(normed, 2 * l + 1)
                pool.wait_ge(*emptied_by(("qkv", l, last, 0)))
                if l == 0:
                    outs = [("new_a_k", 512, 128), ("new_a_v", 640, 128), ("new_b_k", 1280, 512), ("new_b_v", 1792, 512)]
                else:
                    outs = [("new_c_k", 1024, 1024), ("new_c_v", 2048, 1024)]
                for name, at, n in outs:
                    pool.dma_start(a[name], qkv[0][:, at:at + n]).then_inc(out_kv[l], 16)
                if l == 1:
                    pool.wait_ge(filled, fill(("qkv", 1, last, 1)))
                    rpb = a["c_rpb"]
                    for r in range(2):
                        for r2 in range(2):
                            src = bass.AP(rpb.tensor, rpb.offset + (r2 - r + 7) * 31 + 15 - 63, [[1, 64], [15 * 31, 16], [1, 64]])
                            pool.dma_start(bias[64 * r:64 * r + 64, :, 64 * r2:64 * r2 + 64], src).then_inc(ld_bias, 16)
                if l == 0:
                    power("sub", 0, 0)
                    power("sub", 0, 1)
                    pool.wait_ge(filled, fill(("O", 0, 1, BATCHES - 1)))
                    pool.dma_start(cache[:, 0:1024], a["cache_c_k"][0, 0].rearrange("k h d -> k (h d)")).then_inc(ld_cache[1], 16)
                    pool.dma_start(cache[:, 1024:2048], a["cache_c_v"][0, 0].rearrange("k h d -> k (h d)")).then_inc(ld_cache[1], 16)
                power("norm", l, 1, 0)
                power("norm", l, 1, 1)
            pool.wait_ge(x_ready, 4 * 4)
            pool.dma_start(a["y_prompt"], x[:, 0, :]).then_inc(out_y, 16)
            pool.dma_start(a["y_sample"], x[:, 1, :]).then_inc(out_y, 16)
            pool.wait_ge(out_kv[0], 64)
            pool.wait_ge(out_kv[1], 32)
            pool.wait_ge(out_y, 32)

        @block.tensor
        def _(pe):
            def bank_free(name):
                k = number[name]
                if k >= 8 and k not in after_loop:
                    pe.wait_ge(*emptied_by(jobs[k - 8][0]))
                return bank_of(name)

            def arrived(u):
                g = unit_no[u]
                pe.wait_ge(dense_ld[g % SLOTS], 16 * len([h for h in range(g + 1) if h % SLOTS == g % SLOTS]))
                return ring[g % SLOTS]

            def transposes(name, parts):
                b = bank_free(name)
                for i, src in enumerate(parts):
                    ins = pe.transpose(b[:, i * P:(i + 1) * P], src, K("ident"))
                ins.then_inc(filled, 1)

            def mod(l, u):
                w = arrived(("mod", l, u))
                b = bank_free(("mod", l, u))
                for c in range(DC):
                    j = 32 * (c % 4)
                    ins = pe.matmul(b[j:j + 32, :], cond[:, c, :], w[:, c, :], start=c < 4, stop=c >= 4,
                                    tile_position=(0, j))
                ins.then_inc(filled, 1)

            def add_groups(l, u):
                v, name = u // 2, mod_sum(l, u)
                b = bank_free(name)
                pe.wait_ge(*emptied_by(("mod", l, u)))
                if v in (2, 5):
                    k = 2 * l + v // 5
                    ins = pe.matmul(b[32 * k:32 * k + 32, :], K("sel2"), m4[:, u % 2, :], start=True, stop=True,
                                    tile_position=(0, 32 * k))
                else:
                    for c in range(4):
                        ins = pe.matmul(b[:, 2 * c:2 * c + 2], m4[:, u % 2, c * P:(c + 1) * P], K("sel2")[:, 0:2],
                                        start=True, stop=True)
                ins.then_inc(filled, 1)

            def norm(l, kind):
                for t in range(TT):
                    pe.wait_ge(xn_ready, 4 * l + 2 * kind + t + 1)
                    for h in range(2):
                        transposes(("hT", l, kind, t, h), [xn[:, t, (4 * h + i) * P:(4 * h + i + 1) * P] for i in range(4)])

            def project(l, u, t):
                w = arrived(("in", l, u))
                n = unit_cols(("in", l, u))
                b = bank_free(("qkv", l, u, t))
                for h in range(2):
                    pe.wait_ge(*emptied_by(("hT", l, 0, t, h)))
                for c in range(DC):
                    ins = pe.matmul(b[:, 0:n], hT[:, c, t * P:(t + 1) * P], w[:, c, 0:n], start=c == 0, stop=c == DC - 1)
                ins.then_inc(filled, 1)

            def reverse_bias(i):
                pe.wait_ge(ld_bias, 64)
                pe.matmul(bank_free(("rev", i))[:, :], K("rev"), bias[:, 4 * i:4 * i + 4, :], start=True, stop=True).then_inc(filled, 1)

            def gate_rows(l, kind, u, t):
                name, k = ("gb", l, kind, u, t), 2 * l + kind
                b = bank_free(name)
                pe.wait_ge(ld_gb, 64)
                pe.wait_ge(*emptied_by(("modG", 1, 11)))
                pe.matmul(b[:, :], K("selg")[:, 2 * k + t:2 * k + t + 1].to_broadcast([P, P]),
                          gates[:, u * UC:(u + 1) * UC], start=True, stop=True).then_inc(filled, 1)

            def out_project(l, u, t):
                w = arrived(("out", l, u))
                b = bank_free(("wo", l, u, t))
                pe.wait_ge(*emptied_by(("O", l, t, BATCHES - 1)))
                if l == 0:
                    pe.wait_ge(*emptied_by(("oT", 0, t)))
                for c in range(DC):
                    ins = pe.matmul(b[:, :], oT(l, t, c), w[:, c, :], start=c == 0, stop=c == DC - 1)
                ins.then_inc(filled, 1)

            job = {"mod": mod, "modT": add_groups, "modG": add_groups, "qkv": project, "rev": reverse_bias,
                   "gb": gate_rows, "wo": out_project}

            def attention(l, t):
                pe.wait_ge(normed, 2 * l + t + 1)
                if t == 1:
                    pe.wait_ge(ld_cache[l], 16 * (4 if l == 0 else 2))
                X = qkv[t]
                chunk = lambda base, at: base[:, at:at + P]
                parts = [[chunk(X, at + i * P) for i in range(4)] for at in Q_CHUNKS[l]]
                if l == 0:
                    parts += [([chunk(cache, 0)] if t else []) + [chunk(X, 512)], [chunk(X, 1280 + i * P) for i in range(4)]]
                    if t:
                        parts += [[chunk(cache, 256 + i * P) for i in range(4)]]
                else:
                    parts += [[chunk(X, 1024 + (4 * h + i) * P) for i in range(4)] for h in range(2)]
                    if t:
                        parts += [[chunk(cache, (4 * h + i) * P) for i in range(4)] for h in range(2)]
                for i, p in enumerate(parts):
                    transposes(("T", l, t, i), p)
                for i in range(len(parts)):
                    pe.wait_ge(*emptied_by(("T", l, t, i)))
                nk = P * (1 + t)

                def scores(b):
                    banks = [bank_free(("S", l, t, b, e)) for e in range(2)]
                    for i in range(2):
                        for e in range(2):
                            h = 4 * b + 2 * i + e
                            kc = h // 2 if l == 1 else (h // 4 if h < 8 else 2 + (h - 8) // 2)
                            rows = slice(64 * e, 64 * e + 64)
                            ins = pe.matmul(banks[e][:, i * nk:(i + 1) * nk], QT[rows, h // 2, :], KT[rows, kc, 0:nk],
                                            start=True, stop=True, tile_position=(64 * e, 0))
                            if i == 1:
                                ins.then_inc(filled, 1)

                def values(b):
                    diff = l == 0 and b >= 2
                    pe.wait_ge(shared, (l * TT + t) * BATCHES + b + 1)
                    heads = range(2) if diff else range(4)
                    pr, pt = PR[:, b % 2], PTs[:, b % 2]
                    chunks = [(kc, h) for kc in range(1 + t) for h in heads]
                    n_jobs = pt_jobs(l, t, b)
                    per = len(chunks) // n_jobs
                    for k in range(n_jobs):
                        transposes(("PT", l, t, b, k), [pr[:, h, kc * P:(kc + 1) * P] for kc, h in chunks[k * per:(k + 1) * per]])
                    ob = bank_free(("O", l, t, b))
                    for k in range(n_jobs):
                        pe.wait_ge(*emptied_by(("PT", l, t, b, k)))
                    if b == 0:
                        pe.wait_ge(*emptied_by(("qkv", l, -(-QKV_COLS[l] // UC) - 1, t)))

                    def keys(kc, own, kept, width):
                        return cache[:, kept:kept + width] if kc < t else X[:, own:own + width]

                    if diff:
                        for h in heads:
                            at = P * (2 * (b - 2) + h)
                            for kc in range(1 + t):
                                ins = pe.matmul(ob[:, h * P:(h + 1) * P], pt[:, 2 * kc + h, :], keys(kc, 1792 + at, 768 + at, P),
                                                start=kc == 0, stop=kc == t)
                    elif l == 0:
                        for kc in range(1 + t):
                            for e in range(2):
                                ins = pe.matmul(ob[64 * e:64 * e + 64, 0:2 * P], keys(kc, 640 + HD * b, 128 + HD * b, HD),
                                                pt[:, 4 * kc + 2 * e:4 * kc + 2 * e + 2, :], start=kc == 0, stop=kc == t,
                                                tile_position=(0, 64 * e))
                    else:
                        for i in range(2):
                            for kc in range(1 + t):
                                for e in range(2):
                                    at = HD * (4 * b + 2 * i + e)
                                    ins = pe.matmul(ob[64 * e:64 * e + 64, i * P:(i + 1) * P], keys(kc, 2 * C_W + at, C_W + at, HD),
                                                    pt[:, 4 * kc + 2 * e + i, :], start=kc == 0, stop=kc == t,
                                                    tile_position=(0, 64 * e))
                    ins.then_inc(filled, 1)

                def meanwhile(point):
                    for name in fill_in(l, t, point):
                        job[name[0]](*name[1:])

                scores(0)
                scores(1)
                meanwhile(0)
                for b in range(BATCHES):
                    values(b)
                    if b + 2 < BATCHES:
                        scores(b + 2)
                    meanwhile(b + 1)
                if l == 0:
                    pe.wait_ge(o_ready, t + 1)
                    transposes(("oT", 0, t), [X[:, 768 + i * P:768 + (i + 1) * P] for i in range(4)])

            def router(l):
                for t in range(TT):
                    for h in range(2):
                        pe.wait_ge(*emptied_by(("hT", l, 1, t, h)))
                pe.wait_ge(ld_router, 32)
                b = bank_free(("rt", l))
                for t in range(TT):
                    for c in range(DC):
                        ins = pe.matmul(b[:, t * NE:(t + 1) * NE], hT[:, c, t * P:(t + 1) * P], wr[:, c, :], start=c == 0, stop=c == DC - 1)
                ins.then_inc(filled, 1)
                for t in range(TT):
                    for h in range(2):
                        transposes(("hk", l, t, h), [hT[:, 4 * h + i, t * P:(t + 1) * P] for i in range(4)])
                for t in range(TT):
                    for u in range(2):
                        gate_rows(l, 1, u, t)
                pe.wait_ge(mask_ready, l + 1)
                b = bank_free(("pos", l))
                pe.matmul(b[:, 0:16], K("upper"), chosen[:, 0, :], start=True, stop=True)
                pe.matmul(b[:, 16:32], K("upper"), chosen[:, 1, :], start=True, stop=False)
                pe.matmul(b[:, 16:32], K("ones"), chosen[:, 0, :], start=False, stop=True)
                pe.matmul(b[:, 32:48], K("ones"), chosen[:, 0, :], start=True, stop=False)
                pe.matmul(b[:, 32:48], K("ones"), chosen[:, 1, :], start=False, stop=True).then_inc(filled, 1)

            def experts(l):
                m = M[l]

                def gather(n):
                    pe.wait_ge(m["picked"], n + 1)
                    for h in range(2):
                        for c in range(4):
                            for t in range(TT):
                                at = (4 * h + c) * P
                                ins = pe.matmul(bank[h][:, c * P:(c + 1) * P], htok[:, t, at:at + P], pick[:, t, :],
                                                start=t == 0, stop=t == 1)
                        ins.then_inc(m["gathered"], 1)

                def scatter(n):
                    pe.wait_ge(m["yd0_ready"], n + 1)
                    pe.wait_ge(m["yd1_ready"], n + 1)
                    for t in range(TT):
                        for h in range(2):
                            pe.matmul(bank[4 + 2 * t + h][:, :], GT[:, t, :], yd[:, h * UC:(h + 1) * UC],
                                      start=True, stop=True).then_inc(m["scattered"], 1)

                def product(n, k, b, lhs):
                    slots = [(MOE_AT[l] + k + e) % SLOTS for e in range(2)]
                    for e in range(2):
                        pe.wait_ge(moe_ld[l][slots[e]], 32 * n + 16 * (1 + k // SLOTS))
                    for c in range(DC):
                        for e in range(2):
                            ins = pe.matmul(bank[b][64 * e:64 * e + 64, :], lhs[:, c, 64 * e:64 * e + 64], ring[slots[e]][:, c, :],
                                            start=c == 0, stop=c == DC - 1, tile_position=(0, 64 * e))
                            if c == DC - 1:
                                ins.then_inc(moe_used[l], 1)

                last = number[("pos", l)]
                for k in range(last - 7, last + 1):
                    pe.wait_ge(*emptied_by(jobs[k][0]))
                pe.wait_ge(rounds_ready, l + 1)
                r_end = pe.value_load(rounds[0:1, 0:1], min_val=1, max_val=ROUNDS_MAX)
                pe.wait_ge(m["y_zeroed"], 1)
                for t in range(TT):
                    for h in range(2):
                        pe.wait_ge(*emptied_by(("hk", l, t, h)))
                pe.sem_inc(moe_used[l], SLOTS)
                gather(0)
                with pe.Fori(0, r_end * PAIRS) as n:
                    pe.wait_ge(m["hg_ready"], 2 * n + 2)
                    product(n, 0, 0, hgT)
                    product(n, 2, 1, hgT)
                    scatter(n)
                    for t in range(TT):
                        ins = pe.transpose(bank[3][:, t * P:(t + 1) * P], gpick[:, t, :], K("ident"))
                    ins.then_inc(m["gt_done"], 1)
                    product(n, 4, 2, hgT)
                    pe.wait_ge(m["gt_ready"], n + 1)
                    product(n, 6, 3, hgT)
                    pe.wait_ge(m["hid_done"], 2 * n + 1)
                    pe.wait_ge(m["y_added"], 4 * n + 4)
                    for c in range(4):
                        ins = pe.transpose(bank[4][:, c * P:(c + 1) * P], hid[:, c * P:(c + 1) * P], K("ident"))
                    ins.then_inc(m["ht_done"], 1)
                    gather(n + 1)
                    pe.wait_ge(m["hid_done"], 2 * n + 2)
                    for c in range(4):
                        ins = pe.transpose(bank[5][:, c * P:(c + 1) * P], hid[:, (4 + c) * P:(5 + c) * P], K("ident"))
                    ins.then_inc(m["ht_done"], 1)
                    pe.wait_ge(m["ht_ready"], 2 * n + 2)
                    product(n, 8, 6, hidT)
                    product(n, 10, 7, hidT)
                scatter(r_end * PAIRS)
                pe.wait_ge(m["y_added"], r_end * (4 * PAIRS) + 4)
                pe.wait_ge(m["hg_ready"], r_end * (2 * PAIRS) + 2)

            pe.wait_ge(ld_const, 16)
            pe.wait_ge(ld_vec, 80)
            pe.transpose(bank_free(("vecT",))[:, 0:48], vecs[:, :], K("ident")[0:48, 0:48]).then_inc(filled, 1)
            pe.transpose(bank_free(("bT",))[:, 0:96], bvec[:, :], K("ident")[0:96, 0:96]).then_inc(filled, 1)
            pe.wait_ge(cond_ready, 1)
            for u in range(4):
                mod(0, u)
                add_groups(0, u)
            for l in range(LAYERS):
                norm(l, 0)
                for u in range(-(-QKV_COLS[l] // UC)):
                    for t in range(TT):
                        if (l, t) != (1, 1) or u < 4:
                            project(l, u, t)
                for t in range(TT):
                    attention(l, t)
                for t in range(l, TT):
                    for u in range(2):
                        out_project(l, u, t)
                norm(l, 1)
                router(l)
                experts(l)

        @block.scalar
        def _(act):
            def mod(l, u):
                act.wait_ge(filled, fill(("mod", l, u)))
                if 12 * l + u >= 2:
                    pl, pu = divmod(12 * l + u - 2, 12)
                    act.wait_ge(filled, fill(("modG" if pu // 2 in (2, 5) else "modT", pl, pu)))
                act.activation(m4[:, u % 2, :], bank_of(("mod", l, u))[:, :], ACT.Copy).then_inc(emptied["act"], 1)

            def norm(l, kind):
                for t in range(TT):
                    act.wait_ge(*((ld_x, 32) if (l, kind) == (0, 0) else (x_ready, 4 * (2 * l + kind) - 2 + 2 * t)))
                    act.activation(xn[:, t, :], x[:, t, :], ACT.Square, accum_out=ss[:, t:t + 1]).then_inc(ssq_ready, 1)

            def modulate(l, kind):
                act.wait_ge(mod_ready, 4 * l + 2 * kind + 2)
                for t in range(TT):
                    name = ("hT", l, kind, t, 0)
                    act.wait_ge(filled, fill(name))
                    for c in range(4):
                        ins = act.activation(hT[:, c, t * P:(t + 1) * P], bank_of(name)[:, c * P:(c + 1) * P], ACT.Identity,
                                             bias=modc[:, l, 2 * kind, t, c:c + 1], scale=modc[:, l, 2 * kind + 1, t, c:c + 1])
                    ins.then_inc(emptied["act"], 1)

            def project(l, u, t):
                name, n = ("qkv", l, u, t), unit_cols(("in", l, u))
                act.wait_ge(filled, fill(name))
                act.activation(qkv[0][:, u * UC:u * UC + n], bank_of(name)[:, 0:n], ACT.Copy).then_inc(emptied["act"], 1)

            def projection(l):
                for u in range(4):
                    project(l, u, 0)
                for t in range(TT):
                    act.wait_ge(*emptied_by(("qkv", l, 3, t)))
                    for lo, hi in SPANS[l]:
                        ins = act.activation(scratch[t][:, lo:hi], qkv[t][:, lo:hi], ACT.Square)
                    ins.then_inc(squares, 1)
                for u in range(4, -(-QKV_COLS[l] // UC)):
                    project(l, u, 0)

            def transposed(l, t):
                own = P * t
                for i in range(2 + K_JOBS[l, t]):
                    name = ("T", l, t, i)
                    act.wait_ge(filled, fill(name))
                    src = bank_of(name)[:, :].rearrange("p (c q) -> p c q", c=4)
                    if i < 2:
                        dst = QT[:, 4 * i:4 * i + 4, :]
                    elif l == 1:
                        at = 0 if i >= 4 else own
                        dst = KT[:, 4 * (i % 2):4 * (i % 2) + 4, at:at + P]
                    elif i == 2:
                        for kv in range(2):
                            for half in range(2):
                                ins = act.activation(KT[64 * half:64 * half + 64, kv, 0:own + P],
                                                     bank_of(name)[64 * kv:64 * kv + 64, 0:own + P], ACT.Copy)
                        ins.then_inc(emptied["act"], 1)
                        continue
                    else:
                        at = 0 if i == 4 else own
                        dst = KT[:, 2:6, at:at + P]
                    act.activation(dst, src, ACT.Copy).then_inc(emptied["act"], 1)

            def exps(l, t, b):
                nk = P * (1 + t)
                banked = (l, t) != (1, 1)
                act.wait_ge(max_ready, (l * TT + t) * BATCHES + b + 1)
                if b >= 2:
                    act.wait_ge(filled, fill(("PT", l, t, b - 2, pt_jobs(l, t, b - 2) - 1)))
                for e in range(2):
                    for i in range(2):
                        j = 2 * e + i
                        src = bank_of(("S", l, t, b, e))[:, i * nk:(i + 1) * nk] if banked else sc[:, b % 2, j, :]
                        ins = act.activation(PR[:, b % 2, j, 0:nk], src, ACT.Exp, bias=nm[:, b % 2, j:j + 1],
                                             scale=SCALE, accum_out=rs[:, b % 2, j:j + 1])
                    if banked:
                        ins.then_inc(emptied["act"], 1)
                if not banked:
                    ins.then_inc(exps_ready, 1)

            def probs_transposed(l, t, b):
                heads = 2 if l == 0 and b >= 2 else 4
                per = heads * (1 + t) // pt_jobs(l, t, b)
                for k in range(pt_jobs(l, t, b)):
                    name = ("PT", l, t, b, k)
                    act.wait_ge(filled, fill(name))
                    act.activation(PTs[:, b % 2, k * per:(k + 1) * per, :],
                                   bank_of(name)[:, 0:per * P].rearrange("p (c q) -> p c q", c=per),
                                   ACT.Copy).then_inc(emptied["act"], 1)

            def spread_gate(l, kind, u, t):
                name = ("gb", l, kind, u, t)
                act.wait_ge(filled, fill(name))
                if 2 * l + kind:
                    act.wait_ge(x_ready, 4 * (2 * l + kind))
                act.activation(gbuf[:, 2 * t + u, :], bank_of(name)[:, :], ACT.Copy).then_inc(emptied["act"], 1)

            def meanwhile(l, t, point):
                for name in fill_in(l, t, point):
                    if engine_of[name] == "act":
                        {"mod": mod, "gb": spread_gate}[name[0]](*name[1:])

            def experts(l):
                m = M[l]
                act.wait_ge(rounds_ready, l + 1)
                r_end = act.value_load(rounds[0:1, 0:1], min_val=1, max_val=ROUNDS_MAX)
                act.activation(yd[:, UC:2 * UC], const[:, 0:UC], ACT.Copy, scale=0.0).then_inc(m["yd1_ready"], 1)

                def gathered(n):
                    for h in range(2):
                        act.wait_ge(m["gathered"], 2 * n + h + 1)
                        act.activation(hgT[:, 4 * h:4 * h + 4, :], bank[h][:, :].rearrange("p (c s) -> p c s", c=4),
                                       ACT.Copy).then_inc(m["hg_ready"], 1)

                def hidden_transposed(n, h):
                    act.wait_ge(m["ht_done"], 2 * n + h + 1)
                    act.activation(hidT[:, 4 * h:4 * h + 4, :], bank[4 + h][:, :].rearrange("p (c s) -> p c s", c=4),
                                   ACT.Copy).then_inc(m["ht_ready"], 1)

                def sigmoid(n, h):
                    act.wait_ge(moe_used[l], n * MOE_UNITS + (SLOTS + 4 * h + 2))
                    act.activation(sg[:, h * UC:(h + 1) * UC], bank[2 * h][:, :], ACT.Sigmoid).then_inc(m["sig_done"], 1)

                gathered(0)
                with act.Fori(0, r_end * PAIRS) as n:
                    sigmoid(n, 0)
                    act.wait_ge(m["gt_done"], n + 1)
                    act.activation(GT[:, :, :], bank[3][:, 0:2 * P].rearrange("p (t q) -> p t q", t=2),
                                   ACT.Copy).then_inc(m["gt_ready"], 1)
                    sigmoid(n, 1)
                    hidden_transposed(n, 0)
                    gathered(n + 1)
                    hidden_transposed(n, 1)
                    act.wait_ge(moe_used[l], n * MOE_UNITS + (SLOTS + 12))
                    act.activation(yd[:, UC:2 * UC], bank[7][:, :], ACT.Copy).then_inc(m["yd1_ready"], 1)

            act.wait_ge(*emptied_by(("vecT",)))
            act.activation(sig[:, :], vT[:, 0:16], ACT.Sigmoid).then_inc(sig_ready, 1)
            norm(0, 0)
            for u in range(4):
                mod(0, u)
            for l in range(LAYERS):
                if l:
                    norm(l, 0)
                modulate(l, 0)
                projection(l)
                if l == 0:
                    act.wait_ge(lam_dot, 1)
                    act.activation(lam[:, 2:4], lam[:, 0:2], ACT.Exp).then_inc(lam_exp, 1)
                for t in range(TT):
                    transposed(l, t)
                    exps(l, t, 0)
                    exps(l, t, 1)
                    meanwhile(l, t, 0)
                    for b in range(BATCHES):
                        probs_transposed(l, t, b)
                        if b + 2 < BATCHES:
                            exps(l, t, b + 2)
                        meanwhile(l, t, b + 1)
                    if l == 0:
                        act.wait_ge(filled, fill(("oT", 0, t)))
                        act.activation(oT(0, t, 4, 4), bank_of(("oT", 0, t))[:, :], ACT.Copy).then_inc(emptied["act"], 1)
                norm(l, 1)
                modulate(l, 1)
                act.wait_ge(out_kv[l], 64 if l == 0 else 32)
                act.wait_ge(*emptied_by(("rt", l)))
                act.activation(sco[:, :, :], lg[:, :, :], ACT.Exp).then_inc(ex_ready, 1)
                for t in range(TT):
                    for h in range(2):
                        name = ("hk", l, t, h)
                        act.wait_ge(filled, fill(name))
                        act.activation(htok[:, t, h * UC:(h + 1) * UC], bank_of(name)[:, :], ACT.Copy).then_inc(emptied["act"], 1)
                for t in range(TT):
                    for u in range(2):
                        spread_gate(l, 1, u, t)
                experts(l)

        @block.vector
        def _(dve):
            steps = [0]

            def then(ins):
                steps[0] += 1
                ins.then_inc(dve_step, 1)
                dve.wait_ge(dve_step, steps[0])

            def rms_inverse(which, n):
                v = powers[which]
                dve.tensor_scalar(v, v, 1.0 / n, EPS, ALU.mult, ALU.add).then_inc(power_asked, 1)
                dve.wait_ge(power_taken, list(powers).index(which) + 1)

            def mod(l, u):
                v = u // 2
                if v in (2, 5):
                    name, k = ("modG", l, u), 2 * l + v // 5
                    dve.wait_ge(filled, fill(name))
                    at = (u % 2) * UC
                    dve.tensor_copy(gates[32 * k:32 * k + 2, at:at + UC], bank_of(name)[32 * k:32 * k + 2, :]).then_inc(emptied["dve"], 1)
                    return
                name, v4, c0 = ("modT", l, u), v - v // 3, 4 * (u % 2)
                dve.wait_ge(filled, fill(name))
                dst = modc[:, l, v4, :, c0:c0 + 4]
                bias_cols = bT[:, 48 * l + 8 * v + c0:48 * l + 8 * v + c0 + 4]
                dve.tensor_tensor(dst, bank_of(name)[:, 0:8].rearrange("p (c t) -> p t c", t=2),
                                  bias_cols.unsqueeze(1).to_broadcast([P, TT, 4]), ALU.add).then_inc(emptied["dve"], 1)
                if v4 % 2:
                    g0 = 16 + 16 * (v4 // 2) + 8 * l + c0
                    dve.wait_ge(*emptied_by(name))
                    dve.scalar_tensor_tensor(out=dst, in0=dst, scalar=1.0, in1=vT[:, g0:g0 + 4].unsqueeze(1).to_broadcast([P, TT, 4]),
                                             op0=ALU.add, op1=ALU.mult).then_inc(mod_ready, 1)

            def norm(l, kind, t):
                dve.wait_ge(ssq_ready, 2 * (2 * l + kind) + t + 1)
                rms_inverse(("norm", l, kind, t), D)
                dve.tensor_scalar(xn[:, t, :], x[:, t, :], ss[:, t:t + 1], None, ALU.mult).then_inc(xn_ready, 1)

            def modulate(l, kind):
                dve.wait_ge(mod_ready, 4 * l + 2 * kind + 2)
                for t in range(TT):
                    name = ("hT", l, kind, t, 1)
                    dve.wait_ge(filled, fill(name))
                    for c in range(4):
                        ins = dve.tensor_scalar(hT[:, 4 + c, t * P:(t + 1) * P], bank_of(name)[:, c * P:(c + 1) * P],
                                                modc[:, l, 2 * kind + 1, t, 4 + c:5 + c], modc[:, l, 2 * kind, t, 4 + c:5 + c],
                                                ALU.mult, ALU.add)
                    ins.then_inc(emptied["dve"], 1)

            def project(l, u, t):
                name, n = ("qkv", l, u, t), unit_cols(("in", l, u))
                dve.wait_ge(filled, fill(name))
                dve.tensor_copy(qkv[1][:, u * UC:u * UC + n], bank_of(name)[:, 0:n]).then_inc(emptied["dve"], 1)

            def heads_of(t, lo, n):
                return qkv[t][:, lo:lo + n * HD].rearrange("p (h d) -> p h d", d=HD)

            def qk_norm(l, t):
                dve.wait_ge(squares, 2 * l + t + 1)
                at, parts = 32 * t, []
                for lo, hi in SPANS[l]:
                    n = (hi - lo) // HD
                    parts.append((lo, n, at))
                    ins = dve.tensor_reduce(hss[:, at:at + n], scratch[t][:, lo:hi].rearrange("p (h d) -> p h d", d=HD), AX.X, ALU.add)
                    at += n
                then(ins)
                rms_inverse(("qk", l, t), HD)
                for lo, n, c in parts:
                    v = heads_of(t, lo, n)
                    ins = dve.tensor_tensor(v, v, hss[:, c:c + n].unsqueeze(2).to_broadcast([P, n, HD]), ALU.mult)
                then(ins)
                for lo, n, g in NORMED[l]:
                    v = heads_of(t, lo, n)
                    ins = dve.tensor_tensor(v, v, gain[:, g, :].unsqueeze(1).to_broadcast([P, n, HD]), ALU.mult)
                if (l, t) != (0, 1):
                    ins.then_inc(normed, 1)
                    return
                then(ins)
                cos, ssin = K("cos"), K("ssin").rearrange("p (a b f) -> p a b f", a=2, b=2)
                for lo, n in ROPED:
                    v = qkv[t][:, lo:lo + n * HD].rearrange("p (h a b f) -> p h a b f", a=2, b=2, f=16)
                    w = scratch[t][:, lo:lo + n * HD].rearrange("p (h a b f) -> p h a b f", a=2, b=2, f=16)
                    for part in range(2):
                        ins = dve.tensor_tensor(w[:, :, :, part, :], v[:, :, :, 1 - part, :],
                                                ssin[:, :, part, :].unsqueeze(1).to_broadcast([P, n, 2, 16]), ALU.mult)
                then(ins)
                for lo, n in ROPED:
                    v = heads_of(t, lo, n)
                    ins = dve.tensor_tensor(v, v, cos.unsqueeze(1).to_broadcast([P, n, HD]), ALU.mult)
                then(ins)
                for lo, n in ROPED:
                    ins = dve.tensor_tensor(qkv[t][:, lo:lo + n * HD], qkv[t][:, lo:lo + n * HD], scratch[t][:, lo:lo + n * HD], ALU.add)
                ins.then_inc(normed, 1)

            def maxima(l, t, b):
                nk = P * (1 + t)
                if b >= 2:
                    dve.wait_ge(*exps_done(l, t, b - 2))
                for e in range(2):
                    name = ("S", l, t, b, e)
                    dve.wait_ge(filled, fill(name))
                    s = bank_of(name)[:, 0:2 * nk].rearrange("p (h k) -> p h k", h=2)
                    if (l, t) == (1, 1):
                        dve.tensor_copy(sc[:, b % 2, 2 * e:2 * e + 2, 0:P], s[:, :, 0:P])
                        dve.tensor_tensor(sc[:, b % 2, 2 * e:2 * e + 2, P:2 * P], s[:, :, P:2 * P],
                                          bias[:, 4 * b + e:4 * b + e + 3:2, :], ALU.add).then_inc(emptied["dve"], 1)
                        dve.wait_ge(*emptied_by(name))
                        s = sc[:, b % 2, 2 * e:2 * e + 2, :]
                    ins = dve.tensor_reduce(nm[:, b % 2, 2 * e:2 * e + 2], s, AX.X, ALU.max, negate=True)
                then(ins)
                dve.tensor_scalar(nm[:, b % 2, :], nm[:, b % 2, :], SCALE, None, ALU.mult).then_inc(max_ready, 1)

            def shares(l, t, b):
                nk = P * (1 + t)
                dve.wait_ge(*exps_done(l, t, b))
                then(dve.reciprocal(rinv[:, b % 2, :], rs[:, b % 2, :]))
                if l == 0 and b >= 2:
                    then(dve.tensor_scalar(rinv[:, b % 2, 2:4], rinv[:, b % 2, 2:4], lam[:, 0:1], None, ALU.mult))
                    for i in range(2):
                        ins = dve.tensor_scalar(PR[:, b % 2, 2 + i, 0:nk], PR[:, b % 2, 2 + i, 0:nk], rinv[:, b % 2, 2 + i:3 + i], None, ALU.mult)
                    then(ins)
                    for i in range(2):
                        ins = dve.scalar_tensor_tensor(out=PR[:, b % 2, i, 0:nk], in0=PR[:, b % 2, i, 0:nk], scalar=rinv[:, b % 2, i:i + 1],
                                                       in1=PR[:, b % 2, 2 + i, 0:nk], op0=ALU.mult, op1=ALU.add)
                else:
                    for j in range(4):
                        ins = dve.tensor_scalar(PR[:, b % 2, j, 0:nk], PR[:, b % 2, j, 0:nk], rinv[:, b % 2, j:j + 1], None, ALU.mult)
                ins.then_inc(shared, 1)

            def outputs(l, t, b):
                name = ("O", l, t, b)
                dve.wait_ge(filled, fill(name))
                at = 768 + 256 * (b - 2)
                dst = qkv[t][:, at:at + 256] if l == 0 and b >= 2 else oT(l, t, 2 * b, 2)
                dve.tensor_copy(dst, bank_of(name)[:, 0:256]).then_inc(emptied["dve"], 1)

            def sub_norm(t):
                v = qkv[t][:, 768:1280].rearrange("p (h d) -> p h d", h=4)
                w = tmp[:, t, :].rearrange("p (h d) -> p h d", h=4)
                dve.wait_ge(*emptied_by(("O", 0, t, BATCHES - 1)))
                then(dve.tensor_tensor(w, v, v, ALU.mult))
                then(dve.tensor_reduce(hss[:, 0:4], w, AX.X, ALU.add))
                rms_inverse(("sub", 0, t), 2 * HD)
                then(dve.tensor_tensor(v, v, hss[:, 0:4].unsqueeze(2).to_broadcast([P, 4, 2 * HD]), ALU.mult))
                dve.tensor_tensor(v, v, subg[:, :].unsqueeze(1).to_broadcast([P, 4, 2 * HD]), ALU.mult).then_inc(o_ready, 1)

            def out_project(l, u, t):
                name, k, cols = ("wo", l, u, t), 2 * t + u, slice(u * UC, (u + 1) * UC)
                dve.wait_ge(*emptied_by(("gb", l, 0, u, t)))
                dve.wait_ge(filled, fill(name))
                dve.tensor_tensor(tmp[:, k % 2, :], bank_of(name)[:, :], gbuf[:, k, :], ALU.mult).then_inc(emptied["dve"], 1)
                dve.wait_ge(*emptied_by(name))
                dve.tensor_tensor(x[:, t, cols], x[:, t, cols], tmp[:, k % 2, :], ALU.add).then_inc(x_ready, 1)

            def add_experts(l, t):
                for u in range(2):
                    k, cols = 2 * t + u, slice(u * UC, (u + 1) * UC)
                    dve.wait_ge(*emptied_by(("gb", l, 1, u, t)))
                    then(dve.tensor_tensor(tmp[:, k % 2, :], y[:, t, cols], gbuf[:, k, :], ALU.mult))
                    dve.tensor_tensor(x[:, t, cols], x[:, t, cols], tmp[:, k % 2, :], ALU.add).then_inc(x_ready, 1)

            def reverse_bias(i):
                name, part = ("rev", i), bias[:, 4 * i:4 * i + 4, :]
                over_heads = lambda v: v.unsqueeze(1).to_broadcast([P, 4, P])
                dve.wait_ge(filled, fill(name))
                dve.tensor_tensor(part, bank_of(name)[:, :].rearrange("p (h k) -> p h k", h=4), over_heads(K("mask8")),
                                  ALU.mult).then_inc(emptied["dve"], 1)
                dve.wait_ge(*emptied_by(name))
                then(dve.tensor_tensor(part, part, over_heads(K("neg")), ALU.add))

            def meanwhile(l, t, point):
                for name in fill_in(l, t, point):
                    if engine_of[name] == "dve":
                        {"modT": mod, "modG": mod, "qkv": project, "rev": reverse_bias, "wo": out_project}[name[0]](*name[1:])

            def beaten(out, values, groups, width):
                v = values.rearrange("p (g i) -> p g i", i=width)
                mine = v.unsqueeze(3).to_broadcast([P, groups, width, width])
                others = v.unsqueeze(2).to_broadcast([P, groups, width, width])
                n = groups * width * width
                more = cmp[:, 0:n].rearrange("p (g i j) -> p g i j", i=width, j=width)
                same = cmq[:, 0:n].rearrange("p (g i j) -> p g i j", i=width, j=width)
                dve.tensor_tensor(more, others, mine, ALU.is_gt)
                then(dve.tensor_tensor(same, others, mine, ALU.is_equal))
                low = K("low4").rearrange("p (i j) -> p i j", i=4).unsqueeze(1).to_broadcast([P, groups, width, width])
                then(dve.tensor_tensor(same, same, low, ALU.mult))
                then(dve.tensor_tensor(more, more, same, ALU.add))
                then(dve.tensor_reduce(out.rearrange("p (g i) -> p g i", i=width), more, AX.X, ALU.add))

            def router(l):
                flat = lambda v: v[:, :, :].rearrange("p t e -> p (t e)")
                per_token = lambda v: v.unsqueeze(2).to_broadcast([P, TT, NE])
                dve.wait_ge(filled, fill(("rt", l)))
                logits = bank_of(("rt", l))[:, 0:TT * NE].rearrange("p (t e) -> p t e", t=TT)
                then(dve.tensor_reduce(st2[:, 0:2], logits, AX.X, ALU.max))
                dve.tensor_tensor(lg[:, :, :], logits, per_token(st2[:, 0:2]), ALU.subtract).then_inc(emptied["dve"], 1)
                dve.wait_ge(*emptied_by(("rt", l)))
                dve.wait_ge(ex_ready, l + 1)
                then(dve.tensor_reduce(st2[:, 2:4], sco[:, :, :], AX.X, ALU.add))
                then(dve.reciprocal(st2[:, 2:4], st2[:, 2:4]))
                then(dve.tensor_tensor(sco[:, :, :], sco[:, :, :], per_token(st2[:, 2:4]), ALU.mult))
                then(dve.tensor_tensor(sel[:, :, :], sco[:, :, :], br[:, :].unsqueeze(1).to_broadcast([P, TT, NE]), ALU.add))
                beaten(flat(top), flat(sel), TT * NG, EG)
                then(dve.tensor_scalar(flat(top), flat(top), float(EG - 2), None, ALU.is_lt))
                then(dve.tensor_tensor(flat(chosen), flat(sel), flat(top), ALU.mult))
                then(dve.tensor_reduce(gsum[:, :], flat(chosen).rearrange("p (g i) -> p g i", i=EG), AX.X, ALU.add))
                beaten(cnt8[:, :], gsum[:, :], TT, NG)
                then(dve.tensor_scalar(cnt8[:, :], cnt8[:, :], 0.0, None, ALU.is_equal))
                dve.tensor_tensor(flat(chosen).rearrange("p (g i) -> p g i", i=EG), flat(top).rearrange("p (g i) -> p g i", i=EG),
                                  cnt8[:, :].unsqueeze(2).to_broadcast([P, TT * NG, EG]), ALU.mult).then_inc(mask_ready, 1)
                dve.wait_ge(mask_ready, l + 1)
                then(dve.tensor_tensor(gate[:, :, :], sco[:, :, :], chosen[:, :, :], ALU.mult))
                then(dve.tensor_reduce(st2[:, 0:2], gate[:, :, :], AX.X, ALU.add))
                then(dve.reciprocal(st2[:, 0:2], st2[:, 0:2]))
                then(dve.tensor_tensor(gate[:, :, :], gate[:, :, :], per_token(st2[:, 0:2]), ALU.mult))
                name = ("pos", l)
                dve.wait_ge(filled, fill(name))
                b = bank_of(name)
                then(dve.tensor_reduce(cnt[:, 0:1], b[:, 32:48], AX.X, ALU.max))
                dve.scalar_tensor_tensor(out=slot_of[:, :, :], in0=b[:, 0:32].rearrange("p (t e) -> p t e", t=TT), scalar=1.0,
                                         in1=chosen[:, :, :], op0=ALU.add, op1=ALU.mult).then_inc(emptied["dve"], 1)
                dve.wait_ge(*emptied_by(name))
                dve.memset(slot_t[:, :, ROUNDS_MAX * NE:], -1.0)
                dve.memset(gate_t[:, :, ROUNDS_MAX * NE:], 0.0)
                for r in range(ROUNDS_MAX):
                    dve.tensor_scalar(slot_t[:, :, r * NE:(r + 1) * NE], slot_of[:, :, :], -1.0 - CAP * r, None, ALU.add)
                    ins = dve.tensor_copy(gate_t[:, :, r * NE:(r + 1) * NE], gate[:, :, :])
                then(ins)
                then(dve.tensor_scalar(cmp[:, 0:ROUNDS_MAX - 1], K("thr"), cnt[:, 0:1], None, ALU.is_lt))
                then(dve.tensor_reduce(cnt[:, 1:2], cmp[:, 0:ROUNDS_MAX - 1], AX.X, ALU.add))
                dve.tensor_scalar(rounds[:, :], cnt[:, 1:2], 1.0, None, ALU.add).then_inc(rounds_ready, 1)
                dve.wait_ge(rounds_ready, l + 1)

            def experts(l):
                m = M[l]
                dve.wait_ge(out_kv[l], 64 if l == 0 else 32)
                dve.memset(work[:, 0:2048], 0.0)
                dve.memset(GT[:, :, :], 0.0).then_inc(m["y_zeroed"], 1)
                dve.memset(yd[:, 0:UC], 0.0).then_inc(m["yd0_ready"], 1)
                r_end = dve.value_load(rounds[0:1, 0:1], min_val=1, max_val=ROUNDS_MAX)

                def one_hots(n):
                    for t in range(TT):
                        for e in range(2):
                            col = bass.ds(2 * n + e, 1)
                            dve.tensor_scalar(pick[:, t, CAP * e:CAP * e + CAP], K("iota"), slot_t[:, t, col], None, ALU.is_equal)
                            ins = dve.tensor_scalar(gpick[:, t, CAP * e:CAP * e + CAP], K("iota"), slot_t[:, t, col], gate_t[:, t, col],
                                                    ALU.is_equal, ALU.mult)
                    ins.then_inc(m["picked"], 1)

                def hidden(n, h):
                    dve.wait_ge(m["sig_done"], 2 * n + h + 1)
                    half = slice(h * UC, (h + 1) * UC)
                    dve.tensor_tensor(hid[:, half], sg[:, half], bank[2 * h][:, :], ALU.mult).then_inc(m["loop_step"], 1)
                    dve.wait_ge(m["loop_step"], 2 * n + h + 1)
                    dve.wait_ge(moe_used[l], n * MOE_UNITS + (SLOTS + 4 * h + 4))
                    dve.tensor_tensor(hid[:, half], hid[:, half], bank[2 * h + 1][:, :], ALU.mult).then_inc(m["hid_done"], 1)

                def add_scattered(n):
                    for t in range(TT):
                        for h in range(2):
                            dve.wait_ge(m["scattered"], 4 * n + (2 * t + h + 1))
                            cols = slice(h * UC, (h + 1) * UC)
                            dve.tensor_tensor(y[:, t, cols], y[:, t, cols], bank[4 + 2 * t + h][:, :], ALU.add).then_inc(m["y_added"], 1)

                one_hots(0)
                with dve.Fori(0, r_end * PAIRS) as n:
                    hidden(n, 0)
                    add_scattered(n)
                    dve.wait_ge(m["gt_done"], n + 1)
                    one_hots(n + 1)
                    hidden(n, 1)
                    dve.wait_ge(moe_used[l], n * MOE_UNITS + (SLOTS + 10))
                    dve.tensor_copy(yd[:, 0:UC], bank[6][:, :]).then_inc(m["yd0_ready"], 1)
                add_scattered(r_end * PAIRS)
                dve.wait_ge(m["y_added"], r_end * (4 * PAIRS) + 4)

            for name, dst in ((("vecT",), vT), (("bT",), bT)):
                dve.wait_ge(filled, fill(name))
                dve.tensor_copy(dst[:, :], bank_of(name)[:, 0:dst.shape[1]]).then_inc(emptied["dve"], 1)
            dve.wait_ge(sig_ready, 1)
            dve.wait_ge(cleared, 2)
            dve.tensor_tensor(cond[:, :, 0:2].rearrange("p c t -> p t c"), vT[:, 0:16].rearrange("p (t c) -> p t c", t=2),
                              sig[:, :].rearrange("p (t c) -> p t c", t=2), ALU.mult).then_inc(cond_ready, 1)
            for t in range(TT):
                norm(0, 0, t)
            for u in range(4):
                mod(0, u)
            for l in range(LAYERS):
                modulate(l, 0)
                for u in range(4):
                    project(l, u, 1)
                if l == 0:
                    dve.wait_ge(ld_small, 16 * 11)
                    then(dve.tensor_tensor(lamw[:, :, :], lamv[:, 0:4:2, :], lamv[:, 1:4:2, :], ALU.mult))
                    dve.tensor_reduce(lam[:, 0:2], lamw[:, :, :], AX.X, ALU.add).then_inc(lam_dot, 1)
                    then(dve.tensor_scalar(subg[:, :], subg[:, :], 1.0 - LAM_INIT, None, ALU.mult))
                qk_norm(l, 0)
                if l == 0:
                    project(0, 4, 1)
                qk_norm(l, 1)
                if l == 0:
                    dve.wait_ge(lam_exp, 1)
                    then(dve.tensor_tensor(lam[:, 0:1], lam[:, 3:4], lam[:, 2:3], ALU.subtract))
                    then(dve.tensor_scalar(lam[:, 0:1], lam[:, 0:1], -LAM_INIT, None, ALU.add))
                for t in range(TT):
                    if (l, t) == (1, 1):
                        dve.wait_ge(out_kv[1], 32)
                    maxima(l, t, 0)
                    maxima(l, t, 1)
                    shares(l, t, 0)
                    meanwhile(l, t, 0)
                    for b in range(BATCHES):
                        outputs(l, t, b)
                        if b + 2 < BATCHES:
                            maxima(l, t, b + 2)
                        if b + 1 < BATCHES:
                            shares(l, t, b + 1)
                        meanwhile(l, t, b + 1)
                    if l == 0:
                        sub_norm(t)
                for t in range(TT):
                    if (l, t) != (1, 0):
                        for u in range(2):
                            out_project(l, u, t)
                    norm(l, 1, t)
                modulate(l, 1)
                router(l)
                experts(l)
                for t in range(TT):
                    add_experts(l, t)
                    if l == 0:
                        norm(1, 0, t)


_INS = ["x_prompt", "x_sample", "cache_a_k", "cache_a_v", "cache_b_k", "cache_b_v", "cache_c_k", "cache_c_v",
        "c", "c_ctx", "w_mod", "b_mod", "norm_mix", "norm_ffn", "w_in_ab", "w_out_ab", "a_q_norm", "a_k_norm",
        "b_q_norm", "b_k_norm", "lam_q1", "lam_k1", "lam_q2", "lam_k2", "b_subln", "w_in_c", "w_out_c",
        "c_q_norm", "c_k_norm", "c_rpb", "w_router", "b_router", "w_gate", "w_up", "w_down"]
_OUTS = [("y_prompt", (1, 128, 1024)), ("y_sample", (1, 128, 1024)),
         ("new_a_k", (1, 1, 128, 2, 64)), ("new_a_v", (1, 1, 128, 2, 64)),
         ("new_b_k", (1, 1, 128, 4, 2, 64)), ("new_b_v", (1, 1, 128, 4, 128)),
         ("new_c_k", (1, 1, 128, 16, 64)), ("new_c_v", (1, 1, 128, 16, 64))]


def kernel(**inputs):
    import concourse.bacc as bacc
    from concourse.bass_utils import run_bass_kernel_spmd

    nc = bacc.Bacc("TRN2", target_bir_lowering=False, num_devices=1)
    arrays, aps = {}, {}
    for name in _INS:
        arr = np.ascontiguousarray(inputs[name])
        arrays["in_" + name] = arr
        aps[name] = nc.dram_tensor("in_" + name, arr.shape, mybir.dt.from_np(arr.dtype), kind="ExternalInput").ap()
    arrays["in_tables"] = constants()
    aps["tables"] = nc.dram_tensor("in_tables", (P, NCONST), F32, kind="ExternalInput").ap()
    for name, shape in _OUTS:
        flat = nc.dram_tensor("out_" + name, (P, int(np.prod(shape)) // P), F32, kind="ExternalOutput").ap()
        aps[name] = flat
    build(nc, aps)
    r = run_bass_kernel_spmd(nc, [arrays], core_ids=[0])
    return tuple(r.results[0]["out_" + name].reshape(shape) for name, shape in _OUTS)
```

```python
import numpy as np
import concourse.bass as bass
from concourse import mybir
from contextlib import ExitStack

F32 = mybir.dt.float32
I32 = mybir.dt.int32
ALU = mybir.AluOpType
ACT = mybir.ActivationFunctionType
AX = mybir.AxisListType

D = 1024
P = 128
DC = D // P
TT = 2
LAYERS = 2
HD = 64
GRID_W = 64
EPS = 1e-6
SCALE = HD ** -0.5
A_Q, A_KV, B_QK, B_V = 512, 128, 512, 512
AB_IN = A_Q + 2 * A_KV + 2 * B_QK + B_V
C_W = 1024
NE, NG, EG = 16, 4, 4
NA_COLS = 16
LAM_INIT = 0.2
MASKED = -1.0e30

UC = 512
SLOTS = 6
CAP = 64
ROUNDS_MAX = TT * P // CAP
PAIRS = NE // 2
MOE_UNITS = 12

CONST = {}
_at = 0
for _name, _n in (("ident", P), ("upper", P), ("ones", P), ("iota", CAP), ("sel2", 32), ("selg", 8), ("rev", P), ("mhalf", HD),
                  ("mask8", P), ("neg", P), ("low4", 16), ("cos", HD), ("ssin", HD), ("thr", ROUNDS_MAX - 1),
                  ("before", ROUNDS_MAX * NE)):
    CONST[_name] = (_at, _n)
    _at += _n
NCONST = _at


def constants():
    c = np.zeros((P, NCONST), np.float32)

    def block(name):
        at, n = CONST[name]
        return c[:, at:at + n]

    row, lane = np.arange(P)[:, None], np.arange(P)[None, :]
    block("ident")[:] = row == lane
    block("upper")[:] = row < lane
    block("ones")[:] = 1.0
    block("iota")[:] = np.arange(CAP)[None, :]
    for t in range(TT):
        block("sel2")[:, t] = (np.arange(P) % 32) == t
        for k in range(4):
            block("selg")[:, 2 * k + t] = (np.arange(P) == 32 * k + t) | (np.arange(P) == 32 * k + 2)
    block("mhalf")[:] = -0.5
    block("rev")[:] = row == lane - lane % GRID_W + GRID_W - 1 - lane % GRID_W
    col = np.arange(P) % GRID_W
    first = np.clip(col - NA_COLS // 2, 0, GRID_W - NA_COLS)
    inside = (col[None, :] >= first[:, None]) & (col[None, :] < first[:, None] + NA_COLS)
    block("mask8")[:] = inside / SCALE
    block("neg")[:] = np.where(inside, 0.0, MASKED)
    block("low4")[:] = (np.arange(4)[None, :] < np.arange(4)[:, None]).reshape(1, 16)
    freq = 10000.0 ** (-np.arange(16, dtype=np.float32) / np.float32(16))
    for half, pos in enumerate((np.arange(P) // GRID_W, np.arange(P) % GRID_W)):
        angle = pos.astype(np.float32)[:, None] * freq.astype(np.float32)[None, :]
        for part, sign in ((0, -1.0), (1, 1.0)):
            at = half * 32 + part * 16
            block("cos")[:, at:at + 16] = np.cos(angle)
            block("ssin")[:, at:at + 16] = sign * np.sin(angle)
    block("before")[:] = -1.0 - CAP * np.repeat(np.arange(ROUNDS_MAX), NE)[None, :]
    block("thr")[:] = CAP * np.arange(1, ROUNDS_MAX)[None, :]
    return c


NORMED = {0: [(0, 8, 0), (512, 2, 1), (768, 8, 2), (1280, 8, 3)], 1: [(0, 16, 4), (1024, 16, 5)]}
SPANS = {0: [(0, 640), (768, 1792)], 1: [(0, 2048)]}
ROPED = [(0, 10), (768, 16)]
QKV_COLS = {0: AB_IN, 1: 3 * C_W}
Q_CHUNKS = {0: [0, 768], 1: [0, 512]}
O_COLS = {0: [0, 768], 1: [0, 512]}
K_JOBS = {(0, 0): 2, (0, 1): 3, (1, 0): 2, (1, 1): 4}
BATCHES = 4


MOD_AT = {(0, 0, -1): 1, (0, 0, 0): 2, (0, 0, 1): 1, (0, 0, 2): 1, (0, 0, 3): 1, (0, 0, 4): 1,
          (0, 1, -1): 0, (0, 1, 0): 2, (0, 1, 1): 1, (0, 1, 2): 1, (0, 1, 3): 1, (0, 1, 4): 1,
          (0, "norm", 0): 2, (0, "router", 0): 5}


def fill_in(*point):
    mods = [(0, u) for u in range(4, 12)] + [(1, u) for u in range(12)]
    ends = [sum(n for at, n in MOD_AT.items() if at[0] <= l) for l in range(LAYERS)]
    names, j = [], 0
    for at, n in MOD_AT.items():
        if at == point:
            for i in range(j, j + n):
                names += [("mod",) + mods[i]] + ([mod_sum(*mods[i - 1])] if i and i not in ends else [])
                if i + 1 in ends:
                    names.append(mod_sum(*mods[i]))
        j += n
    others = {(0, 1, 4): [("gb", 0, 0, u, tt) for tt in range(TT) for u in range(2)],
              (1, 0, 0): [("qkv", 1, 4, 1)], (1, 0, 1): [("qkv", 1, 5, 1)],
              (1, 0, 2): [("gb", 1, 0, u, tt) for tt in range(TT) for u in range(2)], (1, 0, 3): [("rev", i) for i in range(4)],
              (1, 1, 0): [("wo", 1, 0, 0)], (1, 1, 1): [("wo", 1, 1, 0)]}
    return names + others.get(point, [])


def mod_sum(l, u):
    return ("modG" if u // 2 in (2, 5) else "modT", l, u)


def dense_units(layer):
    kinds, units, at = {"mod": "mod", "qkv": "in", "wo": "out"}, [], 0
    for job in psum_jobs():
        if job is None:
            at += 1
        elif at == layer and job[0][0] in kinds:
            unit = (kinds[job[0][0]],) + job[0][1:3]
            if unit not in units:
                units.append(unit)
    return units


EMPTIED_BY = {"vecT": "dve", "bT": "dve", "mod": "act", "modG": "dve", "modT": "dve", "T": "act", "PT": "act",
              "O": "dve", "oT": "act", "gb": "act", "wo": "dve", "hk": "act", "rt": "act", "pos": "dve", "rev": "dve"}


def psum_jobs():
    names = [("vecT",), ("bT",)]
    for u in range(4):
        names += [("mod", 0, u), mod_sum(0, u)]
    for l in range(LAYERS):
        names += [("hT", l, 0, t, h) for t in range(TT) for h in range(2)]
        for u in range(-(-QKV_COLS[l] // UC)):
            names += [("qkv", l, u, t) for t in range(TT) if ("qkv", l, u, t) not in fill_in(l, 0, 0) + fill_in(l, 0, 1)]
        for t in range(TT):
            names += fill_in(l, t, -1)
            names += [("T", l, t, i) for i in range(2 + K_JOBS[l, t])]
            names += [("S", l, t, b, e) for b in range(2) for e in range(2)]
            names += fill_in(l, t, 0)
            for b in range(BATCHES):
                names += [("PT", l, t, b, k) for k in range(pt_jobs(l, t, b))] + [("O", l, t, b)]
                if b + 2 < BATCHES:
                    names += [("S", l, t, b + 2, e) for e in range(2)]
                names += fill_in(l, t, b + 1)
            if l == 0:
                names += [("oT", 0, t)]
        names += [("wo", l, u, 0) for u in range(2) if l == 0] + [("wo", l, 0, 1)]
        for t in range(TT):
            names += fill_in(l, "norm", 0) if t else []
            names += [("hT", l, 1, t, h) for h in range(2)] + ([] if t else [("wo", l, 1, 1)])
            names += [("rt", l, t)] + [("hk", l, t, h) for h in range(2)]
        names += fill_in(l, "router", 0)
        names += [("gb", l, 1, u, t) for t in range(TT) for u in range(2)] + [("pos", l), None]

    def engine(name):
        kind = name[0]
        if kind == "hT":
            return ("act", "dve")[name[4]]
        if kind == "qkv":
            return ("act", "dve")[name[3]]
        if kind == "S":
            return "dve" if name[1:3] == (1, 1) else "act"
        return EMPTIED_BY[kind]

    return [name and (name, engine(name)) for name in names]


def pt_jobs(l, t, b):
    return 2 if t == 1 and (l == 1 or b < 2) else 1


def build(nc, a):
    ctx = ExitStack()
    with ctx:
        def sb(name, shape, dt=F32):
            return ctx.enter_context(nc.sbuf_tensor(name, shape, dt))

        def sem(name):
            return ctx.enter_context(nc.semaphore(name))

        ring = [sb(f"ring{i}", [P, DC, UC]) for i in range(SLOTS)]
        x = sb("x", [P, TT, D])
        hT = sb("hT", [P, DC, TT * P])
        work = sb("work", [P, 15360])
        const = sb("const", [P, NCONST])
        gates = sb("gates", [P, D])
        gbuf = sb("gbuf", [P, 4, UC])
        tmp = sb("tmp", [P, 2, UC])
        m4 = sb("m4", [P, 2, UC])
        vecs = sb("vecs", [48, P])
        bvec = sb("bvec", [96, P])
        vT = sb("vT", [P, 48])
        bT = sb("bT", [P, 96])
        sig = sb("sig", [P, 16])
        cond = sb("cond", [P, DC, 32])
        modc = sb("modc", [P, LAYERS, 4, TT, DC])
        gain = sb("gain", [P, 6, HD])
        subg = sb("subg", [P, P])
        lamv = sb("lamv", [P, 4, HD])
        lamw = sb("lamw", [P, 2, HD])
        lam = sb("lam", [P, 4])
        wr = sb("wr", [P, DC, NE])
        br = sb("br", [P, NE])
        ss = sb("ss", [P, 4])
        hss = sb("hss", [P, 64])
        nm = sb("nm", [P, 2, 4])
        rs = sb("rs", [P, 2, 4])
        rinv = sb("rinv", [P, 2, 4])
        sco = sb("sco", [P, TT, NE])
        sel = sb("sel", [P, TT, NE])
        cmp = sb("cmp", [P, 128])
        cmq = sb("cmq", [P, 128])
        top = sb("top", [P, TT, NE])
        gsum = sb("gsum", [P, TT * NG])
        chosen = sb("chosen", [P, TT, NE])
        gate = sb("gate", [P, TT, NE])
        st2 = sb("st2", [P, 4])
        cnt = sb("cnt", [P, 4])
        cnt8 = sb("cnt8", [P, TT * NG])
        rounds = sb("rounds", [P, 1], I32)
        slot_of = sb("slot_of", [P, TT, NE])
        SLOT_COLS = ROUNDS_MAX * NE + 2
        slot_t = sb("slot_t", [P, TT, SLOT_COLS])
        gate_t = sb("gate_t", [P, TT, SLOT_COLS])

        bank = [ctx.enter_context(nc.psum_tensor(f"bank{i}", [P, 512], F32)) for i in range(8)]

        def K(name):
            at, n = CONST[name]
            return const[:, at:at + n]

        qkv = [work[:, 3072 * t:3072 * (t + 1)] for t in range(TT)]
        cache = work[:, 6144:8192]
        QT = work[:, 8192:9216].rearrange("p (c q) -> p c q", c=8)
        KT = work[:, 9216:11264].rearrange("p (c k) -> p c k", c=8)
        PR = work[:, 11264:13312].rearrange("p (b h k) -> p b h k", b=2, h=4)
        PTs = work[:, 13312:15360].rearrange("p (b h q) -> p b h q", b=2, h=8)
        xn = work[:, 11264:13312].rearrange("p (t d) -> p t d", t=2)
        scratch = [work[:, 11264:13312], work[:, 13312:15360]]
        bias = hT[:, :, :].rearrange("p c n -> p (c n)").rearrange("p (h k) -> p h k", h=16)
        sc = work[:, 1024:3072].rearrange("p (b h k) -> p b h k", b=2, h=4)
        def oT(l, t, c, n=1):
            at = 3072 * t + P * c + (2304 - 4 * P if l == 0 and c >= 4 else 0)
            return work[:, at:at + n * P]

        rot = hT[:, :, :].rearrange("p c n -> p (c n)")
        y = work[:, 0:2048].rearrange("p (t d) -> p t d", t=2)
        htok = work[:, 2048:4096].rearrange("p (t d) -> p t d", t=2)
        hgT = work[:, 4096:5120].rearrange("p (c s) -> p c s", c=8)
        yd = work[:, 5120:6144]
        sg = work[:, 8192:9216]
        hid = work[:, 9216:10240]
        hidT = work[:, 10240:11264].rearrange("p (c s) -> p c s", c=8)
        pick = work[:, 13312:13568].rearrange("p (t s) -> p t s", t=2)
        gpick = work[:, 13568:13824].rearrange("p (t s) -> p t s", t=2)
        GT = work[:, 13824:14080].rearrange("p (t q) -> p t q", t=2)

        filled = sem("bank_filled")
        emptied = {"act": sem("bank_emptied_act"), "dve": sem("bank_emptied_dve")}
        dense_ld = [sem(f"dense_loaded{i}") for i in range(SLOTS)]
        moe_used = [sem(f"moe_used{l}") for l in range(LAYERS)]
        moe_ld = [[sem(f"moe_loaded{l}_{i}") for i in range(SLOTS)] for l in range(LAYERS)]
        ld_const, ld_vec, ld_x, ld_gb, ld_small, ld_router = (
            sem(n) for n in ("ld_const", "ld_vec", "ld_x", "ld_gate_bias", "ld_small", "ld_router"))
        ld_cache = [sem(f"ld_cache{l}") for l in range(LAYERS)]
        ld_bias = sem("ld_bias")
        turns = sem("turns")
        out_kv = [sem(f"out_kv{l}") for l in range(LAYERS)]
        out_y = sem("out_y")
        cleared = sem("cleared")
        sig_ready, cond_ready, lam_dot, lam_exp, lam_ready = (
            sem(n) for n in ("sig_ready", "cond_ready", "lam_dot", "lam_exp", "lam_ready"))
        mod_ready = sem("mod_ready")
        power_asked, power_taken = sem("power_asked"), sem("power_taken")
        ssq_ready, xn_ready, x_ready = sem("ssq_ready"), sem("xn_ready"), sem("x_ready")
        squares, normed = sem("squares"), sem("qk_normed")
        max_ready, exps_ready, shared, o_ready = (
            sem(n) for n in ("max_ready", "exps_ready", "probs_shared", "o_ready"))
        logit_max, mask_ready, rounds_ready = (sem(n) for n in ("logit_max", "mask_ready", "rounds_ready"))
        dve_step = sem("dve_step")
        M = [{n: sem(f"{n}{l}") for n in (
            "y_zeroed", "picked", "gathered", "hg_ready", "sig_done", "hid_done", "scattered", "y_added",
            "gt_done", "gt_ready", "ht_done", "ht_ready", "yd0_ready", "yd1_ready", "loop_step")} for l in range(LAYERS)]

        powers = {}
        for l in range(LAYERS):
            n = sum(hi - lo for lo, hi in SPANS[l]) // HD
            powers["norm", l, 0, 0], powers["norm", l, 0, 1] = ss[:, 0:1], ss[:, 1:2]
            powers["qk", l, 0], powers["qk", l, 1] = hss[:, 0:n], hss[:, 32:32 + n]
            if l == 0:
                powers["sub", 0, 0], powers["sub", 0, 1] = hss[:, 0:4], hss[:, 0:4]
            powers["norm", l, 1, 0], powers["norm", l, 1, 1] = ss[:, 0:1], ss[:, 1:2]

        jobs = [j for j in psum_jobs() if j]
        number = {name: k for k, (name, _) in enumerate(jobs)}
        engine_of = dict(jobs)
        done_at, seen = {}, {"act": 0, "dve": 0}
        for name, eng in jobs:
            seen[eng] += 1
            done_at[name] = seen[eng]
        after_loop, k = set(), 0
        for j in psum_jobs():
            if j is None:
                after_loop.update(range(k, k + 8))
            else:
                k += 1
        units = dense_units(0) + dense_units(1)
        N0 = len(dense_units(0))
        unit_no = {u: i for i, u in enumerate(units)}
        MOE_AT = [N0 % SLOTS, len(units) % SLOTS]

        def fill(name):
            return number[name] + 1

        def read_at(g):
            kind, l, u = units[g]
            return fill({"mod": ("mod", l, u), "in": ("qkv", l, u, 1), "out": ("wo", l, u, 1)}[kind])

        def emptied_by(name):
            return emptied[engine_of[name]], done_at[name]

        def exps_done(l, t, b):
            return (exps_ready, b + 1) if (l, t) == (1, 1) else emptied_by(("S", l, t, b, 1))

        def bank_of(name):
            return bank[number[name] % 8]

        w_in = [a["w_in_ab"][0], a["w_in_c"][0]]
        w_out = [a["w_out_ab"][0], a["w_out_c"][0]]

        def unit_cols(u):
            kind, l, i = u
            return min(UC, QKV_COLS[l] - i * UC) if kind == "in" else UC

        def unit_src(u):
            kind, l, i = u
            w = {"mod": a["w_mod"][l], "in": w_in[l], "out": w_out[l]}[kind]
            return w[:, i * UC:i * UC + unit_cols(u)].rearrange("(c p) n -> p c n", p=P)

        block = ctx.enter_context(nc.Block())

        @block.sync
        def _(sp):
            def dense(layer, rounds_of_0=None):
                for i, u in enumerate(dense_units(layer)):
                    g = N0 * layer + i
                    if layer == 1 and i < SLOTS:
                        sp.wait_ge(moe_used[0], rounds_of_0 * (PAIRS * MOE_UNITS) + (i + 1))
                    elif g >= SLOTS:
                        sp.wait_ge(filled, read_at(g - SLOTS))
                    sp.dma_start(ring[g % SLOTS][:, :, 0:unit_cols(u)], unit_src(u)).then_inc(dense_ld[g % SLOTS], 16)

            def experts(l):
                def load(k, at, wait):
                    w, half = [(a["w_gate"], 0), (a["w_up"], 0), (a["w_gate"], 1), (a["w_up"], 1),
                               (a["w_down"], 0), (a["w_down"], 1)][k // 2]
                    flat = w[l].rearrange("e k n -> (e k n)")[bass.ds(at, D * D)]
                    src = flat.rearrange("(c p n) -> p c n", p=P, n=D)[:, :, half * UC:(half + 1) * UC]
                    slot = (MOE_AT[l] + k) % SLOTS
                    if wait is not None:
                        sp.wait_ge(moe_used[l], wait)
                        sp.sem_inc(turns, 1)
                    sp.dma_start(ring[slot][:, :, :], src).then_inc(moe_ld[l][slot], 16)

                def units_of(n, i, which):
                    at = [sp.snap(i * (2 * D * D) + e * D * D) for e in range(2)]
                    for k in which:
                        load(k, at[k % 2], n * MOE_UNITS + (k + 1))

                first, later = range(SLOTS), range(SLOTS, MOE_UNITS)

                for k in range(SLOTS):
                    sp.wait_ge(filled, read_at((N0 if l == 0 else len(units)) - SLOTS + k))
                    load(k, (k % 2) * D * D, None)
                sp.wait_ge(rounds_ready, l + 1)
                r_end = sp.value_load(rounds[0:1, 0:1], min_val=1, max_val=ROUNDS_MAX)
                with sp.Fori(0, r_end) as r:
                    with sp.Fori(0, PAIRS - 1) as i:
                        units_of(r * PAIRS + i, i, later)
                        units_of(r * PAIRS + i + 1, i + 1, first)
                    units_of(r * PAIRS + (PAIRS - 1), PAIRS - 1, later)
                    with sp.If(r + 1 < r_end):
                        units_of((r + 1) * PAIRS, 0, first)
                    sp.nop()
                return r_end

            sp.dma_start(const[:, :], a["tables"]).then_inc(ld_const, 16)
            for row, src in ((0, a["c_ctx"]), (8, a["c"]), (16, a["norm_mix"]), (32, a["norm_ffn"])):
                n = 16 if row >= 16 else 8
                flat = src if len(src.shape) == 1 else src.rearrange("a b -> (a b)")
                sp.dma_start(vecs[row:row + n, :], flat.rearrange("(r p) -> r p", p=P)).then_inc(ld_vec, 16)
            sp.dma_start(bvec[:, :], a["b_mod"].rearrange("l (r p) -> (l r) p", p=P)).then_inc(ld_vec, 16)
            for t, name in enumerate(("x_prompt", "x_sample")):
                sp.dma_start(x[:, t, :], a[name][0]).then_inc(ld_x, 16)
            dense(0)
            r0 = experts(0)
            dense(1, r0)
            experts(1)
            for t, name in enumerate(("y_prompt", "y_sample")):
                sp.wait_ge(x_ready, 4 * 4 - 1 + t)
                sp.dma_start(a[name], x[:, t, :]).then_inc(out_y, 16)
            sp.wait_ge(out_y, 32)

        @block.gpsimd
        def _(pool):
            pool.memset(cond[:, :, :], 0.0).then_inc(cleared, 1)
            pool.memset(gates[:, :], 0.0).then_inc(cleared, 1)
            pool.wait_ge(cleared, 2)
            for l in range(LAYERS):
                for kind in range(2):
                    k = 2 * l + kind
                    at = (2 + 3 * kind) * D
                    pool.dma_start(gates[32 * k + 2:32 * k + 3, :], a["b_mod"][l:l + 1, at:at + D]).then_inc(ld_gb, 16)
            for i, name in enumerate(("a_q_norm", "a_k_norm", "b_q_norm", "b_k_norm", "c_q_norm", "c_k_norm")):
                pool.dma_start(gain[:, i, :], a[name][0].partition_broadcast(P)).then_inc(ld_small, 16)
            pool.dma_start(subg[:, :], a["b_subln"][0].partition_broadcast(P)).then_inc(ld_small, 16)
            for i, name in enumerate(("lam_q1", "lam_k1", "lam_q2", "lam_k2")):
                pool.dma_start(lamv[:, i, :], a[name][0].partition_broadcast(P)).then_inc(ld_small, 16)
            at = 0
            for name in ("cache_a_k", "cache_a_v", "cache_b_k", "cache_b_v"):
                src = a[name][0, 0]
                src = src.rearrange("k h s d -> k (h s d)") if len(src.shape) == 4 else src.rearrange("k h d -> k (h d)")
                pool.dma_start(cache[:, at:at + src.shape[1]], src).then_inc(ld_cache[0], 16)
                at += src.shape[1]
            pool.dma_start(wr[:, :, :], a["w_router"].rearrange("(c p) e -> p c e", p=P)).then_inc(ld_router, 16)
            pool.dma_start(br[:, :], a["b_router"].partition_broadcast(P)).then_inc(ld_router, 16)

            def power(*which):
                v = powers[which]
                pool.wait_ge(power_asked, list(powers).index(which) + 1)
                pool.tensor_tensor(v, v, K("mhalf")[:, 0:v.shape[1]], ALU.pow).then_inc(power_taken, 1)

            pool.wait_ge(ld_const, 16)
            for l in range(LAYERS):
                power("norm", l, 0, 0)
                power("norm", l, 0, 1)
                last = -(-QKV_COLS[l] // UC) - 1
                power("qk", l, 0)
                power("qk", l, 1)
                pool.wait_ge(normed, 2 * l + 1)
                pool.wait_ge(*emptied_by(("qkv", l, last, 0)))
                if l == 0:
                    outs = [("new_a_k", 512, 128), ("new_a_v", 640, 128), ("new_b_k", 1280, 512), ("new_b_v", 1792, 512)]
                else:
                    outs = [("new_c_k", 1024, 1024), ("new_c_v", 2048, 1024)]
                for name, at, n in outs:
                    pool.dma_start(a[name], qkv[0][:, at:at + n]).then_inc(out_kv[l], 16)
                if l == 1:
                    pool.wait_ge(filled, fill(("qkv", 1, last, 1)))
                    rpb = a["c_rpb"]
                    for r in range(2):
                        for r2 in range(2):
                            src = bass.AP(rpb.tensor, rpb.offset + (r2 - r + 7) * 31 + 15 - 63, [[1, 64], [15 * 31, 16], [1, 64]])
                            pool.dma_start(bias[64 * r:64 * r + 64, :, 64 * r2:64 * r2 + 64], src).then_inc(ld_bias, 16)
                if l == 0:
                    power("sub", 0, 0)
                    power("sub", 0, 1)
                    pool.wait_ge(filled, fill(("O", 0, 1, BATCHES - 1)))
                    pool.dma_start(cache[:, 0:1024], a["cache_c_k"][0, 0].rearrange("k h d -> k (h d)")).then_inc(ld_cache[1], 16)
                    pool.dma_start(cache[:, 1024:2048], a["cache_c_v"][0, 0].rearrange("k h d -> k (h d)")).then_inc(ld_cache[1], 16)
                power("norm", l, 1, 0)
                power("norm", l, 1, 1)
            pool.wait_ge(out_kv[0], 64)
            pool.wait_ge(out_kv[1], 32)

        @block.tensor
        def _(pe):
            def bank_free(name):
                k = number[name]
                if k >= 8 and k not in after_loop:
                    pe.wait_ge(*emptied_by(jobs[k - 8][0]))
                return bank_of(name)

            def arrived(u):
                g = unit_no[u]
                pe.wait_ge(dense_ld[g % SLOTS], 16 * len([h for h in range(g + 1) if h % SLOTS == g % SLOTS]))
                return ring[g % SLOTS]

            def transposes(name, parts):
                b = bank_free(name)
                for i, src in enumerate(parts):
                    ins = pe.transpose(b[:, i * P:(i + 1) * P], src, K("ident"))
                ins.then_inc(filled, 1)

            def mod(l, u):
                w = arrived(("mod", l, u))
                b = bank_free(("mod", l, u))
                for c in range(DC):
                    j = 32 * (c % 4)
                    ins = pe.matmul(b[j:j + 32, :], cond[:, c, :], w[:, c, :], start=c < 4, stop=c >= 4,
                                    tile_position=(0, j))
                ins.then_inc(filled, 1)

            def add_groups(l, u):
                v, name = u // 2, mod_sum(l, u)
                b = bank_free(name)
                pe.wait_ge(*emptied_by(("mod", l, u)))
                if v in (2, 5):
                    k = 2 * l + v // 5
                    ins = pe.matmul(b[32 * k:32 * k + 32, :], K("sel2"), m4[:, u % 2, :], start=True, stop=True,
                                    tile_position=(0, 32 * k))
                else:
                    for c in range(4):
                        ins = pe.matmul(b[:, 2 * c:2 * c + 2], m4[:, u % 2, c * P:(c + 1) * P], K("sel2")[:, 0:2],
                                        start=True, stop=True)
                ins.then_inc(filled, 1)

            def norm(l, kind, t):
                pe.wait_ge(xn_ready, 4 * l + 2 * kind + t + 1)
                for h in range(2):
                    transposes(("hT", l, kind, t, h), [xn[:, t, (4 * h + i) * P:(4 * h + i + 1) * P] for i in range(4)])

            def project(l, u, t):
                w = arrived(("in", l, u))
                n = unit_cols(("in", l, u))
                b = bank_free(("qkv", l, u, t))
                for h in range(2):
                    pe.wait_ge(*emptied_by(("hT", l, 0, t, h)))
                for c in range(DC):
                    ins = pe.matmul(b[:, 0:n], hT[:, c, t * P:(t + 1) * P], w[:, c, 0:n], start=c == 0, stop=c == DC - 1)
                ins.then_inc(filled, 1)

            def reverse_bias(i):
                pe.wait_ge(ld_bias, 64)
                pe.matmul(bank_free(("rev", i))[:, :], K("rev"), bias[:, 4 * i:4 * i + 4, :], start=True, stop=True).then_inc(filled, 1)

            def gate_rows(l, kind, u, t):
                name, k = ("gb", l, kind, u, t), 2 * l + kind
                b = bank_free(name)
                pe.wait_ge(ld_gb, 64)
                pe.wait_ge(*emptied_by([n for n, _ in jobs[:number[name]] if n[0] == "modG"][-1]))
                pe.matmul(b[:, :], K("selg")[:, 2 * k + t:2 * k + t + 1].to_broadcast([P, P]),
                          gates[:, u * UC:(u + 1) * UC], start=True, stop=True).then_inc(filled, 1)

            def out_project(l, u, t):
                w = arrived(("out", l, u))
                b = bank_free(("wo", l, u, t))
                pe.wait_ge(*emptied_by(("O", l, t, BATCHES - 1)))
                if l == 0:
                    pe.wait_ge(*emptied_by(("oT", 0, t)))
                for c in range(DC):
                    ins = pe.matmul(b[:, :], oT(l, t, c), w[:, c, :], start=c == 0, stop=c == DC - 1)
                ins.then_inc(filled, 1)

            def meanwhile(*point):
                job = {"mod": mod, "modT": add_groups, "modG": add_groups, "qkv": project, "rev": reverse_bias,
                       "gb": gate_rows, "wo": out_project}
                for name in fill_in(*point):
                    job[name[0]](*name[1:])

            def attention(l, t):
                meanwhile(l, t, -1)
                pe.wait_ge(normed, 2 * l + t + 1)
                if t == 1:
                    pe.wait_ge(ld_cache[l], 16 * (4 if l == 0 else 2))
                X = qkv[t]
                chunk = lambda base, at: base[:, at:at + P]
                parts = [[chunk(X, at + i * P) for i in range(4)] for at in Q_CHUNKS[l]]
                if l == 0:
                    parts += [([chunk(cache, 0)] if t else []) + [chunk(X, 512)], [chunk(X, 1280 + i * P) for i in range(4)]]
                    if t:
                        parts += [[chunk(cache, 256 + i * P) for i in range(4)]]
                else:
                    parts += [[chunk(X, 1024 + (4 * h + i) * P) for i in range(4)] for h in range(2)]
                    if t:
                        parts += [[chunk(cache, (4 * h + i) * P) for i in range(4)] for h in range(2)]
                for i, p in enumerate(parts):
                    transposes(("T", l, t, i), p)
                for i in range(len(parts)):
                    pe.wait_ge(*emptied_by(("T", l, t, i)))
                nk = P * (1 + t)

                def scores(b):
                    banks = [bank_free(("S", l, t, b, e)) for e in range(2)]
                    for i in range(2):
                        for e in range(2):
                            h = 4 * b + 2 * i + e
                            kc = h // 2 if l == 1 else (h // 4 if h < 8 else 2 + (h - 8) // 2)
                            rows = slice(64 * e, 64 * e + 64)
                            ins = pe.matmul(banks[e][:, i * nk:(i + 1) * nk], QT[rows, h // 2, :], KT[rows, kc, 0:nk],
                                            start=True, stop=True, tile_position=(64 * e, 0))
                            if i == 1:
                                ins.then_inc(filled, 1)

                def values(b):
                    diff = l == 0 and b >= 2
                    pe.wait_ge(shared, (l * TT + t) * BATCHES + b + 1)
                    heads = range(2) if diff else range(4)
                    pr, pt = PR[:, b % 2], PTs[:, b % 2]
                    chunks = [(kc, h) for kc in range(1 + t) for h in heads]
                    n_jobs = pt_jobs(l, t, b)
                    per = len(chunks) // n_jobs
                    for k in range(n_jobs):
                        transposes(("PT", l, t, b, k), [pr[:, h, kc * P:(kc + 1) * P] for kc, h in chunks[k * per:(k + 1) * per]])
                    ob = bank_free(("O", l, t, b))
                    for k in range(n_jobs):
                        pe.wait_ge(*emptied_by(("PT", l, t, b, k)))
                    if b == 0:
                        pe.wait_ge(*emptied_by(("qkv", l, -(-QKV_COLS[l] // UC) - 1, t)))

                    def keys(kc, own, kept, width):
                        return cache[:, kept:kept + width] if kc < t else X[:, own:own + width]

                    if diff:
                        for h in heads:
                            at = P * (2 * (b - 2) + h)
                            for kc in range(1 + t):
                                ins = pe.matmul(ob[:, h * P:(h + 1) * P], pt[:, 2 * kc + h, :], keys(kc, 1792 + at, 768 + at, P),
                                                start=kc == 0, stop=kc == t)
                    elif l == 0:
                        for kc in range(1 + t):
                            for e in range(2):
                                ins = pe.matmul(ob[64 * e:64 * e + 64, 0:2 * P], keys(kc, 640 + HD * b, 128 + HD * b, HD),
                                                pt[:, 4 * kc + 2 * e:4 * kc + 2 * e + 2, :], start=kc == 0, stop=kc == t,
                                                tile_position=(0, 64 * e))
                    else:
                        for i in range(2):
                            for kc in range(1 + t):
                                for e in range(2):
                                    at = HD * (4 * b + 2 * i + e)
                                    ins = pe.matmul(ob[64 * e:64 * e + 64, i * P:(i + 1) * P], keys(kc, 2 * C_W + at, C_W + at, HD),
                                                    pt[:, 4 * kc + 2 * e + i, :], start=kc == 0, stop=kc == t,
                                                    tile_position=(0, 64 * e))
                    ins.then_inc(filled, 1)

                scores(0)
                scores(1)
                meanwhile(l, t, 0)
                for b in range(BATCHES):
                    values(b)
                    if b + 2 < BATCHES:
                        scores(b + 2)
                    meanwhile(l, t, b + 1)
                if l == 0:
                    pe.wait_ge(o_ready, t + 1)
                    transposes(("oT", 0, t), [X[:, 768 + i * P:768 + (i + 1) * P] for i in range(4)])

            def logits(l, t):
                for h in range(2):
                    pe.wait_ge(*emptied_by(("hT", l, 1, t, h)))
                pe.wait_ge(ld_router, 32)
                b = bank_free(("rt", l, t))
                for c in range(DC):
                    ins = pe.matmul(b[:, 0:NE], hT[:, c, t * P:(t + 1) * P], wr[:, c, :], start=c == 0, stop=c == DC - 1)
                ins.then_inc(filled, 1)
                for h in range(2):
                    transposes(("hk", l, t, h), [hT[:, 4 * h + i, t * P:(t + 1) * P] for i in range(4)])

            def router(l):
                meanwhile(l, "router", 0)
                for t in range(TT):
                    for u in range(2):
                        gate_rows(l, 1, u, t)
                pe.wait_ge(mask_ready, l + 1)
                b = bank_free(("pos", l))
                pe.matmul(b[:, 0:16], K("upper"), chosen[:, 0, :], start=True, stop=True)
                pe.matmul(b[:, 16:32], K("upper"), chosen[:, 1, :], start=True, stop=False)
                pe.matmul(b[:, 16:32], K("ones"), chosen[:, 0, :], start=False, stop=True)
                pe.matmul(b[:, 32:48], K("ones"), chosen[:, 0, :], start=True, stop=False)
                pe.matmul(b[:, 32:48], K("ones"), chosen[:, 1, :], start=False, stop=True).then_inc(filled, 1)

            def experts(l):
                m = M[l]

                def gather(n):
                    pe.wait_ge(m["picked"], n + 1)
                    for h in range(2):
                        for c in range(4):
                            for t in range(TT):
                                at = (4 * h + c) * P
                                ins = pe.matmul(bank[h][:, c * P:(c + 1) * P], htok[:, t, at:at + P], pick[:, t, :],
                                                start=t == 0, stop=t == 1)
                        ins.then_inc(m["gathered"], 1)

                def scatter(n):
                    for h in range(2):
                        pe.wait_ge(m[f"yd{h}_ready"], n + 1)
                        for t in range(TT):
                            pe.matmul(bank[4 + 2 * t + h][:, :], GT[:, t, :], yd[:, h * UC:(h + 1) * UC],
                                      start=True, stop=True).then_inc(m["scattered"], 1)

                def product(n, k, b, lhs, halves=None):
                    slots = [(MOE_AT[l] + k + e) % SLOTS for e in range(2)]
                    for e in range(2):
                        pe.wait_ge(moe_ld[l][slots[e]], 32 * n + 16 * (1 + k // SLOTS))
                    for c in range(DC):
                        if halves and c % 4 == 0:
                            pe.wait_ge(halves, 2 * n + (1 + c // 4))
                        for e in range(2):
                            ins = pe.matmul(bank[b][64 * e:64 * e + 64, :], lhs[:, c, 64 * e:64 * e + 64], ring[slots[e]][:, c, :],
                                            start=c == 0, stop=c == DC - 1, tile_position=(0, 64 * e))
                            if c == DC - 1:
                                ins.then_inc(moe_used[l], 1)

                last = number[("pos", l)]
                for k in range(last - 7, last + 1):
                    pe.wait_ge(*emptied_by(jobs[k][0]))
                for t in range(TT):
                    for h in range(2):
                        pe.wait_ge(*emptied_by(("hk", l, t, h)))
                pe.sem_inc(moe_used[l], SLOTS)
                gather(0)
                pe.wait_ge(m["y_zeroed"], 1)
                pe.wait_ge(rounds_ready, l + 1)
                r_end = pe.value_load(rounds[0:1, 0:1], min_val=1, max_val=ROUNDS_MAX)
                with pe.Fori(0, r_end * PAIRS) as n:
                    product(n, 0, 0, hgT, m["hg_ready"])
                    product(n, 2, 1, hgT)
                    scatter(n)
                    for t in range(TT):
                        ins = pe.transpose(bank[3][:, t * P:(t + 1) * P], gpick[:, t, :], K("ident"))
                    ins.then_inc(m["gt_done"], 1)
                    product(n, 4, 2, hgT)
                    pe.wait_ge(m["gt_ready"], n + 1)
                    product(n, 6, 3, hgT)
                    pe.wait_ge(m["hid_done"], 2 * n + 1)
                    pe.wait_ge(m["y_added"], 4 * n + 4)
                    for c in range(4):
                        ins = pe.transpose(bank[4][:, c * P:(c + 1) * P], hid[:, c * P:(c + 1) * P], K("ident"))
                    ins.then_inc(m["ht_done"], 1)
                    gather(n + 1)
                    pe.wait_ge(m["hid_done"], 2 * n + 2)
                    for c in range(4):
                        ins = pe.transpose(bank[5][:, c * P:(c + 1) * P], hid[:, (4 + c) * P:(5 + c) * P], K("ident"))
                    ins.then_inc(m["ht_done"], 1)
                    pe.wait_ge(m["ht_ready"], 2 * n + 2)
                    product(n, 8, 6, hidT)
                    product(n, 10, 7, hidT)
                scatter(r_end * PAIRS)
                pe.wait_ge(m["y_added"], r_end * (4 * PAIRS) + 4)
                pe.wait_ge(m["hg_ready"], r_end * (2 * PAIRS) + 2)

            pe.wait_ge(ld_const, 16)
            pe.wait_ge(ld_vec, 80)
            pe.transpose(bank_free(("vecT",))[:, 0:48], vecs[:, :], K("ident")[0:48, 0:48]).then_inc(filled, 1)
            pe.transpose(bank_free(("bT",))[:, 0:96], bvec[:, :], K("ident")[0:96, 0:96]).then_inc(filled, 1)
            pe.wait_ge(cond_ready, 1)
            for u in range(4):
                mod(0, u)
                add_groups(0, u)
            for l in range(LAYERS):
                for t in range(TT):
                    norm(l, 0, t)
                for u in range(-(-QKV_COLS[l] // UC)):
                    for t in range(TT):
                        if (l, t) != (1, 1) or u < 4:
                            project(l, u, t)
                for t in range(TT):
                    attention(l, t)
                if l == 0:
                    out_project(0, 0, 0)
                    out_project(0, 1, 0)
                out_project(l, 0, 1)
                norm(l, 1, 0)
                out_project(l, 1, 1)
                logits(l, 0)
                meanwhile(l, "norm", 0)
                norm(l, 1, 1)
                logits(l, 1)
                router(l)
                experts(l)

        @block.scalar
        def _(act):
            def mod(l, u):
                act.wait_ge(filled, fill(("mod", l, u)))
                if 12 * l + u >= 2:
                    pl, pu = divmod(12 * l + u - 2, 12)
                    act.wait_ge(filled, fill(("modG" if pu // 2 in (2, 5) else "modT", pl, pu)))
                act.activation(m4[:, u % 2, :], bank_of(("mod", l, u))[:, :], ACT.Copy).then_inc(emptied["act"], 1)

            def norm(l, kind, t):
                done = 4 * (2 * l + kind)
                act.wait_ge(*((ld_x, 32) if done == 0 else (x_ready, done - (1 - t) * (1 + kind))))
                act.activation(xn[:, t, :], x[:, t, :], ACT.Square, accum_out=ss[:, t:t + 1]).then_inc(ssq_ready, 1)

            def modulate(l, kind, t):
                act.wait_ge(mod_ready, 4 * l + 2 * kind + 2)
                name = ("hT", l, kind, t, 0)
                act.wait_ge(filled, fill(name))
                for c in range(4):
                    ins = act.activation(hT[:, c, t * P:(t + 1) * P], bank_of(name)[:, c * P:(c + 1) * P], ACT.Identity,
                                         bias=modc[:, l, 2 * kind, t, c:c + 1], scale=modc[:, l, 2 * kind + 1, t, c:c + 1])
                ins.then_inc(emptied["act"], 1)

            def router(l, t):
                name = ("rt", l, t)
                act.wait_ge(logit_max, TT * l + t + 1)
                act.activation(sco[:, t, :], bank_of(name)[:, 0:NE], ACT.Exp, bias=st2[:, t:t + 1],
                               accum_out=st2[:, 2 + t:3 + t]).then_inc(emptied["act"], 1)
                act.wait_ge(out_kv[l], 64 if l == 0 else 32)
                for h in range(2):
                    name = ("hk", l, t, h)
                    act.wait_ge(filled, fill(name))
                    act.activation(htok[:, t, h * UC:(h + 1) * UC], bank_of(name)[:, :], ACT.Copy).then_inc(emptied["act"], 1)

            def project(l, u, t):
                name, n = ("qkv", l, u, t), unit_cols(("in", l, u))
                act.wait_ge(filled, fill(name))
                act.activation(qkv[0][:, u * UC:u * UC + n], bank_of(name)[:, 0:n], ACT.Copy).then_inc(emptied["act"], 1)

            def projection(l):
                for u in range(4):
                    project(l, u, 0)
                for t in range(TT):
                    act.wait_ge(*emptied_by(("qkv", l, 3, t)))
                    for lo, hi in SPANS[l]:
                        ins = act.activation(scratch[t][:, lo:hi], qkv[t][:, lo:hi], ACT.Square)
                    ins.then_inc(squares, 1)
                for u in range(4, -(-QKV_COLS[l] // UC)):
                    project(l, u, 0)

            def transposed(l, t):
                own = P * t
                for i in range(2 + K_JOBS[l, t]):
                    name = ("T", l, t, i)
                    act.wait_ge(filled, fill(name))
                    src = bank_of(name)[:, :].rearrange("p (c q) -> p c q", c=4)
                    if i < 2:
                        dst = QT[:, 4 * i:4 * i + 4, :]
                    elif l == 1:
                        at = 0 if i >= 4 else own
                        dst = KT[:, 4 * (i % 2):4 * (i % 2) + 4, at:at + P]
                    elif i == 2:
                        for kv in range(2):
                            for half in range(2):
                                ins = act.activation(KT[64 * half:64 * half + 64, kv, 0:own + P],
                                                     bank_of(name)[64 * kv:64 * kv + 64, 0:own + P], ACT.Copy)
                        ins.then_inc(emptied["act"], 1)
                        continue
                    else:
                        at = 0 if i == 4 else own
                        dst = KT[:, 2:6, at:at + P]
                    act.activation(dst, src, ACT.Copy).then_inc(emptied["act"], 1)

            def exps(l, t, b):
                nk = P * (1 + t)
                banked = (l, t) != (1, 1)
                act.wait_ge(max_ready, (l * TT + t) * BATCHES + b + 1)
                if b >= 2:
                    act.wait_ge(filled, fill(("PT", l, t, b - 2, pt_jobs(l, t, b - 2) - 1)))
                for e in range(2):
                    for i in range(2):
                        j = 2 * e + i
                        src = bank_of(("S", l, t, b, e))[:, i * nk:(i + 1) * nk] if banked else sc[:, b % 2, j, :]
                        ins = act.activation(PR[:, b % 2, j, 0:nk], src, ACT.Exp, bias=nm[:, b % 2, j:j + 1],
                                             scale=SCALE, accum_out=rs[:, b % 2, j:j + 1])
                    if banked:
                        ins.then_inc(emptied["act"], 1)
                if not banked:
                    ins.then_inc(exps_ready, 1)

            def probs_transposed(l, t, b):
                heads = 2 if l == 0 and b >= 2 else 4
                per = heads * (1 + t) // pt_jobs(l, t, b)
                for k in range(pt_jobs(l, t, b)):
                    name = ("PT", l, t, b, k)
                    act.wait_ge(filled, fill(name))
                    act.activation(PTs[:, b % 2, k * per:(k + 1) * per, :],
                                   bank_of(name)[:, 0:per * P].rearrange("p (c q) -> p c q", c=per),
                                   ACT.Copy).then_inc(emptied["act"], 1)

            def spread_gate(l, kind, u, t):
                name = ("gb", l, kind, u, t)
                act.wait_ge(filled, fill(name))
                if 2 * l + kind:
                    act.wait_ge(x_ready, 4 * (2 * l + kind))
                act.activation(gbuf[:, 2 * t + u, :], bank_of(name)[:, :], ACT.Copy).then_inc(emptied["act"], 1)

            def meanwhile(*point):
                for name in fill_in(*point):
                    if engine_of[name] == "act":
                        {"mod": mod, "gb": spread_gate}[name[0]](*name[1:])

            def experts(l):
                m = M[l]
                act.wait_ge(rounds_ready, l + 1)
                r_end = act.value_load(rounds[0:1, 0:1], min_val=1, max_val=ROUNDS_MAX)
                act.activation(yd[:, UC:2 * UC], const[:, 0:UC], ACT.Copy, scale=0.0).then_inc(m["yd1_ready"], 1)

                def gathered(n):
                    for h in range(2):
                        act.wait_ge(m["gathered"], 2 * n + h + 1)
                        act.activation(hgT[:, 4 * h:4 * h + 4, :], bank[h][:, :].rearrange("p (c s) -> p c s", c=4),
                                       ACT.Copy).then_inc(m["hg_ready"], 1)

                def hidden_transposed(n, h):
                    act.wait_ge(m["ht_done"], 2 * n + h + 1)
                    act.activation(hidT[:, 4 * h:4 * h + 4, :], bank[4 + h][:, :].rearrange("p (c s) -> p c s", c=4),
                                   ACT.Copy).then_inc(m["ht_ready"], 1)

                def sigmoid(n, h):
                    act.wait_ge(moe_used[l], n * MOE_UNITS + (SLOTS + 4 * h + 2))
                    act.activation(sg[:, h * UC:(h + 1) * UC], bank[2 * h][:, :], ACT.Sigmoid).then_inc(m["sig_done"], 1)

                gathered(0)
                with act.Fori(0, r_end * PAIRS) as n:
                    sigmoid(n, 0)
                    act.wait_ge(m["gt_done"], n + 1)
                    act.activation(GT[:, :, :], bank[3][:, 0:2 * P].rearrange("p (t q) -> p t q", t=2),
                                   ACT.Copy).then_inc(m["gt_ready"], 1)
                    sigmoid(n, 1)
                    hidden_transposed(n, 0)
                    gathered(n + 1)
                    hidden_transposed(n, 1)
                    act.wait_ge(moe_used[l], n * MOE_UNITS + (SLOTS + 12))
                    act.activation(yd[:, UC:2 * UC], bank[7][:, :], ACT.Copy).then_inc(m["yd1_ready"], 1)

            act.wait_ge(*emptied_by(("vecT",)))
            act.activation(sig[:, :], vT[:, 0:16], ACT.Sigmoid).then_inc(sig_ready, 1)
            for t in range(TT):
                norm(0, 0, t)
            for u in range(4):
                mod(0, u)
            for l in range(LAYERS):
                for t in range(TT) if l else ():
                    norm(l, 0, t)
                for t in range(TT):
                    modulate(l, 0, t)
                projection(l)
                if l == 0:
                    act.wait_ge(lam_dot, 1)
                    act.activation(lam[:, 2:4], lam[:, 0:2], ACT.Exp).then_inc(lam_exp, 1)
                for t in range(TT):
                    meanwhile(l, t, -1)
                    transposed(l, t)
                    exps(l, t, 0)
                    exps(l, t, 1)
                    meanwhile(l, t, 0)
                    for b in range(BATCHES):
                        probs_transposed(l, t, b)
                        if b + 2 < BATCHES:
                            exps(l, t, b + 2)
                        meanwhile(l, t, b + 1)
                    if l == 0:
                        act.wait_ge(filled, fill(("oT", 0, t)))
                        act.activation(oT(0, t, 4, 4), bank_of(("oT", 0, t))[:, :], ACT.Copy).then_inc(emptied["act"], 1)
                norm(l, 1, 0)
                modulate(l, 1, 0)
                norm(l, 1, 1)
                router(l, 0)
                meanwhile(l, "norm", 0)
                modulate(l, 1, 1)
                router(l, 1)
                meanwhile(l, "router", 0)
                for t in range(TT):
                    for u in range(2):
                        spread_gate(l, 1, u, t)
                experts(l)

        @block.vector
        def _(dve):
            steps = [0]

            def then(ins):
                steps[0] += 1
                ins.then_inc(dve_step, 1)
                dve.wait_ge(dve_step, steps[0])

            def ask(which, n):
                v = powers[which]
                dve.tensor_scalar(v, v, 1.0 / n, EPS, ALU.mult, ALU.add).then_inc(power_asked, 1)

            def taken(which):
                dve.wait_ge(power_taken, list(powers).index(which) + 1)

            def rms_inverse(which, n):
                ask(which, n)
                taken(which)

            def mod(l, u):
                v = u // 2
                if v in (2, 5):
                    name, k = ("modG", l, u), 2 * l + v // 5
                    dve.wait_ge(filled, fill(name))
                    at = (u % 2) * UC
                    dve.tensor_copy(gates[32 * k:32 * k + 2, at:at + UC], bank_of(name)[32 * k:32 * k + 2, :]).then_inc(emptied["dve"], 1)
                    return
                name, v4, c0 = ("modT", l, u), v - v // 3, 4 * (u % 2)
                dve.wait_ge(filled, fill(name))
                dst = modc[:, l, v4, :, c0:c0 + 4]
                bias_cols = bT[:, 48 * l + 8 * v + c0:48 * l + 8 * v + c0 + 4]
                dve.tensor_tensor(dst, bank_of(name)[:, 0:8].rearrange("p (c t) -> p t c", t=2),
                                  bias_cols.unsqueeze(1).to_broadcast([P, TT, 4]), ALU.add).then_inc(emptied["dve"], 1)
                if v4 % 2:
                    g0 = 16 + 16 * (v4 // 2) + 8 * l + c0
                    dve.wait_ge(*emptied_by(name))
                    dve.scalar_tensor_tensor(out=dst, in0=dst, scalar=1.0, in1=vT[:, g0:g0 + 4].unsqueeze(1).to_broadcast([P, TT, 4]),
                                             op0=ALU.add, op1=ALU.mult).then_inc(mod_ready, 1)

            def norm(l, kind, t):
                dve.wait_ge(ssq_ready, 2 * (2 * l + kind) + t + 1)
                rms_inverse(("norm", l, kind, t), D)
                dve.tensor_scalar(xn[:, t, :], x[:, t, :], ss[:, t:t + 1], None, ALU.mult).then_inc(xn_ready, 1)

            def modulate(l, kind, t):
                dve.wait_ge(mod_ready, 4 * l + 2 * kind + 2)
                name = ("hT", l, kind, t, 1)
                dve.wait_ge(filled, fill(name))
                for c in range(4):
                    ins = dve.tensor_scalar(hT[:, 4 + c, t * P:(t + 1) * P], bank_of(name)[:, c * P:(c + 1) * P],
                                            modc[:, l, 2 * kind + 1, t, 4 + c:5 + c], modc[:, l, 2 * kind, t, 4 + c:5 + c],
                                            ALU.mult, ALU.add)
                ins.then_inc(emptied["dve"], 1)

            def largest_logit(l, t):
                name = ("rt", l, t)
                dve.wait_ge(filled, fill(name))
                then(dve.tensor_reduce(st2[:, t:t + 1], bank_of(name)[:, 0:NE], AX.X, ALU.max))
                dve.tensor_scalar(st2[:, t:t + 1], st2[:, t:t + 1], -1.0, None, ALU.mult).then_inc(logit_max, 1)

            def project(l, u, t):
                name, n = ("qkv", l, u, t), unit_cols(("in", l, u))
                dve.wait_ge(filled, fill(name))
                dve.tensor_copy(qkv[1][:, u * UC:u * UC + n], bank_of(name)[:, 0:n]).then_inc(emptied["dve"], 1)

            def heads_of(t, lo, n):
                return qkv[t][:, lo:lo + n * HD].rearrange("p (h d) -> p h d", d=HD)

            def qk_sums(l, t):
                dve.wait_ge(squares, 2 * l + t + 1)
                at = 32 * t
                for lo, hi in SPANS[l]:
                    n = (hi - lo) // HD
                    ins = dve.tensor_reduce(hss[:, at:at + n], scratch[t][:, lo:hi].rearrange("p (h d) -> p h d", d=HD), AX.X, ALU.add)
                    at += n
                then(ins)
                ask(("qk", l, t), HD)

            def qk_norm(l, t):
                taken(("qk", l, t))
                at = 32 * t
                for lo, hi in SPANS[l]:
                    n = (hi - lo) // HD
                    v = heads_of(t, lo, n)
                    ins = dve.tensor_tensor(v, v, hss[:, at:at + n].unsqueeze(2).to_broadcast([P, n, HD]), ALU.mult)
                    at += n
                then(ins)
                for lo, n, g in NORMED[l]:
                    v = heads_of(t, lo, n)
                    ins = dve.tensor_tensor(v, v, gain[:, g, :].unsqueeze(1).to_broadcast([P, n, HD]), ALU.mult)
                if (l, t) != (0, 1):
                    ins.then_inc(normed, 1)
                    return
                then(ins)

            def rotate_by_sines():
                ssin = K("ssin").rearrange("p (a b f) -> p a b f", a=2, b=2)
                for lo, n in ROPED:
                    v, w = (z[:, lo:lo + n * HD].rearrange("p (h a b f) -> p h a b f", a=2, b=2, f=16) for z in (qkv[1], rot))
                    for part in range(2):
                        ins = dve.tensor_tensor(w[:, :, :, part, :], v[:, :, :, 1 - part, :],
                                                ssin[:, :, part, :].unsqueeze(1).to_broadcast([P, n, 2, 16]), ALU.mult)
                then(ins)

            def rotate_by_cosines():
                for lo, n in ROPED:
                    v = heads_of(1, lo, n)
                    ins = dve.tensor_tensor(v, v, K("cos").unsqueeze(1).to_broadcast([P, n, HD]), ALU.mult)
                then(ins)
                for lo, n in ROPED:
                    cols = slice(lo, lo + n * HD)
                    ins = dve.tensor_tensor(qkv[1][:, cols], qkv[1][:, cols], rot[:, cols], ALU.add)
                ins.then_inc(normed, 1)

            def maxima(l, t, b):
                nk = P * (1 + t)
                if b >= 2:
                    dve.wait_ge(*exps_done(l, t, b - 2))
                for e in range(2):
                    name = ("S", l, t, b, e)
                    dve.wait_ge(filled, fill(name))
                    s = bank_of(name)[:, 0:2 * nk].rearrange("p (h k) -> p h k", h=2)
                    if (l, t) == (1, 1):
                        dve.tensor_copy(sc[:, b % 2, 2 * e:2 * e + 2, 0:P], s[:, :, 0:P])
                        dve.tensor_tensor(sc[:, b % 2, 2 * e:2 * e + 2, P:2 * P], s[:, :, P:2 * P],
                                          bias[:, 4 * b + e:4 * b + e + 3:2, :], ALU.add).then_inc(emptied["dve"], 1)
                        dve.wait_ge(*emptied_by(name))
                        s = sc[:, b % 2, 2 * e:2 * e + 2, :]
                    ins = dve.tensor_reduce(nm[:, b % 2, 2 * e:2 * e + 2], s, AX.X, ALU.max, negate=True)
                then(ins)
                dve.tensor_scalar(nm[:, b % 2, :], nm[:, b % 2, :], SCALE, None, ALU.mult).then_inc(max_ready, 1)

            def shares(l, t, b):
                nk = P * (1 + t)
                dve.wait_ge(*exps_done(l, t, b))
                then(dve.reciprocal(rinv[:, b % 2, :], rs[:, b % 2, :]))
                if l == 0 and b >= 2:
                    then(dve.tensor_scalar(rinv[:, b % 2, 2:4], rinv[:, b % 2, 2:4], lam[:, 0:1], None, ALU.mult))
                    for i in range(2):
                        ins = dve.tensor_scalar(PR[:, b % 2, 2 + i, 0:nk], PR[:, b % 2, 2 + i, 0:nk], rinv[:, b % 2, 2 + i:3 + i], None, ALU.mult)
                    then(ins)
                    for i in range(2):
                        ins = dve.scalar_tensor_tensor(out=PR[:, b % 2, i, 0:nk], in0=PR[:, b % 2, i, 0:nk], scalar=rinv[:, b % 2, i:i + 1],
                                                       in1=PR[:, b % 2, 2 + i, 0:nk], op0=ALU.mult, op1=ALU.add)
                else:
                    for j in range(4):
                        ins = dve.tensor_scalar(PR[:, b % 2, j, 0:nk], PR[:, b % 2, j, 0:nk], rinv[:, b % 2, j:j + 1], None, ALU.mult)
                ins.then_inc(shared, 1)

            def outputs(l, t, b):
                name = ("O", l, t, b)
                dve.wait_ge(filled, fill(name))
                at = 768 + 256 * (b - 2)
                dst = qkv[t][:, at:at + 256] if l == 0 and b >= 2 else oT(l, t, 2 * b, 2)
                dve.tensor_copy(dst, bank_of(name)[:, 0:256]).then_inc(emptied["dve"], 1)

            def sub_norm(t):
                v = qkv[t][:, 768:1280].rearrange("p (h d) -> p h d", h=4)
                w = tmp[:, t, :].rearrange("p (h d) -> p h d", h=4)
                dve.wait_ge(*emptied_by(("O", 0, t, BATCHES - 1)))
                then(dve.tensor_tensor(w, v, v, ALU.mult))
                then(dve.tensor_reduce(hss[:, 0:4], w, AX.X, ALU.add))
                rms_inverse(("sub", 0, t), 2 * HD)
                then(dve.tensor_tensor(v, v, hss[:, 0:4].unsqueeze(2).to_broadcast([P, 4, 2 * HD]), ALU.mult))
                dve.tensor_tensor(v, v, subg[:, :].unsqueeze(1).to_broadcast([P, 4, 2 * HD]), ALU.mult).then_inc(o_ready, 1)

            def out_project(l, u, t):
                name, k, cols = ("wo", l, u, t), 2 * t + u, slice(u * UC, (u + 1) * UC)
                dve.wait_ge(*emptied_by(("gb", l, 0, u, t)))
                dve.wait_ge(filled, fill(name))
                dve.tensor_tensor(tmp[:, k % 2, :], bank_of(name)[:, :], gbuf[:, k, :], ALU.mult).then_inc(emptied["dve"], 1)
                dve.wait_ge(*emptied_by(name))
                dve.tensor_tensor(x[:, t, cols], x[:, t, cols], tmp[:, k % 2, :], ALU.add).then_inc(x_ready, 1)

            def reverse_bias(i):
                name, part = ("rev", i), bias[:, 4 * i:4 * i + 4, :]
                over_heads = lambda v: v.unsqueeze(1).to_broadcast([P, 4, P])
                dve.wait_ge(filled, fill(name))
                dve.tensor_tensor(part, bank_of(name)[:, :].rearrange("p (h k) -> p h k", h=4), over_heads(K("mask8")),
                                  ALU.mult).then_inc(emptied["dve"], 1)
                dve.wait_ge(*emptied_by(name))
                then(dve.tensor_tensor(part, part, over_heads(K("neg")), ALU.add))

            def meanwhile(*point):
                for name in fill_in(*point):
                    if engine_of[name] == "dve":
                        {"modT": mod, "modG": mod, "qkv": project, "rev": reverse_bias, "wo": out_project}[name[0]](*name[1:])

            def beaten(out, values, groups, width):
                v = values.rearrange("p (g i) -> p g i", i=width)
                mine = v.unsqueeze(3).to_broadcast([P, groups, width, width])
                others = v.unsqueeze(2).to_broadcast([P, groups, width, width])
                n = groups * width * width
                more = cmp[:, 0:n].rearrange("p (g i j) -> p g i j", i=width, j=width)
                same = cmq[:, 0:n].rearrange("p (g i j) -> p g i j", i=width, j=width)
                dve.tensor_tensor(more, others, mine, ALU.is_gt)
                then(dve.tensor_tensor(same, others, mine, ALU.is_equal))
                low = K("low4").rearrange("p (i j) -> p i j", i=4).unsqueeze(1).to_broadcast([P, groups, width, width])
                then(dve.tensor_tensor(same, same, low, ALU.mult))
                then(dve.tensor_tensor(more, more, same, ALU.add))
                then(dve.tensor_reduce(out.rearrange("p (g i) -> p g i", i=width), more, AX.X, ALU.add))

            def router(l):
                flat = lambda v: v[:, :, :].rearrange("p t e -> p (t e)")
                per_token = lambda v: v.unsqueeze(2).to_broadcast([P, TT, NE])
                for t in range(TT):
                    dve.wait_ge(*emptied_by(("rt", l, t)))
                then(dve.reciprocal(st2[:, 2:4], st2[:, 2:4]))
                then(dve.tensor_tensor(sco[:, :, :], sco[:, :, :], per_token(st2[:, 2:4]), ALU.mult))
                then(dve.tensor_tensor(sel[:, :, :], sco[:, :, :], br[:, :].unsqueeze(1).to_broadcast([P, TT, NE]), ALU.add))
                beaten(flat(top), flat(sel), TT * NG, EG)
                then(dve.tensor_scalar(flat(top), flat(top), float(EG - 2), None, ALU.is_lt))
                then(dve.tensor_tensor(flat(chosen), flat(sel), flat(top), ALU.mult))
                then(dve.tensor_reduce(gsum[:, :], flat(chosen).rearrange("p (g i) -> p g i", i=EG), AX.X, ALU.add))
                beaten(cnt8[:, :], gsum[:, :], TT, NG)
                then(dve.tensor_scalar(cnt8[:, :], cnt8[:, :], 0.0, None, ALU.is_equal))
                dve.tensor_tensor(flat(chosen).rearrange("p (g i) -> p g i", i=EG), flat(top).rearrange("p (g i) -> p g i", i=EG),
                                  cnt8[:, :].unsqueeze(2).to_broadcast([P, TT * NG, EG]), ALU.mult).then_inc(mask_ready, 1)
                dve.wait_ge(mask_ready, l + 1)
                meanwhile(l, "router", 0)
                then(dve.tensor_tensor(gate[:, :, :], sco[:, :, :], chosen[:, :, :], ALU.mult))
                then(dve.tensor_reduce(st2[:, 2:4], gate[:, :, :], AX.X, ALU.add))
                then(dve.reciprocal(st2[:, 2:4], st2[:, 2:4]))
                then(dve.tensor_tensor(gate[:, :, :], gate[:, :, :], per_token(st2[:, 2:4]), ALU.mult))
                by_rounds = lambda v: v.unsqueeze(1).to_broadcast([P, ROUNDS_MAX, NE])
                table = lambda v, t: v[:, t, 0:ROUNDS_MAX * NE].rearrange("p (r e) -> p r e", e=NE)
                dve.memset(slot_t[:, :, ROUNDS_MAX * NE:], -1.0)
                dve.memset(gate_t[:, :, ROUNDS_MAX * NE:], 0.0)
                for t in range(TT):
                    dve.tensor_copy(table(gate_t, t), by_rounds(gate[:, t, :]))
                name = ("pos", l)
                dve.wait_ge(filled, fill(name))
                b = bank_of(name)
                dve.scalar_tensor_tensor(out=slot_of[:, :, :], in0=b[:, 0:32].rearrange("p (t e) -> p t e", t=TT), scalar=1.0,
                                         in1=chosen[:, :, :], op0=ALU.add, op1=ALU.mult)
                dve.tensor_reduce(cnt[:, 0:1], b[:, 32:48], AX.X, ALU.max).then_inc(emptied["dve"], 1)
                dve.wait_ge(*emptied_by(name))
                for t in range(TT):
                    ins = dve.tensor_tensor(table(slot_t, t), by_rounds(slot_of[:, t, :]), K("before").rearrange("p (r e) -> p r e", e=NE), ALU.add)
                then(ins)

            def clear(l):
                dve.wait_ge(out_kv[l], 64 if l == 0 else 32)
                dve.memset(work[:, 0:2048], 0.0)
                dve.memset(GT[:, :, :], 0.0).then_inc(M[l]["y_zeroed"], 1)
                dve.memset(yd[:, 0:UC], 0.0).then_inc(M[l]["yd0_ready"], 1)

            def count_rounds(l):
                then(dve.tensor_scalar(cmp[:, 0:ROUNDS_MAX - 1], K("thr"), cnt[:, 0:1], None, ALU.is_lt))
                then(dve.tensor_reduce(cnt[:, 1:2], cmp[:, 0:ROUNDS_MAX - 1], AX.X, ALU.add))
                dve.tensor_scalar(rounds[:, :], cnt[:, 1:2], 1.0, None, ALU.add).then_inc(rounds_ready, 1)
                dve.wait_ge(rounds_ready, l + 1)

            def experts(l):
                m = M[l]
                def one_hots(n):
                    for t in range(TT):
                        for e in range(2):
                            col = bass.ds(2 * n + e, 1)
                            dve.tensor_scalar(pick[:, t, CAP * e:CAP * e + CAP], K("iota"), slot_t[:, t, col], None, ALU.is_equal)
                            ins = dve.tensor_scalar(gpick[:, t, CAP * e:CAP * e + CAP], K("iota"), slot_t[:, t, col], gate_t[:, t, col],
                                                    ALU.is_equal, ALU.mult)
                    ins.then_inc(m["picked"], 1)

                def hidden(n, h):
                    dve.wait_ge(m["sig_done"], 2 * n + h + 1)
                    half = slice(h * UC, (h + 1) * UC)
                    dve.tensor_tensor(hid[:, half], sg[:, half], bank[2 * h][:, :], ALU.mult).then_inc(m["loop_step"], 1)
                    dve.wait_ge(m["loop_step"], 2 * n + h + 1)
                    dve.wait_ge(moe_used[l], n * MOE_UNITS + (SLOTS + 4 * h + 4))
                    dve.tensor_tensor(hid[:, half], hid[:, half], bank[2 * h + 1][:, :], ALU.mult).then_inc(m["hid_done"], 1)

                def add_scattered(n):
                    for h in range(2):
                        for t in range(TT):
                            dve.wait_ge(m["scattered"], 4 * n + (2 * h + t + 1))
                            cols = slice(h * UC, (h + 1) * UC)
                            dve.tensor_tensor(y[:, t, cols], y[:, t, cols], bank[4 + 2 * t + h][:, :], ALU.add).then_inc(m["y_added"], 1)

                one_hots(0)
                count_rounds(l)
                r_end = dve.value_load(rounds[0:1, 0:1], min_val=1, max_val=ROUNDS_MAX)
                with dve.Fori(0, r_end * PAIRS) as n:
                    hidden(n, 0)
                    add_scattered(n)
                    dve.wait_ge(m["gt_done"], n + 1)
                    one_hots(n + 1)
                    hidden(n, 1)
                    dve.wait_ge(moe_used[l], n * MOE_UNITS + (SLOTS + 10))
                    dve.tensor_copy(yd[:, 0:UC], bank[6][:, :]).then_inc(m["yd0_ready"], 1)
                last = r_end * PAIRS
                dve.wait_ge(m["y_added"], 4 * last)
                for u in range(2):
                    for t in range(TT):
                        cols = slice(u * UC, (u + 1) * UC)
                        dve.wait_ge(*emptied_by(("gb", l, 1, u, t)))
                        then(dve.tensor_tensor(tmp[:, t, :], y[:, t, cols], gbuf[:, 2 * t + u, :], ALU.mult))
                        ins = dve.tensor_tensor(x[:, t, cols], x[:, t, cols], tmp[:, t, :], ALU.add)
                then(ins)
                for u in range(2):
                    for t in range(TT):
                        cols = slice(u * UC, (u + 1) * UC)
                        dve.wait_ge(m["scattered"], 4 * last + (2 * u + t + 1))
                        dve.tensor_tensor(tmp[:, t, :], bank[4 + 2 * t + u][:, :], gbuf[:, 2 * t + u, :], ALU.mult).then_inc(m["y_added"], 1)
                        dve.wait_ge(m["y_added"], 4 * last + (2 * u + t + 1))
                        dve.tensor_tensor(x[:, t, cols], x[:, t, cols], tmp[:, t, :], ALU.add).then_inc(x_ready, 1)

            for name, dst in ((("vecT",), vT), (("bT",), bT)):
                dve.wait_ge(filled, fill(name))
                dve.tensor_copy(dst[:, :], bank_of(name)[:, 0:dst.shape[1]]).then_inc(emptied["dve"], 1)
            dve.wait_ge(sig_ready, 1)
            dve.wait_ge(cleared, 2)
            dve.tensor_tensor(cond[:, :, 0:2].rearrange("p c t -> p t c"), vT[:, 0:16].rearrange("p (t c) -> p t c", t=2),
                              sig[:, :].rearrange("p (t c) -> p t c", t=2), ALU.mult).then_inc(cond_ready, 1)
            for t in range(TT):
                norm(0, 0, t)
            for u in range(4):
                mod(0, u)
            for l in range(LAYERS):
                for t in range(TT):
                    modulate(l, 0, t)
                for u in range(4):
                    project(l, u, 1)
                if l == 0:
                    dve.wait_ge(ld_small, 16 * 11)
                    then(dve.tensor_tensor(lamw[:, :, :], lamv[:, 0:4:2, :], lamv[:, 1:4:2, :], ALU.mult))
                    dve.tensor_reduce(lam[:, 0:2], lamw[:, :, :], AX.X, ALU.add).then_inc(lam_dot, 1)
                    then(dve.tensor_scalar(subg[:, :], subg[:, :], 1.0 - LAM_INIT, None, ALU.mult))
                qk_sums(l, 0)
                if l == 0:
                    project(0, 4, 1)
                qk_sums(l, 1)
                qk_norm(l, 0)
                if l == 0:
                    dve.wait_ge(lam_exp, 1)
                    then(dve.tensor_tensor(lam[:, 0:1], lam[:, 3:4], lam[:, 2:3], ALU.subtract))
                    then(dve.tensor_scalar(lam[:, 0:1], lam[:, 0:1], -LAM_INIT, None, ALU.add))
                for t in range(TT):
                    if (l, t) == (1, 1):
                        dve.wait_ge(out_kv[1], 32)
                    meanwhile(l, t, -1)
                    maxima(l, t, 0)
                    maxima(l, t, 1)
                    shares(l, t, 0)
                    meanwhile(l, t, 0)
                    if t == 0:
                        qk_norm(l, 1)
                    for b in range(BATCHES):
                        outputs(l, t, b)
                        if b + 2 < BATCHES:
                            maxima(l, t, b + 2)
                        if b + 1 < BATCHES:
                            shares(l, t, b + 1)
                        meanwhile(l, t, b + 1)
                        if (l, t) == (0, 0) and b < 2:
                            (rotate_by_sines, rotate_by_cosines)[b]()
                    if l == 0:
                        sub_norm(t)
                if l == 0:
                    out_project(0, 0, 0)
                    out_project(0, 1, 0)
                norm(l, 1, 0)
                out_project(l, 0, 1)
                modulate(l, 1, 0)
                out_project(l, 1, 1)
                norm(l, 1, 1)
                largest_logit(l, 0)
                meanwhile(l, "norm", 0)
                modulate(l, 1, 1)
                clear(l)
                largest_logit(l, 1)
                router(l)
                experts(l)
                for t in range(TT) if l == 0 else ():
                    norm(1, 0, t)


_INS = ["x_prompt", "x_sample", "cache_a_k", "cache_a_v", "cache_b_k", "cache_b_v", "cache_c_k", "cache_c_v",
        "c", "c_ctx", "w_mod", "b_mod", "norm_mix", "norm_ffn", "w_in_ab", "w_out_ab", "a_q_norm", "a_k_norm",
        "b_q_norm", "b_k_norm", "lam_q1", "lam_k1", "lam_q2", "lam_k2", "b_subln", "w_in_c", "w_out_c",
        "c_q_norm", "c_k_norm", "c_rpb", "w_router", "b_router", "w_gate", "w_up", "w_down"]
_OUTS = [("y_prompt", (1, 128, 1024)), ("y_sample", (1, 128, 1024)),
         ("new_a_k", (1, 1, 128, 2, 64)), ("new_a_v", (1, 1, 128, 2, 64)),
         ("new_b_k", (1, 1, 128, 4, 2, 64)), ("new_b_v", (1, 1, 128, 4, 128)),
         ("new_c_k", (1, 1, 128, 16, 64)), ("new_c_v", (1, 1, 128, 16, 64))]


def kernel(**inputs):
    import concourse.bacc as bacc
    from concourse.bass_utils import run_bass_kernel_spmd

    nc = bacc.Bacc("TRN2", target_bir_lowering=False, num_devices=1)
    arrays, aps = {}, {}
    for name in _INS:
        arr = np.ascontiguousarray(inputs[name])
        arrays["in_" + name] = arr
        aps[name] = nc.dram_tensor("in_" + name, arr.shape, mybir.dt.from_np(arr.dtype), kind="ExternalInput").ap()
    arrays["in_tables"] = constants()
    aps["tables"] = nc.dram_tensor("in_tables", (P, NCONST), F32, kind="ExternalInput").ap()
    for name, shape in _OUTS:
        flat = nc.dram_tensor("out_" + name, (P, int(np.prod(shape)) // P), F32, kind="ExternalOutput").ap()
        aps[name] = flat
    build(nc, aps)
    r = run_bass_kernel_spmd(nc, [arrays], core_ids=[0])
    return tuple(r.results[0]["out_" + name].reshape(shape) for name, shape in _OUTS)
```
